# Optimizing a Trainium2 kernel written in Bass

```python
import math
import jax, jax.numpy as jnp
from jax import lax
import numpy as np

D_MODEL = 1024
BATCH = 1
SEQ = 256
DEPTH = 1

HEAD_DIM = 64
DILATED_GROUPS = ((128, 1), (512, 4), (2048, 16))
N_DIL = len(DILATED_GROUPS)
HEADS_PER_GROUP = 8
N_ATTN_HEADS = N_DIL * HEADS_PER_GROUP
ATTN_WIDTH = N_ATTN_HEADS * HEAD_DIM
ATTN_OUT_WIDTH = HEADS_PER_GROUP * HEAD_DIM
ATTN_BLOCK = 128
N_REL_BUCKETS = 32
REL_MAX_DISTANCE = 2048

D_INNER = 2 * D_MODEL
SSM_HEAD_DIM = 64
N_SSM_HEADS = D_INNER // SSM_HEAD_DIM
N_SSM_GROUPS = 4
HEADS_PER_SSM_GROUP = N_SSM_HEADS // N_SSM_GROUPS
D_STATE = 128
CONV_WIDTH = 4
SSD_CHUNK = 128
XBC_WIDTH = D_INNER + 2 * N_SSM_GROUPS * D_STATE

N_BRANCHES = 2
D_FF = -(-8 * D_MODEL // (3 * 256)) * 256
IN_PROJ_WIDTH = 3 * ATTN_WIDTH + D_INNER + XBC_WIDTH + N_SSM_HEADS + N_BRANCHES * D_MODEL
EPS = 1e-6


def rmsnorm(x, w):
    xf = x.astype(jnp.float32)
    y = xf * lax.rsqrt(jnp.mean(xf * xf, axis=-1, keepdims=True) + EPS)
    return (y * w.astype(jnp.float32)).astype(x.dtype)

def t5_causal_bucket(dist):
    max_exact = N_REL_BUCKETS // 2
    d_f = jnp.maximum(dist, 1).astype(jnp.float32)
    large = max_exact + (jnp.log(d_f / max_exact) / math.log(REL_MAX_DISTANCE / max_exact)
                         * (N_REL_BUCKETS - max_exact)).astype(jnp.int32)
    large = jnp.minimum(large, N_REL_BUCKETS - 1)
    return jnp.where(dist < max_exact, dist, large)

def rel_bias_block(rel_bias_g, dilation, n_steps):
    qi = jnp.arange(ATTN_BLOCK)[:, None]
    kj = jnp.arange(2 * ATTN_BLOCK)[None, :]
    steps = jnp.clip(qi + ATTN_BLOCK - kj, 0, n_steps)
    bucket = t5_causal_bucket(steps * dilation)
    return jnp.transpose(rel_bias_g[bucket], (2, 0, 1)).astype(jnp.float32)

def dilated_window_attention(q, k, v, bias, dilation, n_steps):
    b, s, h, dh = q.shape
    seg = s // dilation
    nb = -(-seg // ATTN_BLOCK)
    segp = nb * ATTN_BLOCK

    def to_blocks(t):
        t = t.reshape(b, seg, dilation, h, dh).transpose(0, 2, 1, 3, 4).reshape(b * dilation, seg, h, dh)
        t = jnp.pad(t, ((0, 0), (0, segp - seg), (0, 0), (0, 0)))
        return t.reshape(b * dilation, nb, ATTN_BLOCK, h, dh)

    def with_prev(t):
        prev = jnp.pad(t[:, :-1], ((0, 0), (1, 0), (0, 0), (0, 0), (0, 0)))
        return jnp.concatenate([prev, t], axis=2)

    qb = to_blocks(q)
    kw = with_prev(to_blocks(k))
    vw = with_prev(to_blocks(v))

    qi = jnp.arange(ATTN_BLOCK)[:, None]
    kj = jnp.arange(2 * ATTN_BLOCK)[None, :]
    steps = qi + ATTN_BLOCK - kj
    blk = jnp.arange(nb)[:, None, None]
    valid = (steps >= 0) & (steps <= n_steps) & (blk * ATTN_BLOCK - ATTN_BLOCK + kj >= 0)

    logits = jnp.einsum('znqhd,znkhd->znhqk', qb, kw).astype(jnp.float32) * (HEAD_DIM ** -0.5) + bias
    logits = jnp.where(valid[None, :, None], logits, -jnp.inf)
    m = jnp.max(logits, axis=-1, keepdims=True)
    p = jnp.exp(logits - m)
    den = jnp.sum(p, axis=-1, keepdims=True)
    o = jnp.einsum('znhqk,znkhd->znqhd', p, vw.astype(jnp.float32)) / jnp.swapaxes(den, 2, 3)
    lse = jnp.swapaxes((m + jnp.log(den))[..., 0], 2, 3)

    o = o.reshape(b, dilation, segp, h, dh)[:, :, :seg]
    o = jnp.swapaxes(o, 1, 2).reshape(b, s, h, dh)
    lse = lse.reshape(b, dilation, segp, h)[:, :, :seg]
    lse = jnp.swapaxes(lse, 1, 2).reshape(b, s, h)
    return o, lse

def causal_depthwise_conv(x, w, bias):
    c = x.shape[-1]
    y = lax.conv_general_dilated(x, w[:, None, :], window_strides=(1,),
                                 padding=((CONV_WIDTH - 1, 0),),
                                 dimension_numbers=('NWC', 'WIO', 'NWC'),
                                 feature_group_count=c)
    return y + bias

def ssd_chunked_scan(xh, dt, a, bm, cm):
    b, s = xh.shape[:2]
    nc = s // SSD_CHUNK

    def chunks(t):
        return jnp.swapaxes(t.reshape(b, nc, SSD_CHUNK, *t.shape[2:]), 0, 1)

    causal = jnp.tril(jnp.ones((SSD_CHUNK, SSD_CHUNK), dtype=bool))[None, :, :, None, None]

    def step(state, inp):
        x_, dt_, b_, c_ = inp
        la = jnp.cumsum(dt_ * a, axis=1)
        seg = la[:, :, None] - la[:, None, :]
        decay = jnp.exp(jnp.where(causal, seg, -jnp.inf))
        cb = jnp.einsum('bign,bjgn->bijg', c_, b_)
        xdt = x_ * dt_[..., None]
        y_intra = jnp.einsum('bijg,bijgh,bjghp->bighp', cb, decay, xdt)
        y_inter = jnp.einsum('bign,bghpn->bighp', c_, state) * jnp.exp(la)[..., None]
        to_end = jnp.exp(la[:, -1:] - la)
        new_state = (state * jnp.exp(la[:, -1])[..., None, None]
                     + jnp.einsum('bjgn,bjgh,bjghp->bghpn', b_, to_end, xdt))
        return new_state, y_intra + y_inter

    state0 = jnp.zeros((b, N_SSM_GROUPS, HEADS_PER_SSM_GROUP, SSM_HEAD_DIM, D_STATE), jnp.float32)
    _, ys = lax.scan(step, state0, (chunks(xh), chunks(dt), chunks(bm), chunks(cm)))
    return jnp.swapaxes(ys, 0, 1).reshape(b, s, N_SSM_GROUPS, HEADS_PER_SSM_GROUP, SSM_HEAD_DIM)

def hybrid_mixer(xn, w_in, conv_w, conv_b, dt_bias, a_log, d_skip, ssm_norm_w,
                 w_attn_branch, w_ssm_branch, w_out, attn_biases):
    b, s, _ = xn.shape
    proj = xn @ w_in
    q, k, v, z, xbc, dt_raw, gate_logits = jnp.split(
        proj, np.cumsum([ATTN_WIDTH, ATTN_WIDTH, ATTN_WIDTH, D_INNER, XBC_WIDTH, N_SSM_HEADS]).tolist(), axis=-1)

    q = q.reshape(b, s, N_DIL, HEADS_PER_GROUP, HEAD_DIM)
    k = k.reshape(b, s, N_DIL, HEADS_PER_GROUP, HEAD_DIM)
    v = v.reshape(b, s, N_DIL, HEADS_PER_GROUP, HEAD_DIM)
    outs, lses = [], []
    for g, (window, dil) in enumerate(DILATED_GROUPS):
        o_g, lse_g = dilated_window_attention(q[:, :, g], k[:, :, g], v[:, :, g],
                                              attn_biases[g], dil, window // dil)
        outs.append(o_g)
        lses.append(lse_g)
    o = jnp.stack(outs, axis=2)
    alpha = jax.nn.softmax(jnp.stack(lses, axis=2), axis=2)
    attn = jnp.sum(alpha[..., None] * o, axis=2).reshape(b, s, ATTN_OUT_WIDTH).astype(xn.dtype)

    xbc = jax.nn.silu(causal_depthwise_conv(xbc, conv_w, conv_b))
    xs, bm, cm = jnp.split(xbc, [D_INNER, D_INNER + N_SSM_GROUPS * D_STATE], axis=-1)
    xh = xs.reshape(b, s, N_SSM_GROUPS, HEADS_PER_SSM_GROUP, SSM_HEAD_DIM).astype(jnp.float32)
    bm = bm.reshape(b, s, N_SSM_GROUPS, D_STATE).astype(jnp.float32)
    cm = cm.reshape(b, s, N_SSM_GROUPS, D_STATE).astype(jnp.float32)
    dt = jax.nn.softplus(dt_raw.astype(jnp.float32) + dt_bias.astype(jnp.float32))
    dt = dt.reshape(b, s, N_SSM_GROUPS, HEADS_PER_SSM_GROUP)
    a = -jnp.exp(a_log.astype(jnp.float32)).reshape(N_SSM_GROUPS, HEADS_PER_SSM_GROUP)
    y = ssd_chunked_scan(xh, dt, a, bm, cm)
    y = y + xh * d_skip.astype(jnp.float32).reshape(N_SSM_GROUPS, HEADS_PER_SSM_GROUP)[..., None]
    yg = (y.reshape(b, s, D_INNER) * jax.nn.silu(z.astype(jnp.float32))).reshape(b, s, N_SSM_GROUPS, D_INNER // N_SSM_GROUPS)
    yg = yg * lax.rsqrt(jnp.mean(yg * yg, axis=-1, keepdims=True) + EPS)
    ssm = (yg.reshape(b, s, D_INNER) * ssm_norm_w.astype(jnp.float32)).astype(xn.dtype)

    gates = jax.nn.sigmoid(gate_logits.astype(jnp.float32)).reshape(b, s, N_BRANCHES, D_MODEL)
    merged = (gates[:, :, 0] * (attn @ w_attn_branch).astype(jnp.float32)
              + gates[:, :, 1] * (ssm @ w_ssm_branch).astype(jnp.float32)).astype(xn.dtype)
    return merged @ w_out

def swiglu(xn, w_ffn_in, w_ffn_out):
    gate, up = jnp.split(xn @ w_ffn_in, 2, axis=-1)
    return (jax.nn.silu(gate) * up) @ w_ffn_out

def first_inputs(seed: int = 0) -> dict:
    key = jax.random.key(seed)
    ks = jax.random.split(key, 20)
    f32 = jnp.float32
    nrm = lambda k, shape, scale: jax.random.normal(k, shape, f32) * scale
    dt0 = jnp.exp(jax.random.uniform(ks[5], (DEPTH, N_SSM_HEADS), f32, math.log(1e-3), math.log(1e-1)))
    return {
        "x": nrm(ks[0], (BATCH, SEQ, D_MODEL), 1.0),
        "norm1_w": 1.0 + nrm(ks[1], (DEPTH, D_MODEL), 0.02),
        "w_in": nrm(ks[2], (DEPTH, D_MODEL, IN_PROJ_WIDTH), D_MODEL ** -0.5),
        "conv_w": nrm(ks[3], (DEPTH, CONV_WIDTH, XBC_WIDTH), CONV_WIDTH ** -0.5),
        "conv_b": nrm(ks[4], (DEPTH, XBC_WIDTH), 0.02),
        "dt_bias": dt0 + jnp.log(-jnp.expm1(-dt0)),
        "a_log": jnp.log(jax.random.uniform(ks[6], (DEPTH, N_SSM_HEADS), f32, 1.0, 16.0)),
        "d_skip": 1.0 + nrm(ks[7], (DEPTH, N_SSM_HEADS), 0.1),
        "ssm_norm_w": 1.0 + nrm(ks[8], (DEPTH, D_INNER), 0.02),
        "w_attn_branch": nrm(ks[9], (DEPTH, ATTN_OUT_WIDTH, D_MODEL), ATTN_OUT_WIDTH ** -0.5),
        "w_ssm_branch": nrm(ks[10], (DEPTH, D_INNER, D_MODEL), D_INNER ** -0.5),
        "w_out": nrm(ks[11], (DEPTH, D_MODEL, D_MODEL), D_MODEL ** -0.5),
        "norm2_w": 1.0 + nrm(ks[12], (DEPTH, D_MODEL), 0.02),
        "w_ffn_in": nrm(ks[13], (DEPTH, D_MODEL, 2 * D_FF), D_MODEL ** -0.5),
        "w_ffn_out": nrm(ks[14], (DEPTH, D_FF, D_MODEL), D_FF ** -0.5),
        "rel_bias": nrm(ks[15], (N_REL_BUCKETS, N_ATTN_HEADS), 0.5),
        "final_norm_w": 1.0 + nrm(ks[16], (D_MODEL,), 0.02),
    }

def first_block(x, norm1_w, w_in, conv_w, conv_b, dt_bias, a_log, d_skip, ssm_norm_w,
              w_attn_branch, w_ssm_branch, w_out, norm2_w, w_ffn_in, w_ffn_out,
              rel_bias, final_norm_w):
    attn_biases = [rel_bias_block(rel_bias[:, g * HEADS_PER_GROUP:(g + 1) * HEADS_PER_GROUP], dil, window // dil)
                   for g, (window, dil) in enumerate(DILATED_GROUPS)]
    h = x
    for layer in range(DEPTH):
        h = h + hybrid_mixer(rmsnorm(h, norm1_w[layer]), w_in[layer], conv_w[layer], conv_b[layer],
                             dt_bias[layer], a_log[layer], d_skip[layer], ssm_norm_w[layer],
                             w_attn_branch[layer], w_ssm_branch[layer], w_out[layer], attn_biases)
        h = h + swiglu(rmsnorm(h, norm2_w[layer]), w_ffn_in[layer], w_ffn_out[layer])
    return rmsnorm(h, final_norm_w)


DEPTH_2 = 4

GRID_W = 64
CTX_LEN = 256
N_MIXERS = 3
D_FF_2 = 4 * D_MODEL

GLA_HEADS = 4
GLA_KEY_DIM = D_MODEL // 2
GLA_VAL_DIM = D_MODEL
GLA_DK = GLA_KEY_DIM // GLA_HEADS
GLA_DV = GLA_VAL_DIM // GLA_HEADS
GLA_RANK = 16
GLA_TAU = 16.0
GLA_CHUNK = 64

CONV_WIDTH_2 = 31
CONV_PAD = CONV_WIDTH_2 // 2

ATTN_HEAD_DIM = 64
ATTN_Q_HEADS = D_MODEL // ATTN_HEAD_DIM
ATTN_KV_HEADS = 4
ATTN_GROUP = ATTN_Q_HEADS // ATTN_KV_HEADS
ATTN_Q_DIM = ATTN_Q_HEADS * ATTN_HEAD_DIM
ATTN_KV_DIM = ATTN_KV_HEADS * ATTN_HEAD_DIM
ATTN_SCALE = ATTN_HEAD_DIM ** -0.5
ROPE_THETA = 10000.0

N_GLA = (DEPTH_2 + 2) // 3
N_CONV = (DEPTH_2 + 1) // 3
N_ATTN = DEPTH_2 // 3


def rms_norm(x, g):
    xf = x.astype(jnp.float32)
    y = xf * lax.rsqrt(jnp.mean(xf * xf, axis=-1, keepdims=True) + EPS)
    return (y * g.astype(jnp.float32)).astype(x.dtype)

def layer_norm(x, g, b):
    xf = x.astype(jnp.float32)
    mu = jnp.mean(xf, axis=-1, keepdims=True)
    xc = xf - mu
    y = xc * lax.rsqrt(jnp.mean(xc * xc, axis=-1, keepdims=True) + EPS)
    return (y * g.astype(jnp.float32) + b.astype(jnp.float32)).astype(x.dtype)

def split_heads(t, n):
    B, L, _ = t.shape
    return t.reshape(B, L, n, -1).transpose(0, 2, 1, 3)

def axial_rope_tables(row_idx, col_idx):
    n = ATTN_HEAD_DIM // 4
    inv = ROPE_THETA ** (-jnp.arange(n, dtype=jnp.float32) / n)
    ang = jnp.concatenate([row_idx.astype(jnp.float32)[:, None] * inv,
                           col_idx.astype(jnp.float32)[:, None] * inv], axis=-1)
    return jnp.cos(ang), jnp.sin(ang)

def apply_rope(x, cos, sin):
    half = x.shape[-1] // 2
    cos = cos.astype(x.dtype)
    sin = sin.astype(x.dtype)
    x1, x2 = x[..., :half], x[..., half:]
    return jnp.concatenate([x1 * cos - x2 * sin, x2 * cos + x1 * sin], axis=-1)

def gla_chunk_scan(q, k, v, logg, s0):
    B, H, L, _ = q.shape
    n = L // GLA_CHUNK

    def to_chunks(a):
        return jnp.moveaxis(a.reshape(B, H, n, GLA_CHUNK, a.shape[-1]), 2, 0)

    mask = jnp.tril(jnp.ones((GLA_CHUNK, GLA_CHUNK), dtype=bool))

    def step(s, inp):
        qc, kc, vc, gc = inp
        b = jnp.cumsum(gc, axis=-2)
        b_last = b[..., -1:, :]
        qb = qc * jnp.exp(b)
        kb = kc * jnp.exp(-b)
        a = jnp.where(mask, jnp.einsum('bhid,bhjd->bhij', qb, kb), 0.0)
        o = jnp.einsum('bhid,bhde->bhie', qb, s) + jnp.einsum('bhij,bhje->bhie', a, vc)
        kd = kc * jnp.exp(b_last - b)
        s_new = jnp.exp(b_last[..., 0, :])[..., None] * s + jnp.einsum('bhjd,bhje->bhde', kd, vc)
        return s_new, o

    s_fin, o = lax.scan(step, s0, (to_chunks(q), to_chunks(k), to_chunks(v), to_chunks(logg)))
    o = jnp.moveaxis(o, 0, 2).reshape(B, H, L, v.shape[-1])
    return o, s_fin

def gla_mixer(h_ctx, h_lat, w_in, w_g1, w_g2, b_g, g_head, w_out, need_ctx):
    f32 = jnp.float32

    def project(h):
        z = h @ w_in
        q, k, v, r = jnp.split(z, [GLA_KEY_DIM, 2 * GLA_KEY_DIM, 2 * GLA_KEY_DIM + GLA_VAL_DIM], axis=-1)
        q = split_heads(q, GLA_HEADS).astype(f32) * (GLA_DK ** -0.5)
        k = split_heads(k, GLA_HEADS).astype(f32)
        v = split_heads(v, GLA_HEADS).astype(f32)
        gates = []
        for d in range(2):
            zg = (h @ w_g1[d]) @ w_g2[d] + b_g[d]
            gates.append(split_heads(jax.nn.log_sigmoid(zg.astype(f32)) / GLA_TAU, GLA_HEADS))
        return q, k, v, r, gates[0], gates[1]

    qc, kc, vc, rc, gcf, gcb = project(h_ctx)
    ql, kl, vl, rl, glf, glb = project(h_lat)

    def flip(a):
        return jnp.flip(a, axis=2)

    B = h_lat.shape[0]
    s0 = jnp.zeros((B, GLA_HEADS, GLA_DK, GLA_DV), f32)
    oc_f, s_f = gla_chunk_scan(qc, kc, vc, gcf, s0)
    oc_b, s_b = gla_chunk_scan(flip(qc), flip(kc), flip(vc), flip(gcb), s0)
    ol_f, _ = gla_chunk_scan(ql, kl, vl, glf, s_f)
    ol_b, _ = gla_chunk_scan(flip(ql), flip(kl), flip(vl), flip(glb), s_b)

    def finish(o, r, dtype):
        o = rms_norm(o, g_head)
        o = o.transpose(0, 2, 1, 3).reshape(o.shape[0], o.shape[2], GLA_VAL_DIM).astype(dtype)
        return (o * jax.nn.silu(r)) @ w_out

    y_lat = finish(ol_f + flip(ol_b), rl, h_lat.dtype)
    y_ctx = finish(oc_f + flip(oc_b), rc, h_ctx.dtype) if need_ctx else None
    return y_ctx, y_lat

def conformer_conv(h, w_pw1, b_pw1, w_dw, b_dw, ln_g, ln_b, w_pw2, b_pw2):
    z = h @ w_pw1 + b_pw1
    a, gt = jnp.split(z, 2, axis=-1)
    u = a * jax.nn.sigmoid(gt)
    u = lax.conv_general_dilated(u, w_dw[:, None, :], window_strides=(1,),
                                 padding=[(CONV_PAD, CONV_PAD)],
                                 dimension_numbers=('NWC', 'WIO', 'NWC'),
                                 feature_group_count=D_MODEL) + b_dw
    u = jax.nn.silu(layer_norm(u, ln_g, ln_b))
    return u @ w_pw2 + b_pw2

def sdpa(q, k, v):
    s = jnp.einsum('bkgqd,bksd->bkgqs', q, k).astype(jnp.float32) * ATTN_SCALE
    p = jax.nn.softmax(s, axis=-1).astype(v.dtype)
    return jnp.einsum('bkgqs,bksd->bkgqd', p, v)

def gqa_mixer(h_ctx, h_lat, w_qkv, g_q, g_k, w_out, cos, sin, need_ctx):

    def project(h, rope):
        B, L, _ = h.shape
        z = h @ w_qkv
        q, k, v = jnp.split(z, [ATTN_Q_DIM, ATTN_Q_DIM + ATTN_KV_DIM], axis=-1)
        q = rms_norm(q.reshape(B, L, ATTN_KV_HEADS, ATTN_GROUP, ATTN_HEAD_DIM), g_q).transpose(0, 2, 3, 1, 4)
        k = rms_norm(k.reshape(B, L, ATTN_KV_HEADS, ATTN_HEAD_DIM), g_k).transpose(0, 2, 1, 3)
        v = v.reshape(B, L, ATTN_KV_HEADS, ATTN_HEAD_DIM).transpose(0, 2, 1, 3)
        if rope:
            q = apply_rope(q, cos, sin)
            k = apply_rope(k, cos, sin)
        return q, k, v

    def merge(o):
        B, _, _, L, _ = o.shape
        return o.transpose(0, 3, 1, 2, 4).reshape(B, L, ATTN_Q_DIM) @ w_out

    qc, kc, vc = project(h_ctx, False)
    ql, kl, vl = project(h_lat, True)
    y_ctx = merge(sdpa(qc, kc, vc)) if need_ctx else None

    k_all = jnp.concatenate([kc, kl], axis=2)
    v_all = jnp.concatenate([vc, vl], axis=2)
    B, KV, G, L, hd = ql.shape
    nb = L // ATTN_BLOCK
    qb = jnp.moveaxis(ql.reshape(B, KV, G, nb, ATTN_BLOCK, hd), 3, 0)
    ob = lax.map(lambda qq: sdpa(qq, k_all, v_all), qb)
    ol = jnp.moveaxis(ob, 0, 3).reshape(B, KV, G, L, hd)
    return y_ctx, merge(ol)

def sq_relu_mlp(h, w_in, w_out):
    return jnp.square(jax.nn.relu(h @ w_in)) @ w_out

def second_inputs(seed: int = 0) -> dict:
    key = jax.random.key(seed)
    ks = iter(jax.random.split(key, 40))
    D = D_MODEL

    def nrm(shape, scale):
        return jax.random.normal(next(ks), shape, jnp.float32) * scale

    return {
        "x": nrm((BATCH, SEQ, D), 1.0),
        "c": nrm((BATCH, D), 1.0),
        "ctx": nrm((BATCH, CTX_LEN, D), 1.0),
        "c_ctx": nrm((D,), 1.0),
        "w_mod": nrm((DEPTH_2, D, 6 * D), 0.5 * D ** -0.5),
        "b_mod": nrm((DEPTH_2, 6 * D), 0.01),
        "g_norm_mix": 1.0 + nrm((DEPTH_2, D), 0.02),
        "g_norm_mlp": 1.0 + nrm((DEPTH_2, D), 0.02),
        "w_mlp_in": nrm((DEPTH_2, D, D_FF_2), D ** -0.5),
        "w_mlp_out": nrm((DEPTH_2, D_FF_2, D), D_FF_2 ** -0.5),
        "gla_w_in": nrm((N_GLA, D, 2 * GLA_KEY_DIM + 2 * GLA_VAL_DIM), D ** -0.5),
        "gla_w_g1": nrm((N_GLA, 2, D, GLA_RANK), D ** -0.5),
        "gla_w_g2": nrm((N_GLA, 2, GLA_RANK, GLA_KEY_DIM), GLA_RANK ** -0.5),
        "gla_b_g": nrm((N_GLA, 2, GLA_KEY_DIM), 0.1),
        "gla_g_head": 1.0 + nrm((N_GLA, GLA_DV), 0.02),
        "gla_w_out": nrm((N_GLA, GLA_VAL_DIM, D), GLA_VAL_DIM ** -0.5),
        "conv_w_pw1": nrm((N_CONV, D, 2 * D), D ** -0.5),
        "conv_b_pw1": nrm((N_CONV, 2 * D), 0.01),
        "conv_w_dw": nrm((N_CONV, CONV_WIDTH_2, D), CONV_WIDTH_2 ** -0.5),
        "conv_b_dw": nrm((N_CONV, D), 0.01),
        "conv_ln_g": 1.0 + nrm((N_CONV, D), 0.02),
        "conv_ln_b": nrm((N_CONV, D), 0.01),
        "conv_w_pw2": nrm((N_CONV, D, D), D ** -0.5),
        "conv_b_pw2": nrm((N_CONV, D), 0.01),
        "attn_w_qkv": nrm((N_ATTN, D, ATTN_Q_DIM + 2 * ATTN_KV_DIM), D ** -0.5),
        "attn_g_q": 1.0 + nrm((N_ATTN, ATTN_HEAD_DIM), 0.02),
        "attn_g_k": 1.0 + nrm((N_ATTN, ATTN_HEAD_DIM), 0.02),
        "attn_w_out": nrm((N_ATTN, ATTN_Q_DIM, D), ATTN_Q_DIM ** -0.5),
    }

def second_block(x, c, ctx, c_ctx, w_mod, b_mod, g_norm_mix, g_norm_mlp, w_mlp_in, w_mlp_out,
              gla_w_in, gla_w_g1, gla_w_g2, gla_b_g, gla_g_head, gla_w_out,
              conv_w_pw1, conv_b_pw1, conv_w_dw, conv_b_dw, conv_ln_g, conv_ln_b, conv_w_pw2, conv_b_pw2,
              attn_w_qkv, attn_g_q, attn_g_k, attn_w_out):
    L = x.shape[1]
    rows = L // GRID_W
    row_idx = jnp.repeat(jnp.arange(rows, dtype=jnp.int32), GRID_W)
    col_idx = jnp.tile(jnp.arange(GRID_W, dtype=jnp.int32), rows)
    cos, sin = axial_rope_tables(row_idx, col_idx)

    silu_c = jax.nn.silu(c)
    silu_cc = jax.nn.silu(c_ctx)
    x_lat, x_ctx = x, ctx
    for i in range(DEPTH_2):
        last = i == DEPTH_2 - 1
        kind = i % N_MIXERS
        j = i // N_MIXERS
        mod_l = (silu_c @ w_mod[i] + b_mod[i])[:, None, :]
        mod_c = (silu_cc @ w_mod[i] + b_mod[i])[None, None, :]
        sh1_l, sc1_l, gt1_l, sh2_l, sc2_l, gt2_l = jnp.split(mod_l, 6, axis=-1)
        sh1_c, sc1_c, gt1_c, sh2_c, sc2_c, gt2_c = jnp.split(mod_c, 6, axis=-1)

        h_l = rms_norm(x_lat, g_norm_mix[i]) * (1.0 + sc1_l) + sh1_l
        h_c = rms_norm(x_ctx, g_norm_mix[i]) * (1.0 + sc1_c) + sh1_c
        if kind == 0:
            y_c, y_l = gla_mixer(h_c, h_l, gla_w_in[j], gla_w_g1[j], gla_w_g2[j], gla_b_g[j],
                                 gla_g_head[j], gla_w_out[j], not last)
        elif kind == 1:
            conv_args = (conv_w_pw1[j], conv_b_pw1[j], conv_w_dw[j], conv_b_dw[j],
                         conv_ln_g[j], conv_ln_b[j], conv_w_pw2[j], conv_b_pw2[j])
            y_l = conformer_conv(h_l, *conv_args)
            y_c = None if last else conformer_conv(h_c, *conv_args)
        else:
            y_c, y_l = gqa_mixer(h_c, h_l, attn_w_qkv[j], attn_g_q[j], attn_g_k[j], attn_w_out[j],
                                 cos, sin, not last)
        x_lat = x_lat + gt1_l * y_l

        h_l = rms_norm(x_lat, g_norm_mlp[i]) * (1.0 + sc2_l) + sh2_l
        x_lat = x_lat + gt2_l * sq_relu_mlp(h_l, w_mlp_in[i], w_mlp_out[i])
        if not last:
            x_ctx = x_ctx + gt1_c * y_c
            h_c = rms_norm(x_ctx, g_norm_mlp[i]) * (1.0 + sc2_c) + sh2_c
            x_ctx = x_ctx + gt2_c * sq_relu_mlp(h_c, w_mlp_in[i], w_mlp_out[i])
    return x_lat


def setup_inputs(seed=0):
    out = dict(first_inputs(seed))
    for name, value in second_inputs(seed + 1).items():
        if name != "x":
            out[name + "_2"] = value
    return out


def reference(
    x, norm1_w, w_in, conv_w, conv_b, dt_bias, a_log, d_skip, ssm_norm_w, w_attn_branch,
    w_ssm_branch, w_out, norm2_w, w_ffn_in, w_ffn_out, rel_bias, final_norm_w, c_2, ctx_2,
    c_ctx_2, w_mod_2, b_mod_2, g_norm_mix_2, g_norm_mlp_2, w_mlp_in_2, w_mlp_out_2, gla_w_in_2,
    gla_w_g1_2, gla_w_g2_2, gla_b_g_2, gla_g_head_2, gla_w_out_2, conv_w_pw1_2, conv_b_pw1_2,
    conv_w_dw_2, conv_b_dw_2, conv_ln_g_2, conv_ln_b_2, conv_w_pw2_2, conv_b_pw2_2,
    attn_w_qkv_2, attn_g_q_2, attn_g_k_2, attn_w_out_2,
):
    x = first_block(
        x, norm1_w, w_in, conv_w, conv_b, dt_bias, a_log, d_skip, ssm_norm_w, w_attn_branch,
        w_ssm_branch, w_out, norm2_w, w_ffn_in, w_ffn_out, rel_bias, final_norm_w,
    )
    return second_block(
        x, c_2, ctx_2, c_ctx_2, w_mod_2, b_mod_2, g_norm_mix_2, g_norm_mlp_2, w_mlp_in_2,
        w_mlp_out_2, gla_w_in_2, gla_w_g1_2, gla_w_g2_2, gla_b_g_2, gla_g_head_2, gla_w_out_2,
        conv_w_pw1_2, conv_b_pw1_2, conv_w_dw_2, conv_b_dw_2, conv_ln_g_2, conv_ln_b_2,
        conv_w_pw2_2, conv_b_pw2_2, attn_w_qkv_2, attn_g_q_2, attn_g_k_2, attn_w_out_2,
    )


_drawn_inputs = setup_inputs


def setup_inputs(seed=0):
    import zlib

    import numpy as np

    out = dict(_drawn_inputs(seed))
    spreads = {}
    factors = {'norm1_w': 2.782,
     'conv_b': 3.427,
     'ssm_norm_w': 4.72,
     'norm2_w': 3.795,
     'g_norm_mix_2': 5.091,
     'g_norm_mlp_2': 3.401,
     'gla_b_g_2': 4.261,
     'gla_g_head_2': 8.0,
     'conv_b_pw1_2': 43.289,
     'conv_b_dw_2': 37.326,
     'conv_ln_g_2': 43.538,
     'conv_ln_b_2': 178.795,
     'conv_b_pw2_2': 64.0,
     'attn_g_q_2': 28.379,
     'attn_g_k_2': 25.991,
     'd_skip': 2.9}
    for name, (base, spread) in spreads.items():
        noise = np.random.default_rng([zlib.crc32(name.encode()), seed]).standard_normal(out[name].shape)
        drawn = base * np.exp(spread * noise) if base else spread * noise
        out[name] = __import__('jax').numpy.asarray(drawn.astype(out[name].dtype))
    for name, factor in factors.items():
        out[name] = (out[name] * factor).astype(out[name].dtype)
    return out
```

```python
from contextlib import ExitStack, contextmanager

import numpy as np

import concourse.bass as bass
from concourse import mybir

F32 = mybir.dt.float32
F32R = mybir.dt.float32r
ALU = mybir.AluOpType
ACT = mybir.ActivationFunctionType
AX = mybir.AxisListType

P = 128
D = 1024
KC = D // P
S = 256
T2 = 2 * S
EPS = 1e-6
UC = 256
UW = KC * UC
RAW = 4
SPL = 2

HD = 64
GROUP_HEADS = 8
DILATIONS = (1, 4, 16)
NG = len(DILATIONS)
BUCKETS = 32
REL_MAX = 2048
NEG = -1e30
AW = NG * GROUP_HEADS * HD
DI = 2 * D
SSM_HEADS = DI // HD
SSM_G = 4
NST = 128
XBC = DI + 2 * SSM_G * NST
FF = 2816
FC = FF // P
XC = XBC // P
LAYERS = 4
FF2 = 4 * D
GH = 4
DV = 256
GCH = 64
TAPS = 31
PADT = TAPS // 2
QH = 16
MODC = 6 * KC


def layout(items):
    at, n = {}, 0
    for name, w in items:
        at[name] = (n, w)
        n += w
    return at, n


VEC, NVEC = layout([
    ("norm1", KC), ("norm2", KC), ("final", KC), ("conv_w", 4 * XC), ("conv_b", XC), ("dskip", DI // P),
    ("ssm_norm", DI // P), ("b_mod", LAYERS * MODC), ("g_mix", LAYERS * KC), ("g_mlp", LAYERS * KC),
    ("gla_b", 2 * 2 * GH), ("pw1_b", 2 * KC), ("dw_w", KC * TAPS), ("dw_b", KC), ("ln_g", KC), ("ln_b", KC),
    ("pw2_b", KC), ("g_q", 1), ("g_k", 1), ("c", 2 * KC), ("dt_b", SSM_HEADS), ("a_log", SSM_HEADS),
    ("g_head", 2 * DV)])
CST, NCST = layout([("ident", P), ("ones", P), ("tri", P), ("blocks", P), ("causal", GCH), ("anticausal", GCH),
                    ("restart", T2)])


def constants():
    c = np.zeros((P, NCST), np.float32)

    def put(name, a):
        o, w = CST[name]
        c[:, o:o + w] = a

    i = np.arange(P)
    put("ident", np.eye(P))
    put("ones", np.ones((P, P)))
    put("tri", i[:, None] <= i[None, :])
    put("blocks", i[:, None] // HD == i[None, :] // HD)
    j = np.arange(GCH)
    put("causal", (i[:, None] % GCH) <= j[None, :])
    put("anticausal", (i[:, None] % GCH) >= j[None, :])
    t = np.arange(T2)
    put("restart", np.broadcast_to(t % GCH != 0, (P, T2)))

    dist = 255 - np.arange(384)
    d = np.clip(dist, 0, None)
    exact = BUCKETS // 2
    large = exact + (np.log(np.maximum(d, 1).astype(np.float32) / exact) / np.float32(np.log(REL_MAX / exact))
                     * (BUCKETS - exact)).astype(np.int32)
    bucket = np.where(d < exact, d, np.minimum(large, BUCKETS - 1))
    hot = (np.arange(BUCKETS)[:, None] == bucket[None, :]).astype(np.float32)
    mask = np.zeros((NG, 384), np.float32)
    for g, dil in enumerate(DILATIONS):
        ok = (dist >= 0) & (dist % dil == 0) & (dist // dil <= P)
        mask[g] = np.where(ok, 0.0, NEG)
    rel = np.zeros((BUCKETS, 384 + NG * 384), np.float32)
    rel[:, :384] = hot
    rel[:GROUP_HEADS, 384:] = mask.reshape(1, -1)

    n = HD // 4
    inv = np.float32(10000.0) ** (-np.arange(n, dtype=np.float32) / np.float32(n))
    tok = np.arange(S)
    ang = np.concatenate([(tok // 64).astype(np.float32)[:, None] * inv,
                          (tok % 64).astype(np.float32)[:, None] * inv], axis=-1)
    rope = np.zeros((P, P + 2 * S), np.float32)
    half = HD // 2
    f = i % HD
    for m in range(P):
        if f[m] < half:
            rope[m + half, m] = -1.0
        else:
            rope[m - half, m] = 1.0
    rope[:, P:P + S] = np.cos(ang).T[f % half]
    rope[:, P + S:] = np.sin(ang).T[f % half]
    return c, rel, rope


class Role:

    def __init__(self, eng, sems):
        self.eng, self.sems, self.n, self.loops, self.started = eng, sems, {}, [], False

    def value(self, key):
        v = self.n.get(key, 0)
        for reg, per in self.loops:
            if per.get(key, 0):
                v = reg * per[key] + v
        return v

    def next(self, name, k=1, key=None):
        key = key or "w " + name
        self.n[key] = self.n.get(key, 0) + k
        return self.sems[name], self.value(key)

    def made(self, name):
        self.n["m " + name] = self.n.get("m " + name, 0) + 1
        return self.sems[name], 1

    def own(self, name):
        return self.sems[name], self.value("m " + name)

    @contextmanager
    def loop(self, count, per):
        before = dict(self.n)
        with self.eng.Fori(0, count) as i:
            self.loops.append((i, per))
            yield i
            self.loops.pop()
        got = {k: v - before.get(k, 0) for k, v in self.n.items() if v != before.get(k, 0)}
        assert got == {k: v for k, v in per.items() if v}, (got, per)
        for k, v in got.items():
            self.n[k] += v * (count - 1)

    def groups(self, n, body):
        whole = n // 4
        peel = 1 if self.started else 2
        self.started = True
        if whole < peel + 2:
            for k in range(n):
                body(k, k % 4, k // 2)
            return
        for k in range(4 * peel):
            if k == 4 * peel - 4:
                before = dict(self.n)
            body(k, k % 4, k // 2)
        per = {k: v - before.get(k, 0) for k, v in self.n.items() if v != before.get(k, 0)}
        with self.loop(whole - peel, per) as i:
            for j in range(4):
                body(i * 4 + (4 * peel + j), j, i * 2 + (2 * peel + j // 2))
        for k in range(4 * whole, n):
            body(k, k % 4, k // 2)


SEMS = (["raw_loaded%d" % i for i in range(RAW)] + [
    "params_loaded", "x_loaded", "rel_table", "rel_stored", "rel_loaded0", "rel_loaded1", "wg2_loaded",
    "rope_loaded", "result_ready", "stored",
    "hi_ready", "lo_ready", "chunk_ready", "chunk_taken", "part_ready", "part_hi", "part_lo",
    "dve_step", "act_step", "norm_input", "square_ready", "square_summed", "stat_read", "rstd_ready",
    "gate_ready", "rel_rows", "cin_ready", "conv_ready",
    "scores_ready", "logits_taken", "neg_max", "exp_ready", "recip_ready", "probs_ready", "turned_ready",
    "turned_taken", "values_ready",
    "dt_abs", "dt_log", "dta_ready", "sums_ready", "xs_turned", "xs_taken", "b_turned", "b_taken",
    "toend_in", "toend_exp", "toend_ready", "state_ready", "state_taken", "cb_ready", "cb_taken",
    "spread_ready", "gap_ready", "decay_ready", "spread_exp", "mix_ready", "y_ready", "y_taken",
    "zg_ready", "zabs_ready", "zlog_ready", "cum_ready", "expb_ready", "gaps_ready", "kd_exp", "kd_ready",
    "kdt_ready", "att_ready", "att_taken", "s_ready", "s_taken", "o_ready", "o_taken", "osq_ready",
    "onorm_ready", "ot_ready", "ot_taken", "dw_ready", "mean_ready", "mean_taken", "centred", "ln_ready",
    "qstat_read", "qn_ready", "rot_ready", "rot_taken"])


def unit_plan():
    u = []

    def run(what, n, mod=None, m0=0):
        for k in range(n):
            u.append((what, k))
            if mod is not None:
                u.append((("mod", mod), m0 + k))

    run("q", 6, 0, 0)
    run("k", 6, 0, 6)
    run("v", 6)
    run("attn_branch", 4)
    run("xbc", 12, 0, 12)
    run("dt", 1)
    run("z", 8)
    run("ssm", 8)
    run("gates", 8)
    run("out", 4)
    for p, n in enumerate((8, 8, 6)):
        run(("ffn_in", p), n)
        run(("ffn_out", p), 4)
    for i in range(LAYERS):
        if i % 3 == 0:
            run(("gla_qk", i // 3), 4)
            run(("gla_v", i // 3), 4)
            run(("gla_g1", i // 3), 1)
            run(("gla_r", i // 3), 4)
            run(("gla_out", i // 3), 4)
        elif i % 3 == 1:
            run("pw1", 8)
            run("pw2", 4)
        else:
            run("att_qk", 6)
            run("att_v", 1)
            run("att_out", 4)
        for p in range(4):
            mod = i + 1 if i + 1 < LAYERS and p < 3 else None
            run((("mlp_in", i), p), 4, mod, 8 * p)
            run((("mlp_out", i), p), 4, mod, 8 * p + 4)
    return u


class Buffers:
    pass


def place(nc, ctx):
    b = Buffers()

    def sb(stack, name, shape, dt=F32):
        return stack.enter_context(nc.sbuf_tensor(name, shape, dt))

    b.vec = sb(ctx, "vec", [P, NVEC])
    b.cst = sb(ctx, "cst", [P, NCST])
    b.raw = [sb(ctx, f"raw{i}", [P, KC, UC]) for i in range(RAW)]
    b.whi = [sb(ctx, f"whi{i}", [P, KC, UC], F32R) for i in range(SPL)]
    b.wlo = [sb(ctx, f"wlo{i}", [P, KC, UC], F32R) for i in range(SPL)]
    b.x = sb(ctx, "x", [P, KC, T2])
    b.part = [sb(ctx, f"part{i}", [P, T2]) for i in range(4)]
    b.rstd = sb(ctx, "rstd", [P, T2])
    b.chi = sb(ctx, "chi", [P, 2 * KC], F32R)
    b.clo = sb(ctx, "clo", [P, 2 * KC], F32R)
    b.mod = [sb(ctx, f"mod{i}", [P, 2 * MODC]) for i in range(2)]
    b.modg = sb(ctx, "modg", [P, 2 * KC * 2])
    b.sg = [sb(ctx, f"sg{i}", [P, T2]) for i in range(2)]
    b.small = sb(ctx, "small", [P, 64])

    with ExitStack() as one:
        b.xn1 = [sb(one, f"xn1{n}", [P, KC, S], F32R) for n in ("hi", "lo")]
        b.attn_out = sb(one, "attn_branch_out", [P, KC, S])
        with ExitStack() as st:
            b.ao = [sb(st, f"ao{n}", [P, 4, S], F32R) for n in ("hi", "lo")]
            b.qk = sb(st, "qk", [P, 2 * AW // P, S])
            b.v = sb(st, "v", [P, 2, AW])
            b.rel = sb(st, "rel", [BUCKETS, 384 * (1 + NG)])
            b.relb = sb(st, "relb", [BUCKETS, NG * GROUP_HEADS])
            b.reltab = sb(st, "reltab", [GROUP_HEADS, NG, 384])
            b.bias = [sb(st, f"bias{i}", [P, NG, S]) for i in range(2)]
            b.logits = [sb(st, f"logits{i}", [P, NG, S]) for i in range(2)]
            b.turned = sb(st, "turned", [P, 6, P])
        b.y = sb(one, "y", [P, DI // P, S])
        with ExitStack() as st:
            b.xbc = sb(st, "xbc", [P, XC, S])
            with ExitStack() as cv:
                b.cin = [sb(cv, f"cin{i}", [P, S + 4]) for i in range(2)]
                b.cacc = [sb(cv, f"cacc{i}", [P, S]) for i in range(2)]
            b.xdt = sb(st, "xdt", [P, 2, DI])
            b.dt = sb(st, "dt", [P, 8, 2, SSM_HEADS])
            b.toend_x = sb(st, "toend_x", [P, 512])
            b.state1 = sb(st, "state1", [P, SSM_G, 512])
            b.bt = sb(st, "bt", [P, SSM_G, P])
            b.cbm = sb(st, "cbm", [P, SSM_G, P])
            b.gap = [sb(st, f"gap{i}", [P, 4, P]) for i in range(2)]
        with ExitStack() as st:
            b.big = [sb(st, f"big{n}", [P, DI // P, S], F32R) for n in ("hi", "lo")]
            b.ssm_out = sb(st, "ssm_branch_out", [P, KC, S])
    b.xn = [sb(ctx, f"xn{n}", [P, KC, T2], F32R) for n in ("hi", "lo")]
    with ExitStack() as st:
        b.hid = [sb(st, f"hid{n}", [P, KC, T2], F32R) for n in ("hi", "lo")]
    with ExitStack() as st:
        b.gqk = sb(st, "gqk", [P, 2 * GH, T2])
        b.gv = sb(st, "gv", [P, 4, D])
        b.go = sb(st, "go", [P, 4, D])
        b.g1 = sb(st, "g1", [48, T2])
        b.wg2 = sb(st, "wg2", [48, 512])
        b.ends = [sb(st, f"ends{i}", [P, 8]) for i in range(2)]
        b.qb = [sb(st, f"qb{i}", [P, T2]) for i in range(2)]
        b.kb = [sb(st, f"kb{i}", [P, T2]) for i in range(2)]
        b.kdt = [sb(st, f"kdt{i}", [P, 4, P]) for i in range(2)]
        b.att = [sb(st, f"att{i}", [P, 4, GCH]) for i in range(2)]
        b.gs2 = [[sb(st, f"gs{i}{j}", [P, DV]) for j in range(2)] for i in range(2)]
    with ExitStack() as st:
        b.u = sb(st, "u", [P, KC, 2, S + TAPS - 1])
        b.dw = sb(st, "dw", [P, KC, T2])
        b.nmean = sb(st, "nmean", [P, T2])
    with ExitStack() as st:
        b.rope = sb(st, "rope", [P, P + 2 * S])
        b.aqk = sb(st, "aqk", [P, 12, T2])
        b.av = sb(st, "av", [P, 4, UC])
        b.prob = [sb(st, f"prob{i}", [P, T2]) for i in range(2)]
        b.pt = sb(st, "pt", [P, 4, P])
    b.bank = [ctx.enter_context(nc.psum_tensor(f"bank{i}", [P, 512], F32)) for i in range(8)]
    return b


def loads(nc, b, dram, R, sp):
    sp.dma_start(b.vec[:], dram["vec"]).then_inc(R.sems["params_loaded"], 16)
    sp.dma_start(b.cst[:], dram["cst"]).then_inc(R.sems["params_loaded"], 16)
    sp.dma_start(b.x[:], dram["x"]).then_inc(R.sems["x_loaded"], 16)
    sp.dma_start(b.rel[:], dram["rel"]).then_inc(R.sems["params_loaded"], 16)
    sp.dma_start(b.relb[:], dram["relb"]).then_inc(R.sems["params_loaded"], 16)
    wall = dram["wall"]
    units = wall.shape[0]

    def unit(u, j, first):
        if not first:
            sp.wait_ge(*R.next("lo_ready"))
        src = wall[u] if isinstance(u, int) else wall[bass.ds(u, 1)].rearrange("a p n -> (a p) n")
        sp.dma_start(b.raw[j][:].rearrange("p k n -> p (k n)"), src).then_inc(R.sems[f"raw_loaded{j}"], 16)

    def run(u0, n):
        k = 0
        while k < n and (u0 + k) % RAW:
            unit(u0 + k, (u0 + k) % RAW, u0 + k < RAW)
            k += 1
        turns = (n - k) // RAW
        if turns > 1:
            with R.loop(turns, {"w lo_ready": RAW}) as i:
                for j in range(RAW):
                    unit(i * RAW + (u0 + k + j), j, False)
            k += RAW * turns
        while k < n:
            unit(u0 + k, (u0 + k) % RAW, u0 + k < RAW)
            k += 1

    run(0, RAW)
    sp.wait_ge(*R.next("rel_table"))
    sp.dma_start(dram["reltab"], b.reltab[:]).then_inc(R.sems["rel_stored"], 16)
    sp.wait_ge(R.sems["rel_stored"], 16)
    tab = dram["reltab"]

    def window(h):
        return bass.AP(tensor=tab.tensor, offset=tab.offset + h * NG * 384, ap=[[1, P], [384, NG], [1, S]])

    at = dram["at"]
    run(RAW, at["attn_branch"])
    for h in range(GROUP_HEADS):
        if h >= 2:
            sp.wait_ge(R.sems["logits_taken"], 2 * (h - 1))
        sp.dma_start(b.bias[h % 2][:], window(h)).then_inc(R.sems[f"rel_loaded{h % 2}"], 16)
    done = at["attn_branch"] + RAW
    for i in range(LAYERS):
        if i % 3 == 0:
            first = at[("gla_g1", i // 3)]
            run(done, first - done)
            done = first
            sp.wait_ge(R.sems["chunk_taken"], 2 * at[("gla_v", i // 3)])
            sp.dma_start(b.wg2[:], dram["wg2"][i // 3]).then_inc(R.sems["wg2_loaded"], 16)
        elif i % 3 == 2:
            first = at["att_v"]
            run(done, first - done)
            done = first
            sp.wait_ge(R.sems["chunk_taken"], 2 * at["att_qk"] + 4)
            sp.dma_start(b.rope[:], dram["rope"]).then_inc(R.sems["rope_loaded"], 16)
    run(done, units - done)
    sp.wait_ge(*R.next("result_ready"))
    sp.dma_start(dram["out"], b.x[:, :, 0:S]).then_inc(R.sems["stored"], 16)
    sp.wait_ge(R.sems["stored"], 16)


def products(nc, b, R, pe, at):
    mm = nc.tensor.matmul
    g = {"chunks": 0, "unit": 0, "norms": 0}
    bank = b.bank
    cst = lambda name: b.cst[:, CST[name][0]:CST[name][0] + CST[name][1]]
    ident, ones, tri = cst("ident"), cst("ones"), cst("tri")

    def three(out, w, x, first, last):
        (wh, wl), (xh, xl) = w, x
        mm(out, wh, xh, start=first, stop=False)
        mm(out, wh, xl, start=False, stop=False)
        return mm(out, wl, xh, start=False, stop=last)

    def unit(x, t, kc=KC, k0=0, tokens_out=False):
        s = g["unit"] % SPL
        pe.wait_ge(*R.next("lo_ready"))
        for c in range(2):
            if g["chunks"] >= 4:
                pe.wait_ge(*R.next("chunk_taken"))
            out = bank[2 * s + c]
            if not tokens_out:
                for k in range(kc):
                    last = three(out[:, 0:t], [w[s][:, k, c * P:(c + 1) * P] for w in (b.whi, b.wlo)],
                                 [h[:, k0 + k, 0:t] for h in x], k == 0, k == kc - 1)
            else:
                tiles = t // P // 2
                for a in range(tiles):
                    o = (c * tiles + a) * P
                    for k in range(kc):
                        last = three(out[:, a * UC:(a + 1) * UC], [h[:, k0 + k, o:o + P] for h in x],
                                     [w[s][:, k, :] for w in (b.whi, b.wlo)], k == 0, k == kc - 1)
            last.then_inc(*R.made("chunk_ready"))
            g["chunks"] += 1
        g["unit"] += 1

    cond = [h[:].rearrange("p (k s) -> p k s", s=2) for h in (b.chi, b.clo)]

    def stage(n, x, t, mod=False, **kw):
        if mod:
            R.groups(2 * n, lambda k, j, k2: unit(cond, 2) if j % 2 else unit(x, t, **kw))
        else:
            R.groups(n, lambda k, j, k2: unit(x, t, **kw))

    def operand(parts):
        pe.wait_ge(*R.next("part_lo", parts))

    def norm_sum(t, lhs=ones, n=KC):
        if g["norms"]:
            pe.wait_ge(*R.next("stat_read"))
        g["norms"] += 1
        for c in range(n):
            pe.wait_ge(*R.next("square_ready"))
            mm(bank[4][:, 0:t], lhs, b.part[c % 2][:, 0:t], start=(c == 0), stop=(c == n - 1)) \
                .then_inc(*R.made("square_summed"))

    pe.wait_ge(R.sems["params_loaded"], 64)
    for gr in range(NG):
        last = mm(bank[5 + gr][0:GROUP_HEADS, 0:384], b.relb[:, gr * GROUP_HEADS:(gr + 1) * GROUP_HEADS],
                  b.rel[:, 0:384], start=True, stop=True)
    last.then_inc(*R.made("rel_rows"))
    operand(1)
    norm_sum(S)
    operand(KC)
    stage(6, b.xn1, S, mod=True)
    stage(6, b.xn1, S, mod=True)
    stage(6, b.xn1, S, tokens_out=True)

    pe.wait_ge(R.sems["chunk_taken"], 2 * at["attn_branch"])
    steps = [(h, qt) for h in range(GROUP_HEADS) for qt in range(2)]

    def scores(n):
        h, qt = steps[n]
        nk = P * (qt + 1)
        base = HD * (h % 2)
        if n >= 2:
            pe.wait_ge(*R.next("logits_taken"))
        for gr in range(NG):
            c = gr * 4 + h // 2
            out = bank[4 + 2 * (n % 2) + gr // 2][:, (gr % 2) * S:(gr % 2) * S + nk]
            last = mm(out, b.qk[base:base + HD, c, qt * P:(qt + 1) * P],
                      b.qk[base:base + HD, 12 + c, 0:nk], start=True, stop=True)
        last.then_inc(*R.made("scores_ready"))

    before = R.n["w part_lo"]
    scores(0)
    for n, (h, qt) in enumerate(steps):
        if n + 1 < len(steps):
            scores(n + 1)
        kt = qt + 1
        pe.wait_ge(*R.next("probs_ready"))
        for i in range(NG * kt):
            last = nc.tensor.transpose(bank[i // 4][:, (i % 4) * P:(i % 4 + 1) * P],
                                       b.logits[n % 2][:, i // kt, (i % kt) * P:(i % kt + 1) * P], ident)
        last.then_inc(*R.made("turned_ready"))
        pe.wait_ge(*R.next("turned_taken"))
        if n >= 8 and n % 4 == 0:
            pe.wait_ge(R.sems["part_lo"], before + h // 2 - 1)
        base = HD * (h % 2)
        for i in range(NG * kt):
            col = (i // kt) * GROUP_HEADS * HD + h * HD
            last = mm(bank[2 + (h // 2) % 2][base:base + HD, qt * P:(qt + 1) * P],
                      b.v[:, i % kt, col:col + HD], b.turned[:, i, :], start=(i == 0), stop=(i == NG * kt - 1))
        last.then_inc(*R.made("values_ready"))
    operand(4)
    stage(4, b.ao, S, kc=4)
    stage(12, b.xn1, S, mod=True)
    stage(1, b.xn1, S, tokens_out=True)

    for ct in range(2):
        for gr in range(SSM_G):
            if gr == 0 and ct == 0:
                pe.wait_ge(R.sems["chunk_taken"], 2 * at["z"])
            if ct * SSM_G + gr >= 2:
                pe.wait_ge(*R.next("xs_taken"))
            for c in range(4):
                last = nc.tensor.transpose(bank[4 + gr % 2][:, c * P:(c + 1) * P],
                                           b.xbc[:, gr * 4 + c, ct * P:(ct + 1) * P], ident)
            last.then_inc(*R.made("xs_turned"))
    pe.wait_ge(*R.next("dta_ready"))
    for ct in range(2):
        mm(bank[6][:, ct * 64:ct * 64 + 32], tri, b.dt[:, 2, ct, :], start=True, stop=True)
        last = mm(bank[6][:, ct * 64 + 32:ct * 64 + 64], ones, b.dt[:, 2, ct, :], start=True, stop=True)
    last.then_inc(*R.made("sums_ready"))
    for gr in range(SSM_G):
        last = nc.tensor.transpose(bank[7][:, gr * P:(gr + 1) * P], b.xbc[:, 16 + gr, 0:P], ident)
    last.then_inc(*R.made("b_turned"))
    pe.wait_ge(*R.next("xs_taken", 2))
    pe.wait_ge(*R.next("b_taken"))
    for gr in range(SSM_G):
        pe.wait_ge(*R.next("toend_ready"))
        mm(bank[4 + gr % 2][:, :], b.bt[:, gr, :], b.toend_x[:], start=True, stop=True) \
            .then_inc(*R.made("state_ready"))
    pe.wait_ge(*R.next("state_taken", SSM_G))
    spread = [5, 6]

    def spread_sums(n):
        ct, quad = n // 8, n % 8
        if 2 <= n < 10:
            pe.wait_ge(*R.next("gap_ready"))
        elif n >= 10:
            pe.wait_ge(*R.next("spread_exp"))
        for h in range(4):
            last = mm(bank[spread[n % 2]][:, h * P:(h + 1) * P],
                      b.dt[:, 2, ct, quad * 4 + h:quad * 4 + h + 1].to_broadcast([P, P]), tri,
                      start=True, stop=True)
        last.then_inc(*R.made("spread_ready"))

    for ct in range(2):
        if ct:
            pe.wait_ge(*R.next("cb_taken"))
        for gr in range(SSM_G):
            last = mm(bank[4][:, gr * P:(gr + 1) * P], b.xbc[:, 16 + gr, ct * P:(ct + 1) * P],
                      b.xbc[:, 20 + gr, ct * P:(ct + 1) * P], start=True, stop=True)
        last.then_inc(*R.made("cb_ready"))
        spread_sums(ct * 8)
        for quad in range(8):
            n = ct * 8 + quad
            if quad < 7:
                spread_sums(n + 1)
            pe.wait_ge(*R.next("mix_ready"))
            if n >= 2:
                pe.wait_ge(*R.next("y_taken"))
            for h in range(4):
                head = quad * 4 + h
                out = bank[n % 2][HD * (h % 2):HD * (h % 2) + HD, (h // 2) * P:(h // 2 + 1) * P]
                last = mm(out, b.xdt[:, ct, head * HD:(head + 1) * HD], b.gap[n % 2][:, h, :],
                          start=True, stop=(ct == 0))
                if ct:
                    last = mm(out, b.state1[:, head // 8, (head % 8) * HD:(head % 8 + 1) * HD],
                              b.part[2 + n % 2][:, h * P:(h + 1) * P], start=False, stop=True)
            last.then_inc(*R.made("y_ready"))
    pe.wait_ge(*R.next("y_taken", 2))
    stage(8, b.xn1, S)
    for gr in range(SSM_G):
        norm_sum(S, n=4)
    operand(DI // P)
    stage(4, b.big, S)
    stage(4, b.big, S, k0=KC)
    stage(8, b.xn1, S)
    operand(KC)
    stage(4, b.big, S)
    norm_sum(S)
    operand(KC)
    for n in (8, 8, 6):
        stage(n, b.xn1, S)
        operand(n)
        stage(4, b.big, S, kc=n)
    norm_sum(S)

    def gla(i, t):
        last_layer = i == LAYERS - 1
        stage(4, b.xn, T2)
        stage(4, b.xn, T2, tokens_out=True)
        stage(1, b.xn, T2)
        pe.wait_ge(R.sems["chunk_taken"], 2 * at[("gla_r", i // 3)])
        pe.wait_ge(R.sems["wg2_loaded"], 16 * (i // 3 + 1))
        for h in range(GH):
            for d in range(2):
                mm(bank[4][:, :], b.wg2[32 * d:32 * d + 16, h * P:(h + 1) * P], b.g1[32 * d:32 * d + 16, :],
                   start=True, stop=True).then_inc(*R.made("zg_ready"))
                pe.wait_ge(*R.next("kd_ready"))
                for tt in range(4):
                    last = nc.tensor.transpose(bank[5][:, tt * P:(tt + 1) * P], b.part[1][:, tt * P:(tt + 1) * P],
                                               ident)
                last.then_inc(*R.made("kdt_ready"))
                for n in range(8):
                    half = 64 * (n % 2)
                    last = mm(bank[6][half:half + 64, (n // 2) * GCH:(n // 2 + 1) * GCH],
                              b.kb[d][:, n * GCH:(n + 1) * GCH], b.qb[d][:, n * GCH:(n + 1) * GCH],
                              start=True, stop=True)
                last.then_inc(*R.made("att_ready"))
                pe.wait_ge(*R.next("att_taken"))
            order = [[4, 5, 6, 7, 0, 1, 2, 3], [7, 6, 5, 4, 3, 2, 1, 0]]
            for s in range(8):
                for d in range(2):
                    n = order[d][s]
                    half, tt = 64 * (n % 2), n // 2
                    vv = b.gv[half:half + 64, tt, h * DV:(h + 1) * DV]
                    if s < 7:
                        if s:
                            pe.wait_ge(*R.next("s_taken"))
                        mm(bank[d][:, 0:DV], b.kdt[d][half:half + 64, tt, :], vv, start=True, stop=True) \
                            .then_inc(*R.made("s_ready"))
                    elif s:
                        pe.wait_ge(*R.next("s_taken"))
                    if s < 4 and last_layer:
                        continue
                    if s == 4 and not last_layer:
                        pe.wait_ge(*R.next("o_taken"))
                    if s == (4 if last_layer else 0) and h:
                        pe.wait_ge(*R.next("o_taken"))
                    out = bank[2 + d][half:half + 64, (tt % 2) * DV:(tt % 2 + 1) * DV]
                    if s:
                        mm(out, b.qb[d][:, n * GCH:(n + 1) * GCH], b.gs2[d][s % 2][:], start=True, stop=False)
                    last = mm(out, b.att[d][half:half + 64, tt, :], vv, start=(s == 0), stop=True)
                    if s % 4 == 3:
                        last.then_inc(*R.made("o_ready"))
        pe.wait_ge(*R.next("o_taken", 2))
        for fc in range(KC):
            if fc == 0:
                pe.wait_ge(*R.next("onorm_ready"))
            if fc >= 2:
                pe.wait_ge(*R.next("ot_taken"))
            for tt in range(t // P):
                last = nc.tensor.transpose(bank[5 + fc % 2][:, tt * P:(tt + 1) * P],
                                           b.go[:, tt, fc * P:(fc + 1) * P], ident)
            last.then_inc(*R.made("ot_ready"))
        pe.wait_ge(*R.next("ot_taken", 2))
        stage(4, b.xn, t)
        operand(KC)
        stage(4, b.xn, t)

    def conv():
        stage(8, b.xn, T2)
        for c in range(KC):
            pe.wait_ge(*R.next("dw_ready"))
            last = mm(bank[5][:, :], ones, b.dw[:, c, :], start=(c == 0), stop=(c == KC - 1))
        last.then_inc(*R.made("mean_ready"))
        norm_sum(T2)
        operand(KC)
        stage(4, b.xn, T2)

    def attention():
        stage(6, b.xn, T2)
        stage(1, b.xn, T2, tokens_out=True)
        pe.wait_ge(R.sems["chunk_taken"], 2 * at["att_out"])
        pe.wait_ge(R.sems["rope_loaded"], 16)
        for c in range(12):
            pe.wait_ge(*R.next("square_ready"))
            if c >= 2:
                pe.wait_ge(*R.next("qstat_read"))
            mm(bank[4 + c % 2][:, :], cst("blocks"), b.part[c % 2][:, :], start=True, stop=True) \
                .then_inc(*R.made("square_summed"))
            pe.wait_ge(*R.next("qn_ready"))
            if c >= 2:
                pe.wait_ge(*R.next("rot_taken"))
            mm(bank[6 + c % 2][:, 0:S], b.rope[:, 0:P], b.aqk[:, c, 0:S], start=True, stop=True) \
                .then_inc(*R.made("rot_ready"))
        pe.wait_ge(*R.next("qstat_read", 2))
        pe.wait_ge(*R.next("rot_taken", 2))
        steps = [(h, qt) for h in range(QH) for qt in range(4)]

        def scores(n):
            h, qt = steps[n]
            base = HD * (h % 2)
            keys = slice(0, T2) if qt < 2 else slice(S, T2)
            if n >= 2:
                pe.wait_ge(*R.next("exp_ready"))
            mm(bank[4 + n % 2][:, 0:keys.stop - keys.start], b.aqk[base:base + HD, h // 2, qt * P:(qt + 1) * P],
               b.aqk[base:base + HD, 8 + h // 4, keys], start=True, stop=True).then_inc(*R.made("scores_ready"))

        before = R.n["w part_lo"]
        scores(0)
        for n, (h, qt) in enumerate(steps):
            if n + 1 < len(steps):
                scores(n + 1)
            tiles = range(4) if qt < 2 else range(2, 4)
            pe.wait_ge(*R.next("probs_ready"))
            for i, _ in enumerate(tiles):
                last = nc.tensor.transpose(bank[6][:, i * P:(i + 1) * P], b.prob[n % 2][:, i * P:(i + 1) * P], ident)
            last.then_inc(*R.made("turned_ready"))
            pe.wait_ge(*R.next("turned_taken"))
            if n % 8 == 0 and n >= 16:
                pe.wait_ge(R.sems["part_lo"], before + h // 2 - 1)
            base = HD * (h % 2)
            for i, kt in enumerate(tiles):
                last = mm(bank[2 + (h // 2) % 2][base:base + HD, qt * P:(qt + 1) * P],
                          b.av[:, kt, (h // 4) * HD:(h // 4 + 1) * HD], b.pt[:, i, :],
                          start=(i == 0), stop=(i == len(tiles) - 1))
            last.then_inc(*R.made("values_ready"))
        operand(KC)
        stage(4, b.xn, T2)

    for i in range(LAYERS):
        t = S if i == LAYERS - 1 else T2
        norm_sum(T2)
        operand(KC)
        if i % 3 == 0:
            gla(i, t)
        elif i % 3 == 1:
            conv()
        else:
            attention()
        norm_sum(t)
        operand(KC)

        def piece(mod):
            stage(4, b.xn, t, mod=mod)
            operand(KC)
            stage(4, b.hid, t, mod=mod)

        if i < LAYERS - 1:
            per = {"w lo_ready": 16, "w chunk_taken": 32, "m chunk_ready": 32, "w part_lo": KC}
            with R.loop(3, per):
                piece(True)
        else:
            per = {"w lo_ready": 8, "w chunk_taken": 16, "m chunk_ready": 16, "w part_lo": KC}
            with R.loop(3, per):
                piece(False)
        piece(False)


def splits_and_functions(nc, b, R, act, at):
    fn = nc.scalar.activation
    g = {"unit": 0, "taken": 0, "part": 0}
    bank = b.bank
    total = at["units"]

    def split():
        u = g["unit"]
        act.wait_ge(*R.next(f"raw_loaded{u % RAW}", 16))
        if u >= SPL:
            act.wait_ge(*R.next("chunk_ready", 2, "hl_free"))
        nc.scalar.copy(b.whi[u % SPL][:], b.raw[u % RAW][:]).then_inc(*R.made("hi_ready"))
        g["unit"] += 1

    def part(dst, src=None, width=None, by_chunk=None):
        if by_chunk is None:
            act.wait_ge(*R.next("part_ready"))
        else:
            act.wait_ge(R.sems["chunk_taken"], by_chunk)
        src = b.part[g["part"] % 4][:, 0:width] if src is None else src
        nc.scalar.copy(dst, src).then_inc(*R.made("part_hi"))
        g["part"] += 1

    def chunk():
        act.wait_ge(*R.next("chunk_ready", 1, "evac"))

    def room():
        act.wait_ge(R.sems["chunk_taken"], R.value("evac") + (-2))

    def stage(n, body=None, mod=False, last=False):
        def one(k, j, k2):
            if not (last and isinstance(k, int) and k == n - 1):
                split()
            if mod and j % 2:
                R.n["evac"] = R.n.get("evac", 0) + 2
            elif body is None:
                R.n["evac"] = R.n.get("evac", 0) + 2
            else:
                body(k2 if mod else k)
            g["taken"] += 1
        R.groups(2 * n if mod else n, one)

    def bank_of(c):
        return bank[2 * (g["taken"] % SPL) + c]

    def squares(src, t, n=KC):
        act.wait_ge(*R.next("norm_input"))
        act.wait_ge(R.sems["part_lo"], R.value("m part_hi"))
        for c in range(n):
            if c >= 2:
                act.wait_ge(*R.next("square_summed"))
            fn(b.part[c % 2][:, 0:t], src(c), ACT.Square).then_inc(*R.made("square_ready"))
        act.wait_ge(*R.next("square_summed", 2))

    def rstd(t, width):
        fn(b.rstd[:, 0:t], bank[4][:, 0:t], ACT.Ln, bias=b.small[:, 63:64], scale=1.0 / width) \
            .then_inc(*R.made("stat_read"))
        act.wait_ge(*R.own("stat_read"))
        fn(b.rstd[:, 0:t], b.rstd[:, 0:t], ACT.Exp, scale=-0.5).then_inc(*R.made("rstd_ready"))

    def norm(t):
        squares(lambda c: b.x[:, c, 0:t], t)
        rstd(t, D)

    act.wait_ge(R.sems["params_loaded"], 64)
    act.wait_ge(R.sems["dve_step"], 1)
    cv = VEC["c"][0]
    fn(b.small[:, 0:16], b.vec[:, cv:cv + 16], ACT.Sigmoid).then_inc(*R.made("gate_ready"))
    part(b.chi[:], width=16)
    split()
    act.wait_ge(R.sems["x_loaded"], 16)
    norm(S)
    for c in range(KC):
        part(b.xn1[0][:, c, :], width=S)
    stage(6, mod=True)
    stage(6, mod=True)
    stage(6)

    def exponent(n):
        act.wait_ge(*R.next("neg_max"))
        nk = P * (n % 2 + 1)
        fn(b.logits[n % 2][:, :, 0:nk], b.logits[n % 2][:, :, 0:nk], ACT.Exp, bias=b.small[:, 20 + n % 2:21 + n % 2],
           accum_out=b.small[:, 24 + n % 2:25 + n % 2]).then_inc(*R.made("exp_ready"))

    for n in range(2 * GROUP_HEADS):
        exponent(n)
        act.wait_ge(*R.next("recip_ready"))
        nk = P * (n % 2 + 1)
        fn(b.logits[n % 2][:, :, 0:nk], b.logits[n % 2][:, :, 0:nk], ACT.Copy,
           scale=b.small[:, 28 + n % 2:29 + n % 2]).then_inc(*R.made("probs_ready"))
        if n % 4 == 3:
            part(b.ao[0][:, n // 4, :], width=S)
    stage(4)

    def conv_in(k):
        for c in range(2):
            chunk()
            nc.scalar.copy(b.cin[c][:, 3:3 + S], bank_of(c)[:, 0:S]).then_inc(*R.made("cin_ready"))
        for c in range(2):
            act.wait_ge(*R.next("conv_ready"))
            fn(b.sg[c][:, 0:S], b.cacc[c][:], ACT.Sigmoid).then_inc(*R.made("gate_ready"))

    stage(12, conv_in, mod=True)
    stage(1)

    al = VEC["a_log"][0]
    fn(b.dt[:, 7, 0, :], b.vec[:, al:al + SSM_HEADS], ACT.Exp).then_inc(*R.made("act_step"))
    act.wait_ge(*R.next("dt_abs"))
    ab = b.dt[:, 1, :, :]
    fn(ab, ab, ACT.Exp, scale=-1.0).then_inc(*R.made("act_step"))
    act.wait_ge(*R.own("act_step"))
    fn(ab, ab, ACT.Ln, bias=1.0).then_inc(*R.made("dt_log"))
    act.wait_ge(*R.next("toend_in"))
    fn(b.dt[:, 6, 0, :], b.dt[:, 6, 0, :], ACT.Exp).then_inc(*R.made("toend_exp"))
    for n in range(16):
        act.wait_ge(*R.next("gap_ready"))
        fn(b.gap[n % 2][:], b.gap[n % 2][:], ACT.Exp).then_inc(*R.made("decay_ready"))
        if n >= 8:
            fn(b.part[n % 2][:], bank[5 + n % 2][:], ACT.Exp).then_inc(*R.made("spread_exp"))

    def gates(k):
        for c in range(2):
            chunk()
            room()
            fn(b.sg[c][:, 0:S], bank_of(c)[:, 0:S], ACT.Sigmoid).then_inc(*R.made("gate_ready"))

    stage(8, gates)
    for gr in range(SSM_G):
        squares(lambda c: b.y[:, 4 * gr + c, :], S, 4)
        rstd(S, DI // SSM_G)
        for c in range(4):
            part(b.big[0][:, 4 * gr + c, :], width=S)
    stage(8)

    def branch_gates(k):
        gates(k)
        if k >= 4:
            for c in range(2):
                part(b.big[0][:, 2 * (k - 4) + c, :], width=S)

    stage(8, branch_gates)
    stage(4)
    norm(S)
    for c in range(KC):
        part(b.xn1[0][:, c, :], width=S)
    for n in (8, 8, 6):
        def ffn(k):
            chunk()
            room()
            fn(b.sg[0][:, 0:S], bank_of(0)[:, 0:S], ACT.Sigmoid).then_inc(*R.made("gate_ready"))
            R.n["evac"] += 1
            part(b.big[0][:, k, :], width=S, by_chunk=R.value("evac"))
        stage(n, ffn)
        stage(4)
    norm(S)

    def operand_parts(t, dst=None):
        for c in range(KC):
            part(b.xn[0][:, c, 0:t], width=t)

    def wide_gates(t):
        def body(k):
            for c in range(2):
                chunk()
                room()
                fn(b.sg[c][:, 0:t], bank_of(c)[:, 0:t], ACT.Sigmoid).then_inc(*R.made("gate_ready"))
        return body

    def gla(i, t):
        stage(9)
        z, ab, eb, enb = b.part
        for h in range(GH):
            for d in range(2):
                act.wait_ge(*R.next("zabs_ready"))
                fn(ab[:], ab[:], ACT.Exp, scale=-1.0).then_inc(*R.made("act_step"))
                act.wait_ge(*R.own("act_step"))
                fn(ab[:], ab[:], ACT.Ln, bias=1.0).then_inc(*R.made("zlog_ready"))
                act.wait_ge(*R.next("cum_ready"))
                fn(eb[:], b.rstd[:], ACT.Exp, scale=1.0 / 16).then_inc(*R.made("expb_ready"))
                fn(enb[:], b.rstd[:], ACT.Exp, scale=-1.0 / 16).then_inc(*R.made("expb_ready"))
                act.wait_ge(*R.next("gaps_ready"))
                fn(z[:], z[:], ACT.Exp, scale=1.0 / 16).then_inc(*R.made("kd_exp"))
        act.wait_ge(*R.next("norm_input"))
        for tt in range(t // P):
            for h in range(GH):
                last = fn(b.part[0][:, 0:DV], b.go[:, tt, h * DV:(h + 1) * DV], ACT.Square,
                          accum_out=b.small[:, 4 * tt + h:4 * tt + h + 1])
                last.then_inc(*R.made("act_step"))
                act.wait_ge(*R.own("act_step"))
        n = 4 * (t // P)
        fn(b.small[:, 16:16 + n], b.small[:, 0:n], ACT.Ln, bias=b.small[:, 63:64], scale=1.0 / DV) \
            .then_inc(*R.made("act_step"))
        act.wait_ge(*R.own("act_step"))
        fn(b.small[:, 32:32 + n], b.small[:, 16:16 + n], ACT.Exp, scale=-0.5).then_inc(*R.made("osq_ready"))
        stage(4, wide_gates(t))
        for c in range(KC):
            part(b.xn[0][:, c, 0:t], src=b.gqk[:, c, 0:t], by_chunk=R.value("evac") - KC + 1 + c)
        stage(4)

    def conv():
        def glu(k):
            chunk()
            chunk()
            room()
            bg = VEC["pw1_b"][0] + KC + k
            fn(b.sg[0][:], bank_of(1)[:], ACT.Sigmoid, bias=b.vec[:, bg:bg + 1]).then_inc(*R.made("gate_ready"))
        stage(8, glu)
        act.wait_ge(*R.next("mean_ready"))
        fn(b.nmean[:], bank[5][:], ACT.Copy, scale=1.0 / D).then_inc(*R.made("mean_taken"))
        squares(lambda c: b.dw[:, c, :], T2)
        rstd(T2, D)
        for c in range(KC):
            act.wait_ge(*R.next("ln_ready"))
            fn(b.sg[c % 2][:], b.dw[:, c, :], ACT.Sigmoid).then_inc(*R.made("gate_ready"))
            part(b.xn[0][:, c, :], width=T2)
        stage(4)

    def attention():
        stage(7)
        act.wait_ge(*R.next("norm_input"))
        for c in range(12):
            fn(b.part[c % 2][:], b.aqk[:, c, :], ACT.Square).then_inc(*R.made("square_ready"))
            act.wait_ge(*R.next("square_summed"))
            if c >= 2:
                act.wait_ge(*R.next("qn_ready"))
            fn(b.sg[c % 2][:], bank[4 + c % 2][:], ACT.Ln, bias=b.small[:, 63:64], scale=1.0 / HD) \
                .then_inc(*R.made("qstat_read"))
            act.wait_ge(*R.own("qstat_read"))
            fn(b.sg[c % 2][:], b.sg[c % 2][:], ACT.Exp, scale=-0.5).then_inc(*R.made("rstd_ready"))

        steps = [(h, qt) for h in range(QH) for qt in range(4)]
        for n, (h, qt) in enumerate(steps):
            nk = T2 if qt < 2 else S
            act.wait_ge(*R.next("neg_max"))
            fn(b.prob[n % 2][:, 0:nk], bank[4 + n % 2][:, 0:nk], ACT.Exp, bias=b.small[:, 20 + n % 2:21 + n % 2],
               scale=HD ** -0.5, accum_out=b.small[:, 24 + n % 2:25 + n % 2]).then_inc(*R.made("exp_ready"))
            act.wait_ge(*R.next("recip_ready"))
            fn(b.prob[n % 2][:, 0:nk], b.prob[n % 2][:, 0:nk], ACT.Copy,
               scale=b.small[:, 28 + n % 2:29 + n % 2]).then_inc(*R.made("probs_ready"))
            if n % 8 == 7:
                part(b.xn[0][:, n // 8, :], width=T2)
        stage(4)

    for i in range(LAYERS):
        t = S if i == LAYERS - 1 else T2
        norm(T2)
        operand_parts(T2)
        if i % 3 == 0:
            gla(i, t)
        elif i % 3 == 1:
            conv()
        else:
            attention()
        norm(t)
        operand_parts(t)

        def piece(mod, last=False):
            def hidden(k):
                for c in range(2):
                    chunk()
                    room()
                    fn(b.sg[c][:, 0:t], bank_of(c)[:, 0:t], ACT.Relu).then_inc(*R.made("gate_ready"))
                for c in range(2):
                    n = R.value("evac") + (c - 1)
                    part(b.hid[0][:, 2 * k + c, 0:t], width=t, by_chunk=n)
            stage(4, hidden, mod=mod)
            stage(4, mod=mod, last=last)

        per = {"w chunk_taken": 0, "hl_free": 32 if i < LAYERS - 1 else 16, "evac": 32 if i < LAYERS - 1 else 16,
               "m hi_ready": 16 if i < LAYERS - 1 else 8, "m gate_ready": 8, "m part_hi": 8}
        for j in range(RAW):
            per[f"w raw_loaded{j}"] = 16 * (4 if i < LAYERS - 1 else 2)
        with R.loop(3, per):
            piece(i < LAYERS - 1)
        piece(False, last=(i == LAYERS - 1))


def halves_and_mixes(nc, b, R, pool):
    tt = nc.gpsimd.tensor_tensor
    g = {"part": 0}

    def part(hi, lo, src=None, width=None):
        pool.wait_ge(*R.next("part_hi"))
        src = b.part[g["part"] % 4][:, 0:width] if src is None else src
        tt(lo, src, hi, ALU.subtract).then_inc(*R.made("part_lo"))
        g["part"] += 1

    def parts(n, pair, t):
        for c in range(n):
            part(pair[0][:, c, 0:t], pair[1][:, c, 0:t], width=t)

    part(b.chi[:], b.clo[:], width=16)
    parts(KC, b.xn1, S)
    parts(4, b.ao, S)
    for n in range(16):
        ct, gr = n // 8, n % 8 // 2
        pool.wait_ge(*R.next("decay_ready"))
        last = tt(b.gap[n % 2][:], b.gap[n % 2][:], b.cbm[:, gr:gr + 1, :].to_broadcast([P, 4, P]), ALU.mult)
        if ct:
            pool.wait_ge(*R.next("spread_exp"))
            last = tt(b.part[2 + n % 2][:].rearrange("p (h t) -> p h t", h=4),
                      b.part[n % 2][:].rearrange("p (h t) -> p h t", h=4),
                      b.xbc[:, 20 + gr:21 + gr, P:2 * P].to_broadcast([P, 4, P]), ALU.mult)
        last.then_inc(*R.made("mix_ready"))
    parts(DI // P, b.big, S)
    parts(KC, b.big, S)
    parts(KC, b.xn1, S)
    for n in (8, 8, 6):
        parts(n, b.big, S)
    for i in range(LAYERS):
        t = S if i == LAYERS - 1 else T2
        parts(KC, b.xn, T2)
        if i % 3 == 0:
            for c in range(KC):
                part(b.xn[0][:, c, 0:t], b.xn[1][:, c, 0:t], src=b.gqk[:, c, 0:t])
        else:
            parts(KC, b.xn, T2)
        parts(KC, b.xn, t)
        with R.loop(4, {"w part_hi": KC, "m part_lo": KC}):
            parts(KC, b.hid, t)


def vectors(nc, b, R, dve, at):
    ttn, sct, stt, cp = nc.vector.tensor_tensor, nc.vector.tensor_scalar, nc.vector.scalar_tensor_tensor, \
        nc.vector.tensor_copy
    g = {"unit": 0, "taken": 0, "part": 0}
    bank = b.bank

    def vec(name, c=0, w=1):
        o = VEC[name][0]
        if isinstance(c, int):
            return b.vec[:, o + c:o + c + w]
        return b.vec[:, bass.ds(c + o, w)]

    def cst(name):
        return b.cst[:, CST[name][0]:CST[name][0] + CST[name][1]]

    def at_chunk(buf, c):
        if isinstance(c, int):
            return buf[:, c, :]
        return buf[:, bass.ds(c, 1), :].rearrange("p a t -> p (a t)")

    def step(ins):
        ins.then_inc(*R.made("dve_step"))
        dve.wait_ge(*R.own("dve_step"))

    def split():
        u = g["unit"]
        dve.wait_ge(*R.next("hi_ready"))
        ttn(b.wlo[u % SPL][:], b.raw[u % RAW][:], b.whi[u % SPL][:], ALU.subtract).then_inc(*R.made("lo_ready"))
        g["unit"] += 1

    def part(width):
        if g["part"] >= 4:
            dve.wait_ge(*R.next("part_lo"))
        g["part"] += 1
        return b.part[(g["part"] - 1) % 4][:, 0:width]

    def in_place():
        R.n["w part_lo"] += 1
        g["part"] += 1

    def chunk():
        dve.wait_ge(*R.next("chunk_ready"))

    def bank_of(c):
        return bank[2 * (g["taken"] % SPL) + c]

    def stage(n, body, mod=None, last=False):
        def one(k, j, k2):
            if not (last and isinstance(k, int) and k == n - 1):
                split()
            if mod is not None and j % 2:
                for c in range(2):
                    chunk()
                    col = (k2 * 2 + (mod[1] + c)) * 2
                    dst = b.mod[mod[0] % 2]
                    dst = dst[:, col:col + 2] if isinstance(col, int) else dst[:, bass.ds(col, 2)]
                    cp(dst, bank_of(c)[:, 0:2]).then_inc(*R.made("chunk_taken"))
            else:
                body(k2 if mod is not None else k)
            g["taken"] += 1
        R.groups(2 * n if mod is not None else n, one)

    def take_to(buf, t, off=0, reverse=False, scale=None):
        def body(k):
            for c in range(2):
                chunk()
                dst, src = at_chunk(buf, k * 2 + (off + c)), bank_of(c)[:, 0:t]
                if reverse:
                    dst = dst.rearrange("p (a t) -> p a t", t=P)
                    src = src.rearrange("p (a t) -> p a t", t=P)[:, :, ::-1]
                if scale is None:
                    cp(dst, src).then_inc(*R.made("chunk_taken"))
                else:
                    sct(dst, src, scale, None, ALU.mult).then_inc(*R.made("chunk_taken"))
        return body

    def x_ready():
        cp(b.small[:, 62:63], b.small[:, 63:64]).then_inc(*R.made("norm_input"))

    def settle():
        step(cp(b.small[:, 61:62], b.small[:, 63:64]))

    def norm1(name, dst=None):
        x_ready()
        dve.wait_ge(*R.next("rstd_ready"))
        for c in range(KC):
            if dst is None:
                stt(part(S), b.x[:, c, 0:S], vec(name, c), b.rstd[:, 0:S], ALU.mult, ALU.mult) \
                    .then_inc(*R.made("part_ready"))
            else:
                stt(dst[:, c, 0:S], b.x[:, c, 0:S], vec(name, c), b.rstd[:, 0:S], ALU.mult, ALU.mult) \
                    .then_inc(*R.made("dve_step"))

    step(nc.vector.memset(b.small[:], EPS))
    dve.wait_ge(R.sems["params_loaded"], 64)
    dve.wait_ge(*R.next("gate_ready"))
    ttn(part(16), vec("c", 0, 16), b.small[:, 0:16], ALU.mult).then_inc(*R.made("part_ready"))
    split()
    dve.wait_ge(*R.next("rel_rows"))
    for gr in range(NG):
        last = ttn(b.reltab[:, gr, :], bank[5 + gr][0:GROUP_HEADS, 0:384],
                   b.rel[0:GROUP_HEADS, 384 * (gr + 1):384 * (gr + 2)], ALU.add)
    last.then_inc(*R.made("rel_table"))
    dve.wait_ge(R.sems["x_loaded"], 16)
    norm1("norm1")
    stage(6, take_to(b.qk, S, reverse=True), mod=(0, 0))
    stage(6, take_to(b.qk, S, off=12), mod=(0, 12))

    def take_v(k):
        for c in range(2):
            chunk()
            dst = b.v[:, c, k * UC:(k + 1) * UC] if isinstance(k, int) else b.v[:, c, bass.ds(k * UC, UC)]
            cp(dst, bank_of(c)[:, 0:UC]).then_inc(*R.made("chunk_taken"))
    stage(6, take_v)

    def front(n):
        h, qt = n // 2, n % 2
        nk = P * (qt + 1)
        L = b.logits[n % 2]
        dve.wait_ge(*R.next("scores_ready"))
        if qt == 0:
            dve.wait_ge(*R.next(f"rel_loaded{h % 2}", 16))
        o = P - P * qt
        two = bank[4 + 2 * (n % 2)][:].rearrange("p (g k) -> p g k", g=2)
        stt(L[:, 0:2, 0:nk], two[:, :, 0:nk], HD ** -0.5, b.bias[h % 2][:, 0:2, o:o + nk], ALU.mult, ALU.add) \
            .then_inc(*R.made("dve_step"))
        stt(L[:, 2, 0:nk], bank[5 + 2 * (n % 2)][:, 0:nk], HD ** -0.5, b.bias[h % 2][:, 2, o:o + nk],
            ALU.mult, ALU.add).then_inc(*R.made("logits_taken"))
        dve.wait_ge(*R.own("logits_taken"))
        step(nc.vector.tensor_reduce(b.small[:, 16 + n % 2:17 + n % 2], L[:, :, 0:nk], AX.XY, ALU.max))
        sct(b.small[:, 20 + n % 2:21 + n % 2], b.small[:, 16 + n % 2:17 + n % 2], -1.0, None, ALU.mult) \
            .then_inc(*R.made("neg_max"))

    front(0)
    for n in range(16):
        if n < 15:
            front(n + 1)
        kt = n % 2 + 1
        dve.wait_ge(*R.next("exp_ready"))
        nc.vector.reciprocal(b.small[:, 28 + n % 2:29 + n % 2], b.small[:, 24 + n % 2:25 + n % 2]) \
            .then_inc(*R.made("recip_ready"))
        dve.wait_ge(*R.next("turned_ready"))
        n0 = min(4, NG * kt)
        last = cp(b.turned[:, 0:n0, :], bank[0][:, 0:n0 * P].rearrange("p (a t) -> p a t", t=P))
        if kt == 2:
            last = cp(b.turned[:, 4:6, :], bank[1][:, 0:2 * P].rearrange("p (a t) -> p a t", t=P))
        last.then_inc(*R.made("turned_taken"))
        if n % 4 == 3:
            dve.wait_ge(*R.next("values_ready", 4))
            cp(part(S).rearrange("p (a t) -> p a t", t=P),
               bank[2 + (n // 4) % 2][:, 0:S].rearrange("p (a t) -> p a t", t=P)[:, :, ::-1]) \
                .then_inc(*R.made("part_ready"))
    stage(4, take_to(b.attn_out, S))

    for c in range(2):
        step(nc.vector.memset(b.cin[c][:, 0:3], 0.0))

    def conv4(k):
        for c in range(2):
            dve.wait_ge(*R.next("cin_ready"))
            R.n["w chunk_ready"] += 1
            ch = k * 2 + c
            sct(b.cacc[c][:], b.cin[c][:, 0:S], vec("conv_w", ch * 4), vec("conv_b", ch), ALU.mult, ALU.add) \
                .then_inc(*R.made("chunk_taken"))
            dve.wait_ge(*R.own("chunk_taken"))
            for tap in (1, 2, 3):
                ins = stt(b.cacc[c][:], b.cin[c][:, tap:tap + S], vec("conv_w", ch * 4 + tap), b.cacc[c][:],
                          ALU.mult, ALU.add)
                if tap < 3:
                    step(ins)
                else:
                    ins.then_inc(*R.made("conv_ready"))
        for c in range(2):
            dve.wait_ge(*R.next("gate_ready"))
            ttn(at_chunk(b.xbc, k * 2 + c), b.cacc[c][:], b.sg[c][:, 0:S], ALU.mult).then_inc(*R.made("dve_step"))
    stage(12, conv4, mod=(0, 24))

    def take_dt(k):
        for c in range(2):
            chunk()
            ttn(b.dt[:, 0, c, :], bank_of(c)[:, 0:SSM_HEADS], vec("dt_b", 0, SSM_HEADS), ALU.add) \
                .then_inc(*R.made("chunk_taken"))
    stage(1, take_dt)
    dve.wait_ge(*R.own("chunk_taken"))
    lin, ab = b.dt[:, 0, :, :], b.dt[:, 1, :, :]
    stt(ab, lin, -1.0, lin, ALU.mult, ALU.max).then_inc(*R.made("dt_abs"))
    dve.wait_ge(*R.next("dt_log"))
    step(stt(b.dt[:, 3, :, :], lin, 0.0, ab, ALU.max, ALU.add))
    for ct in range(2):
        last = stt(b.dt[:, 2, ct, :], b.dt[:, 3, ct, :], -1.0, b.dt[:, 7, 0, :], ALU.mult, ALU.mult)
    last.then_inc(*R.made("dta_ready"))
    for ct in range(2):
        for gr in range(SSM_G):
            dve.wait_ge(*R.next("xs_turned"))
            ttn(b.xdt[:, ct, gr * 512:(gr + 1) * 512].rearrange("p (h d) -> p h d", d=HD),
                bank[4 + gr % 2][:].rearrange("p (h d) -> p h d", d=HD),
                b.dt[:, 3, ct, gr * 8:gr * 8 + 8].unsqueeze(2).to_broadcast([P, 8, HD]), ALU.mult) \
                .then_inc(*R.made("xs_taken"))
    dve.wait_ge(*R.next("sums_ready"))
    for s in range(2):
        last = cp(b.dt[:, 4 + s, :, :], bank[6][:, 0:128].rearrange("p (c s h) -> p s c h", c=2, s=2)[:, s, :, :])
        step(last)
    ttn(b.dt[:, 6, 0, :], b.dt[:, 5, 0, :], b.dt[:, 4, 0, :], ALU.subtract).then_inc(*R.made("toend_in"))
    dve.wait_ge(*R.next("b_turned"))
    cp(b.bt[:].rearrange("p g t -> p (g t)"), bank[7][:]).then_inc(*R.made("b_taken"))
    dve.wait_ge(*R.next("toend_exp"))
    dve.wait_ge(*R.own("xs_taken"))
    for gr in range(SSM_G):
        ttn(b.toend_x[:].rearrange("p (h d) -> p h d", d=HD),
            b.xdt[:, 0, gr * 512:(gr + 1) * 512].rearrange("p (h d) -> p h d", d=HD),
            b.dt[:, 6, 0, gr * 8:gr * 8 + 8].unsqueeze(2).to_broadcast([P, 8, HD]), ALU.mult) \
            .then_inc(*R.made("toend_ready"))
        dve.wait_ge(*R.next("state_ready"))
        cp(b.state1[:, gr, :], bank[4 + gr % 2][:]).then_inc(*R.made("state_taken"))

    def cb():
        dve.wait_ge(*R.next("cb_ready"))
        ttn(b.cbm[:], bank[4][:].rearrange("p (g t) -> p g t", g=4),
            cst("tri").unsqueeze(1).to_broadcast([P, 4, P]), ALU.mult).then_inc(*R.made("cb_taken"))

    def gap(n):
        ct, quad = n // 8, n % 8
        dve.wait_ge(*R.next("spread_ready"))
        for h in range(4):
            head = quad * 4 + h
            last = sct(b.gap[n % 2][:, h, :], bank[5 + n % 2][:, h * P:(h + 1) * P], b.dt[:, 4, ct, head:head + 1],
                       0.0, ALU.subtract, ALU.min)
        last.then_inc(*R.made("gap_ready"))

    cb()
    gap(0)
    for n in range(16):
        if n < 15 and n != 7:
            gap(n + 1)
        ct, quad = n // 8, n % 8
        dve.wait_ge(*R.next("y_ready"))
        for c in range(2):
            ch = quad * 2 + c
            last = stt(b.y[:, ch, ct * P:(ct + 1) * P], b.xbc[:, ch, ct * P:(ct + 1) * P], vec("dskip", ch),
                       bank[n % 2][:, c * P:(c + 1) * P], ALU.mult, ALU.add)
        last.then_inc(*R.made("y_taken"))
        if n == 7:
            cb()
            gap(8)

    dve.wait_ge(*R.own("y_taken"))

    def take_z(k):
        for c in range(2):
            chunk()
            dve.wait_ge(*R.next("gate_ready"))
            y = at_chunk(b.y, k * 2 + c)
            step(ttn(y, y, b.sg[c][:, 0:S], ALU.mult))
            ttn(y, bank_of(c)[:, 0:S], y, ALU.mult).then_inc(*R.made("chunk_taken"))
    stage(8, take_z)
    for gr in range(SSM_G):
        x_ready()
        dve.wait_ge(*R.next("rstd_ready"))
        for c in range(4):
            ch = 4 * gr + c
            stt(part(S), b.y[:, ch, :], vec("ssm_norm", ch), b.rstd[:, 0:S], ALU.mult, ALU.mult) \
                .then_inc(*R.made("part_ready"))

    def take_ssm(k):
        for c in range(2):
            chunk()
            o = b.ssm_out[:, 2 * (k % 4) + c, :]
            if k < 4:
                cp(o, bank_of(c)[:, 0:S]).then_inc(*R.made("chunk_taken"))
            else:
                ttn(o, bank_of(c)[:, 0:S], o, ALU.add).then_inc(*R.made("chunk_taken"))
    stage(8, take_ssm)
    dve.wait_ge(*R.own("chunk_taken"))

    def take_gates(k):
        for c in range(2):
            R.n["w chunk_ready"] += 1
            dve.wait_ge(*R.next("gate_ready"))
            ch = 2 * (k % 4) + c
            o = b.attn_out[:, ch, :] if k < 4 else b.ssm_out[:, ch, :]
            ttn(o, o, b.sg[c][:, 0:S], ALU.mult).then_inc(*R.made("chunk_taken"))
            if k >= 4:
                dve.wait_ge(*R.own("chunk_taken"))
                ttn(part(S), o, b.attn_out[:, ch, :], ALU.add).then_inc(*R.made("part_ready"))
    stage(8, take_gates)

    def add_to_x(k):
        for c in range(2):
            chunk()
            o = b.x[:, 2 * k + c, 0:S]
            ttn(o, bank_of(c)[:, 0:S], o, ALU.add).then_inc(*R.made("chunk_taken"))
    stage(4, add_to_x)
    norm1("norm2")
    for n in (8, 8, 6):
        def ffn(k):
            chunk()
            dve.wait_ge(*R.next("gate_ready"))
            ttn(b.sg[1][:, 0:S], bank_of(0)[:, 0:S], b.sg[0][:, 0:S], ALU.mult).then_inc(*R.made("chunk_taken"))
            dve.wait_ge(*R.own("chunk_taken"))
            p = part(S)
            chunk()
            ttn(p, bank_of(1)[:, 0:S], b.sg[1][:, 0:S], ALU.mult).then_inc(*R.made("chunk_taken"))
        stage(n, ffn)
        stage(4, add_to_x)
    norm1("final", b.x)
    settle()

    def streams(t):
        return [(s, s * S) for s in range(t // S)]

    def mcol(i, v, c, s):
        o = 2 * (v * KC + c) + s
        return b.mod[i % 2][:, o:o + 1]

    def norm_mod(i, which, t):
        x_ready()
        if which == 0:
            m = b.mod[i % 2][:].rearrange("p (m s) -> p m s", s=2)
            step(ttn(m, m, vec("b_mod", i * MODC, MODC).unsqueeze(2).to_broadcast([P, MODC, 2]), ALU.add))
            for n, name in enumerate(("g_mix", "g_mlp")):
                sc = m[:, (1 + 3 * n) * KC:(2 + 3 * n) * KC, :]
                step(stt(b.modg[:].rearrange("p (n c s) -> p n c s", n=2, s=2)[:, n, :, :], sc, 1.0,
                         vec(name, i * KC, KC).unsqueeze(2).to_broadcast([P, KC, 2]), ALU.add, ALU.mult))
        dve.wait_ge(*R.next("rstd_ready"))
        for c in range(KC):
            p = part(t)
            step(ttn(p, b.x[:, c, 0:t], b.rstd[:, 0:t], ALU.mult))
            for s, o in streams(t):
                gcol = 2 * (which * KC + c) + s
                last = sct(p[:, o:o + S], p[:, o:o + S], b.modg[:, gcol:gcol + 1],
                           mcol(i, 3 * which, c, s), ALU.mult, ALU.add)
            last.then_inc(*R.made("part_ready"))

    def add_gated(i, v, t):
        def body(k):
            for c in range(2):
                chunk()
                for s, o in streams(t):
                    ch = 2 * k + c
                    last = stt(b.x[:, ch, o:o + S], bank_of(c)[:, o:o + S], mcol(i, v, ch, s),
                               b.x[:, ch, o:o + S], ALU.mult, ALU.add)
                last.then_inc(*R.made("chunk_taken"))
        return body

    def gla(i, t):
        last_layer = i == LAYERS - 1
        gi = i // 3

        def qk(k):
            for c in range(2):
                chunk()
                ch = 2 * k + c
                scale = (D // 2 // GH) ** -0.5 if k < 2 else 1.0
                sct(b.gqk[:, ch, :], bank_of(c)[:], scale, None, ALU.mult).then_inc(*R.made("chunk_taken"))
        stage(4, qk)

        def vtake(k):
            for c in range(2):
                chunk()
                cp(b.gv[:, 2 * c:2 * c + 2, k * UC:(k + 1) * UC], bank_of(c)[:].rearrange("p (a n) -> p a n", a=2)) \
                    .then_inc(*R.made("chunk_taken"))
        stage(4, vtake)

        def g1take(k):
            for c in range(2):
                chunk()
                cp(b.g1[32 * c:32 * c + 16, :], bank_of(c)[32 * c:32 * c + 16, :]).then_inc(*R.made("chunk_taken"))
        stage(1, g1take)
        dve.wait_ge(*R.own("chunk_taken"))
        z, ab, eb, enb = b.part
        cum = b.rstd
        for h in range(GH):
            q, k = b.gqk[:, h, :], b.gqk[:, GH + h, :]
            for d in range(2):
                dve.wait_ge(*R.next("zg_ready"))
                step(sct(z[:], bank[4][:], vec("gla_b", (gi * 2 + d) * GH + h), None, ALU.add))
                stt(ab[:], z[:], -1.0, z[:], ALU.mult, ALU.max).then_inc(*R.made("zabs_ready"))
                dve.wait_ge(*R.next("zlog_ready"))
                step(stt(z[:], z[:], 0.0, ab[:], ALU.min, ALU.subtract))
                if d == 0:
                    nc.vector.tensor_tensor_scan(cum[:], cst("restart"), z[:], 0.0, ALU.mult, ALU.add) \
                        .then_inc(*R.made("cum_ready"))
                else:
                    nc.vector.tensor_tensor_scan(cum[:, ::-1], cst("restart"), z[:, ::-1], 0.0, ALU.mult, ALU.add) \
                        .then_inc(*R.made("cum_ready"))
                dve.wait_ge(*R.own("cum_ready"))
                end = GCH - 1 if d == 0 else 0
                c3 = cum[:].rearrange("p (n t) -> p n t", t=GCH)
                ttn(z[:].rearrange("p (n t) -> p n t", t=GCH), c3[:, :, end:end + 1].to_broadcast([P, 8, GCH]), c3,
                    ALU.subtract).then_inc(*R.made("gaps_ready"))
                dve.wait_ge(*R.next("expb_ready"))
                ttn(b.qb[d][:], q, eb[:], ALU.mult).then_inc(*R.made("dve_step"))
                cp(b.ends[d][:].unsqueeze(2), eb[:].rearrange("p (n t) -> p n t", t=GCH)[:, :, end:end + 1]) \
                    .then_inc(*R.made("dve_step"))
                dve.wait_ge(*R.next("expb_ready"))
                ttn(b.kb[d][:], k, enb[:], ALU.mult).then_inc(*R.made("dve_step"))
                dve.wait_ge(*R.next("kd_exp"))
                ttn(ab[:], k, z[:], ALU.mult).then_inc(*R.made("kd_ready"))
                dve.wait_ge(*R.next("kdt_ready"))
                cp(b.kdt[d][:].rearrange("p a t -> p (a t)"), bank[5][:]).then_inc(*R.made("dve_step"))
                dve.wait_ge(*R.next("att_ready"))
                ttn(b.att[d][:], bank[6][:, 0:4 * GCH].rearrange("p (a t) -> p a t", t=GCH),
                    cst("causal" if d == 0 else "anticausal").unsqueeze(1).to_broadcast([P, 4, GCH]), ALU.mult) \
                    .then_inc(*R.made("att_taken"))
            order = [[4, 5, 6, 7, 0, 1, 2, 3], [7, 6, 5, 4, 3, 2, 1, 0]]

            def take_o(s):
                for d in range(2):
                    dve.wait_ge(*R.next("o_ready"))
                    st = 0 if s == 7 else 2
                    dst = b.go[:, st:st + 2, h * DV:(h + 1) * DV]
                    src = bank[2 + d][:].rearrange("p (a n) -> p a n", a=2)
                    if d == 0:
                        cp(dst, src).then_inc(*R.made("o_taken"))
                    else:
                        dve.wait_ge(*R.own("o_taken"))
                        ttn(dst, src, dst, ALU.add).then_inc(*R.made("o_taken"))

            for s in range(7):
                for d in range(2):
                    n = order[d][s]
                    dve.wait_ge(*R.next("s_ready"))
                    new, old = b.gs2[d][(s + 1) % 2], b.gs2[d][s % 2]
                    if s == 0:
                        cp(new[:], bank[d][:, 0:DV]).then_inc(*R.made("s_taken"))
                    else:
                        dve.wait_ge(R.sems["s_taken"], R.n["m s_taken"] - 1)
                        stt(new[:], old[:], b.ends[d][:, n:n + 1], bank[d][:, 0:DV], ALU.mult, ALU.add) \
                            .then_inc(*R.made("s_taken"))
                if s == 3 and not last_layer:
                    take_o(3)
            take_o(7)
        x_ready()
        dve.wait_ge(*R.next("osq_ready"))
        gh = VEC["g_head"][0] + gi * DV
        for tt in range(t // P):
            for h in range(GH):
                o = b.go[:, tt, h * DV:(h + 1) * DV]
                col = 32 + 4 * tt + h
                last = stt(o, o, b.small[:, col:col + 1], b.vec[:, gh:gh + DV], ALU.mult, ALU.mult)
        last.then_inc(*R.made("onorm_ready"))
        for fc in range(KC):
            dve.wait_ge(*R.next("ot_ready"))
            cp(b.gqk[:, fc, 0:t], bank[5 + fc % 2][:, 0:t]).then_inc(*R.made("ot_taken"))
        dve.wait_ge(*R.own("ot_taken"))

        def take_r(k):
            for c in range(2):
                chunk()
                dve.wait_ge(*R.next("gate_ready"))
                in_place()
                o = b.gqk[:, 2 * k + c, 0:t]
                step(ttn(o, o, b.sg[c][:, 0:t], ALU.mult))
                ttn(o, bank_of(c)[:, 0:t], o, ALU.mult).then_inc(*R.made("chunk_taken"))
        stage(4, take_r)
        stage(4, add_gated(i, 2, t))

    def conv(i):
        for c in range(KC):
            for o in (0, PADT + S):
                nc.vector.memset(b.u[:, c, :, o:o + PADT], 0.0).then_inc(*R.made("dve_step"))
        dve.wait_ge(*R.own("dve_step"))

        def glu(k):
            chunk()
            dve.wait_ge(*R.next("gate_ready"))
            u = b.u[:, k, :, PADT:PADT + S]
            stt(u, bank_of(0)[:].rearrange("p (s t) -> p s t", s=2), vec("pw1_b", k),
                b.sg[0][:].rearrange("p (s t) -> p s t", s=2), ALU.add, ALU.mult).then_inc(*R.made("chunk_taken"))
            chunk()
            dve.wait_ge(*R.own("chunk_taken"))
            acc = b.dw[:, k, :].rearrange("p (s t) -> p s t", s=2)
            w = lambda tap: vec("dw_w", k * TAPS + tap)
            sct(acc, b.u[:, k, :, 0:S], w(0), vec("dw_b", k), ALU.mult, ALU.add).then_inc(*R.made("chunk_taken"))
            dve.wait_ge(*R.own("chunk_taken"))
            for tap in range(1, TAPS):
                ins = stt(acc, b.u[:, k, :, tap:tap + S], w(tap), acc, ALU.mult, ALU.add)
                if tap < TAPS - 1:
                    step(ins)
                else:
                    ins.then_inc(*R.made("dw_ready"))
        stage(8, glu)
        dve.wait_ge(*R.next("mean_taken"))
        for c in range(KC):
            ttn(b.dw[:, c, :], b.dw[:, c, :], b.nmean[:], ALU.subtract).then_inc(*R.made("dve_step"))
        x_ready()
        dve.wait_ge(*R.next("rstd_ready"))
        for c in range(KC):
            step(ttn(b.dw[:, c, :], b.dw[:, c, :], b.rstd[:], ALU.mult))
            sct(b.dw[:, c, :], b.dw[:, c, :], vec("ln_g", c), vec("ln_b", c), ALU.mult, ALU.add) \
                .then_inc(*R.made("ln_ready"))
            if c:
                silu(c - 1)
        silu(KC - 1)

        def take(k):
            for c in range(2):
                chunk()
                ch = 2 * k + c
                step(sct(b.sg[c][:], bank_of(c)[:], vec("pw2_b", ch), None, ALU.add))
                for s, o in streams(T2):
                    last = stt(b.x[:, ch, o:o + S], b.sg[c][:, o:o + S], mcol(i, 2, ch, s),
                               b.x[:, ch, o:o + S], ALU.mult, ALU.add)
                last.then_inc(*R.made("chunk_taken"))
        stage(4, take)

    def silu(c):
        dve.wait_ge(*R.next("gate_ready"))
        ttn(part(T2), b.dw[:, c, :], b.sg[c % 2][:], ALU.mult).then_inc(*R.made("part_ready"))

    def attention(i):
        stage(6, take_to(b.aqk, T2))

        def vtake(k):
            for c in range(2):
                chunk()
                cp(b.av[:, 2 * c:2 * c + 2, :], bank_of(c)[:].rearrange("p (a n) -> p a n", a=2)) \
                    .then_inc(*R.made("chunk_taken"))
        stage(1, vtake)
        x_ready()
        dve.wait_ge(R.sems["rope_loaded"], 16)
        cos, sin = b.rope[:, P:P + S], b.rope[:, P + S:P + 2 * S]
        for c in range(12):
            dve.wait_ge(*R.next("rstd_ready"))
            stt(b.aqk[:, c, :], b.aqk[:, c, :], vec("g_q" if c < 8 else "g_k"), b.sg[c % 2][:], ALU.mult,
                ALU.mult).then_inc(*R.made("qn_ready"))
            dve.wait_ge(*R.next("rot_ready"))
            ttn(b.part[2][:, 0:S], bank[6 + c % 2][:, 0:S], sin, ALU.mult).then_inc(*R.made("dve_step"))
            step(ttn(b.part[2][:, S:T2], b.aqk[:, c, 0:S], cos, ALU.mult))
            ttn(b.aqk[:, c, 0:S], b.part[2][:, 0:S], b.part[2][:, S:T2], ALU.add).then_inc(*R.made("rot_taken"))

        steps = [(h, qt) for h in range(QH) for qt in range(4)]

        def front(n):
            nk = T2 if steps[n][1] < 2 else S
            dve.wait_ge(*R.next("scores_ready"))
            step(nc.vector.tensor_reduce(b.small[:, 16 + n % 2:17 + n % 2], bank[4 + n % 2][:, 0:nk], AX.X, ALU.max))
            sct(b.small[:, 20 + n % 2:21 + n % 2], b.small[:, 16 + n % 2:17 + n % 2], -(HD ** -0.5), None,
                ALU.mult).then_inc(*R.made("neg_max"))

        front(0)
        for n, (h, qt) in enumerate(steps):
            if n + 1 < len(steps):
                front(n + 1)
            nt = 4 if qt < 2 else 2
            dve.wait_ge(*R.next("exp_ready"))
            nc.vector.reciprocal(b.small[:, 28 + n % 2:29 + n % 2], b.small[:, 24 + n % 2:25 + n % 2]) \
                .then_inc(*R.made("recip_ready"))
            dve.wait_ge(*R.next("turned_ready"))
            cp(b.pt[:, 0:nt, :], bank[6][:, 0:nt * P].rearrange("p (a t) -> p a t", t=P)) \
                .then_inc(*R.made("turned_taken"))
            if n % 8 == 7:
                dve.wait_ge(*R.next("values_ready", 8))
                cp(part(T2), bank[2 + (n // 8) % 2][:]).then_inc(*R.made("part_ready"))
        stage(4, add_gated(i, 2, T2))

    for i in range(LAYERS):
        t = S if i == LAYERS - 1 else T2
        norm_mod(i, 0, T2)
        if i % 3 == 0:
            gla(i, t)
        elif i % 3 == 1:
            conv(i)
        else:
            attention(i)
        norm_mod(i, 1, t)
        mixed = i < LAYERS - 1

        def piece(mod0, last=False):
            def hidden(k):
                for c in range(2):
                    chunk()
                    dve.wait_ge(*R.next("gate_ready"))
                    stt(part(t), bank_of(c)[:, 0:t], 0.0, b.sg[c][:, 0:t], ALU.max, ALU.mult) \
                        .then_inc(*R.made("chunk_taken"))
            stage(4, hidden, mod=None if mod0 is None else (i + 1, mod0))
            stage(4, add_gated(i, 5, t), mod=None if mod0 is None else (i + 1, mod0 + 8), last=last)

        m = 2 if mixed else 1
        per = {"w hi_ready": 8 * m, "m lo_ready": 8 * m, "w chunk_ready": 16 * m, "m chunk_taken": 16 * m,
               "w gate_ready": 8, "w part_lo": 8}
        with R.loop(3, per) as p:
            piece(p * 16 if mixed else None)
        piece(None, last=not mixed)
    cp(b.small[:, 60:61], b.small[:, 63:64]).then_inc(*R.made("result_ready"))


def program(nc, x, vec, cst, rel, relb, wall, wg2, rope, out):
    plan = unit_plan()
    at = {"units": len(plan)}
    for n, (what, k) in enumerate(plan):
        if k == 0:
            at[what] = n
    reltab = nc.dram_tensor("relative_offsets", [GROUP_HEADS, NG, 384], F32, kind="Internal").ap()
    dram = {"x": x, "vec": vec, "cst": cst, "rel": rel, "relb": relb, "wall": wall, "wg2": wg2, "rope": rope,
            "out": out, "reltab": reltab, "at": at}
    with ExitStack() as ctx:
        b = place(nc, ctx)
        sems = {n: ctx.enter_context(nc.semaphore(n)) for n in SEMS}
        block = ctx.enter_context(nc.Block())

        @block.sync
        def _(sp):
            loads(nc, b, dram, Role(nc.sync, sems), sp)

        @block.tensor
        def _(pe):
            products(nc, b, Role(nc.tensor, sems), pe, at)

        @block.scalar
        def _(act):
            splits_and_functions(nc, b, Role(nc.scalar, sems), act, at)

        @block.gpsimd
        def _(pool):
            halves_and_mixes(nc, b, Role(nc.gpsimd, sems), pool)

        @block.vector
        def _(dve):
            vectors(nc, b, Role(nc.vector, sems), dve, at)


def lay_out(a):
    def feat(v):
        return np.ascontiguousarray(v.reshape(-1, P).T)

    def rows(v):
        return np.broadcast_to(v.reshape(1, -1), (P, v.size))

    def taps(w):
        t, n = w.shape
        return w.reshape(t, n // P, P).transpose(2, 1, 0).reshape(P, -1)

    cols = {
        "norm1": feat(a["norm1_w"]), "norm2": feat(a["norm2_w"]), "final": feat(a["final_norm_w"]),
        "conv_w": taps(a["conv_w"][0]), "conv_b": feat(a["conv_b"]),
        "dskip": feat(np.repeat(a["d_skip"][0], HD)), "ssm_norm": feat(a["ssm_norm_w"]),
        "b_mod": feat(a["b_mod_2"]), "g_mix": feat(a["g_norm_mix_2"]), "g_mlp": feat(a["g_norm_mlp_2"]),
        "gla_b": feat(a["gla_b_g_2"]), "pw1_b": feat(a["conv_b_pw1_2"]), "dw_w": taps(a["conv_w_dw_2"][0]),
        "dw_b": feat(a["conv_b_dw_2"]), "ln_g": feat(a["conv_ln_g_2"]), "ln_b": feat(a["conv_ln_b_2"]),
        "pw2_b": feat(a["conv_b_pw2_2"]), "g_q": np.tile(a["attn_g_q_2"][0], 2)[:, None],
        "g_k": np.tile(a["attn_g_k_2"][0], 2)[:, None],
        "c": np.stack([feat(a["c_2"]), feat(a["c_ctx_2"])], axis=2).reshape(P, -1),
        "dt_b": rows(a["dt_bias"]), "a_log": rows(a["a_log"]), "g_head": rows(a["gla_g_head_2"]),
    }
    vec = np.concatenate([cols[n] for n in VEC], axis=1)

    def unit(w):
        r, c = w.shape
        u = np.zeros((P, KC, UC), np.float32)
        u[:, :r // P, :c] = w.reshape(r // P, P, c).transpose(1, 0, 2)
        return u.reshape(P, UW)

    w_in = a["w_in"][0]
    o_k, o_v = AW, 2 * AW
    o_z = 3 * AW
    o_xbc = o_z + DI
    o_dt = o_xbc + XBC
    o_gate = o_dt + SSM_HEADS
    ffn_in, ffn_out = a["w_ffn_in"][0], a["w_ffn_out"][0]
    att = a["attn_w_qkv_2"][0]
    kv = D + 4 * HD

    def one(what, k):
        c = slice(k * UC, (k + 1) * UC)
        if isinstance(what, tuple):
            kind, i = what
            if kind == "mod":
                return a["w_mod_2"][i][:, c]
            if kind == "ffn_in":
                f = (8 * i + k) * P
                return np.concatenate([ffn_in[:, f:f + P], ffn_in[:, FF + f:FF + f + P]], axis=1)
            if kind == "ffn_out":
                return ffn_out[i * D:min((i + 1) * D, FF), c]
            if kind == "gla_qk":
                return a["gla_w_in_2"][i][:, c]
            if kind == "gla_v":
                return a["gla_w_in_2"][i][:, D:][:, c]
            if kind == "gla_r":
                return a["gla_w_in_2"][i][:, 2 * D:][:, c]
            if kind == "gla_g1":
                w = np.zeros((D, UC), np.float32)
                w[:, 0:16] = a["gla_w_g1_2"][i, 0]
                w[:, P + 32:P + 48] = a["gla_w_g1_2"][i, 1]
                return w
            if kind == "gla_out":
                return a["gla_w_out_2"][i][:, c]
            (kind, layer), p = kind, i
            if kind == "mlp_in":
                return a["w_mlp_in_2"][layer][:, p * D:(p + 1) * D][:, c]
            return a["w_mlp_out_2"][layer][p * D:(p + 1) * D][:, c]
        if what == "q":
            return w_in[:, c]
        if what == "k":
            return w_in[:, o_k:][:, c]
        if what == "v":
            return w_in[:, o_v:][:, c]
        if what == "attn_branch":
            return a["w_attn_branch"][0][:, c]
        if what == "xbc":
            return w_in[:, o_xbc:][:, c]
        if what == "dt":
            return w_in[:, o_dt:o_gate]
        if what == "z":
            return w_in[:, o_z:][:, c]
        if what == "ssm":
            return a["w_ssm_branch"][0][(k // 4) * D:(k // 4 + 1) * D, (k % 4) * UC:(k % 4 + 1) * UC]
        if what == "gates":
            return w_in[:, o_gate:][:, c]
        if what == "out":
            return a["w_out"][0][:, c]
        if what == "pw1":
            w = a["conv_w_pw1_2"][0]
            return np.concatenate([w[:, k * P:(k + 1) * P], w[:, D + k * P:D + (k + 1) * P]], axis=1)
        if what == "pw2":
            return a["conv_w_pw2_2"][0][:, c]
        if what == "att_qk":
            if k < 4:
                return att[:, c]
            heads = [att[:, D + (2 * (k - 4) + n) * HD:D + (2 * (k - 4) + n + 1) * HD] for n in range(2)]
            return np.concatenate([heads[0], heads[0], heads[1], heads[1]], axis=1)
        if what == "att_v":
            return att[:, kv:kv + UC]
        return a["attn_w_out_2"][0][:, c]

    plan = unit_plan()
    wall = np.empty((len(plan), P, UW), np.float32)
    for n, (what, k) in enumerate(plan):
        wall[n] = unit(one(what, k))
    wg2 = np.zeros((2, 48, 512), np.float32)
    wg2[:, 0:16] = a["gla_w_g2_2"][:, 0]
    wg2[:, 32:48] = a["gla_w_g2_2"][:, 1]
    relb = np.ascontiguousarray(a["rel_bias"])
    tokens = np.concatenate([a["x"][0], a["ctx_2"][0]])
    x = np.ascontiguousarray(tokens.T.reshape(KC, P, T2).transpose(1, 0, 2))
    cst, rel, rope = constants()
    return {"x": x, "vec": vec, "cst": cst, "rel": rel, "relb": relb, "wall": wall, "wg2": wg2, "rope": rope}


def kernel(**inputs):
    import concourse.bacc as _bacc
    from concourse.bass_utils import run_bass_kernel_spmd as _run

    arrays = lay_out({k: np.asarray(v) for k, v in inputs.items()})
    nc = _bacc.Bacc("TRN2", target_bir_lowering=False, num_devices=1)
    args = {n: nc.dram_tensor(f"in_{n}", v.shape, mybir.dt.from_np(v.dtype), kind="ExternalInput").ap()
            for n, v in arrays.items()}
    out = nc.dram_tensor("out", (P, KC, S), F32, kind="ExternalOutput").ap()
    program(nc, out=out, **args)
    r = _run(nc, [{f"in_{n}": v for n, v in arrays.items()}], core_ids=[0])
    y = r.results[0]["out"]
    return np.ascontiguousarray(y.transpose(1, 0, 2).reshape(D, S).T).reshape(1, S, D)
```

```python
from contextlib import ExitStack, contextmanager

import numpy as np

import concourse.bass as bass
from concourse import mybir

F32 = mybir.dt.float32
F32R = mybir.dt.float32r
ALU = mybir.AluOpType
ACT = mybir.ActivationFunctionType
AX = mybir.AxisListType

P = 128
D = 1024
KC = D // P
S = 256
T2 = 2 * S
EPS = 1e-6
UC = 256
UW = KC * UC
RAW = 4
SPL = 2
MODU = 24

HD = 64
GROUP_HEADS = 8
DILATIONS = (1, 4, 16)
NG = len(DILATIONS)
BUCKETS = 32
REL_MAX = 2048
NEG = -1e30
AW = NG * GROUP_HEADS * HD
DI = 2 * D
SSM_HEADS = DI // HD
SSM_G = 4
NST = 128
XBC = DI + 2 * SSM_G * NST
FF = 2816
FC = FF // P
XC = XBC // P
LAYERS = 4
FF2 = 4 * D
GH = 4
DV = 256
GCH = 64
TAPS = 31
PADT = TAPS // 2
TAPS_BESIDE = 11
QH = 16
MODC = 6 * KC


def layout(items):
    at, n = {}, 0
    for name, w in items:
        at[name] = (n, w)
        n += w
    return at, n


VEC, NVEC = layout([
    ("norm1", KC), ("norm2", KC), ("final", KC), ("conv_w", 4 * XC), ("conv_b", XC), ("dskip", DI // P),
    ("ssm_norm", DI // P), ("b_mod", LAYERS * MODC), ("g_mix", LAYERS * KC), ("g_mlp", LAYERS * KC),
    ("gla_b", 2 * 2 * GH), ("pw1_b", 2 * KC), ("dw_w", KC * TAPS), ("dw_b", KC), ("ln_g", KC), ("ln_b", KC),
    ("pw2_b", KC), ("g_q", 1), ("g_k", 1), ("c", 2 * KC), ("dt_b", SSM_HEADS), ("a_log", SSM_HEADS),
    ("g_head", 2 * DV)])
CST, NCST = layout([("ident", P), ("ones", P), ("tri", P), ("blocks", P), ("causal", GCH), ("anticausal", GCH),
                    ("restart", T2)])


def constants():
    c = np.zeros((P, NCST), np.float32)

    def put(name, a):
        o, w = CST[name]
        c[:, o:o + w] = a

    i = np.arange(P)
    put("ident", np.eye(P))
    put("ones", np.ones((P, P)))
    put("tri", i[:, None] <= i[None, :])
    put("blocks", i[:, None] // HD == i[None, :] // HD)
    j = np.arange(GCH)
    put("causal", (i[:, None] % GCH) <= j[None, :])
    put("anticausal", (i[:, None] % GCH) >= j[None, :])
    put("restart", np.broadcast_to(np.arange(T2) % GCH != 0, (P, T2)))

    dist = 255 - np.arange(384)
    d = np.clip(dist, 0, None)
    exact = BUCKETS // 2
    large = exact + (np.log(np.maximum(d, 1).astype(np.float32) / exact) / np.float32(np.log(REL_MAX / exact))
                     * (BUCKETS - exact)).astype(np.int32)
    bucket = np.where(d < exact, d, np.minimum(large, BUCKETS - 1))
    hot = (np.arange(BUCKETS)[:, None] == bucket[None, :]).astype(np.float32)
    mask = np.zeros((NG, 384), np.float32)
    for g, dil in enumerate(DILATIONS):
        ok = (dist >= 0) & (dist % dil == 0) & (dist // dil <= P)
        mask[g] = np.where(ok, 0.0, NEG)
    rel = np.zeros((BUCKETS, 384 + NG * 384), np.float32)
    rel[:, :384] = hot
    rel[:GROUP_HEADS, 384:] = mask.reshape(1, -1)

    n = HD // 4
    inv = np.float32(10000.0) ** (-np.arange(n, dtype=np.float32) / np.float32(n))
    tok = np.arange(S)
    ang = np.concatenate([(tok // 64).astype(np.float32)[:, None] * inv,
                          (tok % 64).astype(np.float32)[:, None] * inv], axis=-1)
    rope = np.zeros((P, P + 2 * S), np.float32)
    half = HD // 2
    f = i % HD
    for m in range(P):
        if f[m] < half:
            rope[m + half, m] = -1.0
        else:
            rope[m - half, m] = 1.0
    rope[:, P:P + S] = np.cos(ang).T[f % half]
    rope[:, P + S:] = np.sin(ang).T[f % half]
    return c, rel, rope


class Role:

    def __init__(self, eng, sems):
        self.eng, self.sems, self.n, self.loops, self.started = eng, sems, {}, [], False

    def value(self, key):
        v = self.n.get(key, 0)
        for reg, per in self.loops:
            if per.get(key, 0):
                v = reg * per[key] + v
        return v

    def next(self, name, k=1, key=None):
        key = key or "w " + name
        self.n[key] = self.n.get(key, 0) + k
        return self.sems[name], self.value(key)

    def made(self, name):
        self.n["m " + name] = self.n.get("m " + name, 0) + 1
        return self.sems[name], 1

    def own(self, name):
        return self.sems[name], self.value("m " + name)

    @contextmanager
    def loop(self, count, per):
        before = dict(self.n)
        with self.eng.Fori(0, count) as i:
            self.loops.append((i, per))
            yield i
            self.loops.pop()
        got = {k: v - before.get(k, 0) for k, v in self.n.items() if v != before.get(k, 0)}
        assert got == {k: v for k, v in per.items() if v}, (got, per)
        for k, v in got.items():
            self.n[k] += v * (count - 1)

    def groups(self, n, body):
        whole = n // 4
        peel = 1 if self.started else 2
        self.started = True
        if whole < peel + 2:
            for k in range(n):
                body(k, k % 4)
            return
        for k in range(4 * peel):
            if k == 4 * peel - 4:
                before = dict(self.n)
            body(k, k % 4)
        per = {k: v - before.get(k, 0) for k, v in self.n.items() if v != before.get(k, 0)}
        with self.loop(whole - peel, per) as i:
            for j in range(4):
                body(i * 4 + (4 * peel + j), j)
        for k in range(4 * whole, n):
            body(k, k % 4)


SEMS = (["raw_loaded%d" % i for i in range(RAW)] + [
    "params_loaded", "x_loaded", "rel_table", "rel_stored", "rel_loaded0", "rel_loaded1", "wg2_loaded",
    "rope_loaded", "result_ready", "stored",
    "mod_loaded0", "mod_loaded1", "cond_ready", "mod_ready", "mod_taken", "weighted", "product_ready", "product_summed", "hi_ready", "lo_ready", "chunk_ready", "chunk_taken", "part_ready", "part_hi", "part_lo",
    "dve_step", "act_step", "norm_input", "square_ready", "square_summed", "sum_ready", "stat_read", "rstd_ready",
    "gate_ready", "rel_rows", "cin_ready", "conv_ready",
    "scores_ready", "logits_taken", "neg_max", "exp_ready", "recip_ready", "probs_ready", "turned_ready",
    "turned_taken", "values_ready",
    "dt_abs", "dt_log", "dta_ready", "sums_ready", "xs_turned", "xs_taken", "b_turned", "b_taken",
    "toend_in", "toend_exp", "toend_ready", "state_ready", "state_taken", "cb_ready", "cb_taken",
    "spread_ready", "gap_ready", "decay_ready", "spread_exp", "mix_ready", "y_ready", "y_taken",
    "zg_ready", "zabs_ready", "zlog_ready", "cum_ready", "expb_ready", "gaps_ready", "kd_exp", "kd_ready",
    "kdt_ready", "att_ready", "att_taken", "s_ready", "s_taken", "o_ready", "o_taken", "osq_ready",
    "onorm_ready", "ot_ready", "ot_taken", "tap_product", "tap_summed", "dw_partial", "dw_ready", "mean_summed", "mean_ready", "mean_taken", "centred", "ln_ready",
    "head_squares", "heads_summed", "qstat_read", "qn_ready", "rot_ready", "rot_taken"])


def unit_plan():
    u = []

    def run(what, n):
        u.extend((what, k) for k in range(n))

    run("q", 6)
    run("k", 6)
    run("v", 6)
    run("attn_branch", 4)
    run("xbc", 12)
    run("dt", 1)
    run("z", 8)
    run("ssm", 8)
    run("gates", 8)
    run("out", 4)
    for p, n in enumerate((8, 8, 6)):
        run(("ffn_in", p), n)
        run(("ffn_out", p), 4)
    for i in range(LAYERS):
        if i % 3 == 0:
            run(("gla_qk", i // 3), 4)
            run(("gla_v", i // 3), 4)
            run(("gla_g1", i // 3), 1)
            run(("gla_r", i // 3), 4)
            run(("gla_out", i // 3), 4)
        elif i % 3 == 1:
            run("pw1", 8)
            run("pw2", 4)
        else:
            run("att_qk", 6)
            run("att_v", 1)
            run("att_out", 4)
        for p in range(4):
            run((("mlp_in", i), p), 4)
            run((("mlp_out", i), p), 4)
    return u


class Buffers:
    pass


def place(nc, ctx):
    b = Buffers()

    def sb(stack, name, shape, dt=F32):
        return stack.enter_context(nc.sbuf_tensor(name, shape, dt))

    b.vec = sb(ctx, "vec", [P, NVEC])
    b.cst = sb(ctx, "cst", [P, NCST])
    b.raw = [sb(ctx, f"raw{i}", [P, KC, UC]) for i in range(RAW)]
    b.whi = [sb(ctx, f"whi{i}", [P, KC, UC], F32R) for i in range(SPL)]
    b.wlo = [sb(ctx, f"wlo{i}", [P, KC, UC], F32R) for i in range(SPL)]
    b.x = sb(ctx, "x", [P, KC, T2])
    b.part = [sb(ctx, f"part{i}", [P, T2]) for i in range(4)]
    b.rstd = sb(ctx, "rstd", [P, T2])
    b.cond = sb(ctx, "cond", [P, KC, 2])
    b.mod = [sb(ctx, f"mod{i}", [P, 2 * MODC]) for i in range(2)]
    b.modg = sb(ctx, "modg", [P, 2 * KC * 2])
    b.sg = [sb(ctx, f"sg{i}", [P, T2]) for i in range(2)]
    b.small = sb(ctx, "small", [P, 64])

    with ExitStack() as one:
        b.xn1 = [sb(one, f"xn1{n}", [P, KC, S], F32R) for n in ("hi", "lo")]
        b.attn_out = sb(one, "attn_branch_out", [P, KC, S])
        with ExitStack() as st:
            b.ao = [sb(st, f"ao{n}", [P, 4, S], F32R) for n in ("hi", "lo")]
            b.qk = sb(st, "qk", [P, 2 * AW // P, S])
            b.v = sb(st, "v", [P, 2, AW])
            b.rel = sb(st, "rel", [BUCKETS, 384 * (1 + NG)])
            b.relb = sb(st, "relb", [BUCKETS, NG * GROUP_HEADS])
            b.reltab = sb(st, "reltab", [GROUP_HEADS, NG, 384])
            with ExitStack() as qk:
                mod_qk = [sb(qk, f"modw_qk{i}", [P, KC, UC]) for i in range(2)]
                sum_qk = [sb(qk, f"mods_qk{i}", [P, 2, UC]) for i in range(2)]
                product_qk = sb(qk, "modp_qk", [P, 4, UC])
            b.bias = [sb(st, f"bias{i}", [P, NG, S]) for i in range(2)]
            b.logits = [sb(st, f"logits{i}", [P, NG, S]) for i in range(2)]
            b.turned = [sb(st, f"turned{i}", [P, 6, P]) for i in range(2)]
        b.y = sb(one, "y", [P, DI // P, S])
        with ExitStack() as st:
            b.xbc = sb(st, "xbc", [P, XC, S])
            with ExitStack() as cv:
                b.cin = [sb(cv, f"cin{i}", [P, S + 4]) for i in range(2)]
                b.cacc = [sb(cv, f"cacc{i}", [P, S]) for i in range(2)]
                mod_xbc = [sb(cv, f"modw_xbc{i}", [P, KC, UC]) for i in range(2)]
                sum_xbc = [sb(cv, f"mods_xbc{i}", [P, 2, UC]) for i in range(2)]
                product_xbc = sb(cv, "modp_xbc", [P, 4, UC])
            b.xdt = sb(st, "xdt", [P, 2, DI])
            b.dt = sb(st, "dt", [P, 8, 2, SSM_HEADS])
            b.toend_x = sb(st, "toend_x", [P, 512])
            b.state1 = sb(st, "state1", [P, SSM_G, 512])
            b.bt = sb(st, "bt", [P, SSM_G, P])
            b.cbm = sb(st, "cbm", [P, SSM_G, P])
            b.gap = [sb(st, f"gap{i}", [P, 4, P]) for i in range(2)]
        with ExitStack() as st:
            b.big = [sb(st, f"big{n}", [P, DI // P, S], F32R) for n in ("hi", "lo")]
            b.ssm_out = sb(st, "ssm_branch_out", [P, KC, S])
    b.xn = [sb(ctx, f"xn{n}", [P, KC, T2], F32R) for n in ("hi", "lo")]
    with ExitStack() as st:
        b.hid = [sb(st, f"hid{n}", [P, KC, T2], F32R) for n in ("hi", "lo")]
        mod_mlp = [sb(st, f"modw_mlp{i}", [P, KC, UC]) for i in range(2)]
        sum_mlp = [sb(st, f"mods_mlp{i}", [P, 2, UC]) for i in range(2)]
        product_mlp = sb(st, "modp_mlp", [P, 4, UC])
    b.modw = {"qk": mod_qk, "xbc": mod_xbc, "mlp": mod_mlp}
    b.mods = {"qk": sum_qk, "xbc": sum_xbc, "mlp": sum_mlp}
    b.modp = {"qk": product_qk, "xbc": product_xbc, "mlp": product_mlp}
    with ExitStack() as st:
        b.gqk = sb(st, "gqk", [P, 2 * GH, T2])
        b.gv = sb(st, "gv", [P, 4, D])
        b.go = sb(st, "go", [P, 4, D])
        b.g1 = sb(st, "g1", [48, T2])
        b.wg2 = sb(st, "wg2", [48, 512])
        two = lambda name, shape: [[sb(st, f"{name}{i}{j}", shape) for j in range(2)] for i in range(2)]
        b.ends, b.qb = two("ends", [P, 8]), two("qb", [P, T2])
        room = [b.gqk[:, 0, :].rearrange("p (d a t) -> p d a t", d=2, t=GCH), b.gqk[:, GH, :]]
        b.kdt = [[sb(st, f"kdt{j}", [P, 4, P]) for j in range(2)],
                 [room[1].rearrange("p (a t) -> p a t", t=P), sb(st, "kdt_odd", [P, 4, P])]]
        b.att = [[sb(st, f"att{j}", [P, 4, GCH]) for j in range(2)], [room[0][:, j, :, :] for j in range(2)]]
        b.gs2 = [[b.sg[i][:, j * DV:(j + 1) * DV] for j in range(2)] for i in range(2)]
    with ExitStack() as st:
        b.u = sb(st, "u", [P, KC, 2, S + TAPS - 1])
        b.dw = sb(st, "dw", [P, KC, T2])
        b.nmean = sb(st, "nmean", [P, T2])
        b.tap = [sb(st, f"tap{i}", [P, T2]) for i in range(4)]
        b.taps = sb(st, "taps", [P, T2])
    with ExitStack() as st:
        b.rope = sb(st, "rope", [P, P + 2 * S])
        b.aqk = sb(st, "aqk", [P, 12, T2])
        b.av = sb(st, "av", [P, 4, UC])
        b.prob = [sb(st, f"prob{i}", [P, T2]) for i in range(3)]
        b.pt = [sb(st, f"pt{i}", [P, 4, P]) for i in range(2)]
    b.bank = [ctx.enter_context(nc.psum_tensor(f"bank{i}", [P, 512], F32)) for i in range(8)]
    return b


def loads(nc, b, dram, R, sp):
    sp.dma_start(b.vec[:], dram["vec"]).then_inc(R.sems["params_loaded"], 16)
    sp.dma_start(b.cst[:], dram["cst"]).then_inc(R.sems["params_loaded"], 16)
    sp.dma_start(b.x[:], dram["x"]).then_inc(R.sems["x_loaded"], 16)
    sp.dma_start(b.rel[:], dram["rel"]).then_inc(R.sems["params_loaded"], 16)
    sp.dma_start(b.relb[:], dram["relb"]).then_inc(R.sems["params_loaded"], 16)
    wall, at = dram["wall"], dram["at"]
    units = at["units"]

    def unit(u, j, first):
        if not first:
            sp.wait_ge(*R.next("lo_ready"))
        src = wall[u] if isinstance(u, int) else wall[bass.ds(u, 1)].rearrange("a p n -> (a p) n")
        sp.dma_start(b.raw[j][:].rearrange("p k n -> p (k n)"), src).then_inc(R.sems[f"raw_loaded{j}"], 16)

    def mod_unit(m, place, first=False):
        number, slot = m
        if not first:
            sp.wait_ge(*R.next("mod_ready"))
        wmod = dram["wmod"]
        src = wmod[number] if isinstance(number, int) else wmod[bass.ds(number, 1)].rearrange("a p n -> (a p) n")
        sp.dma_start(b.modw[place][slot][:].rearrange("p k n -> p (k n)"), src) \
            .then_inc(R.sems[f"mod_loaded{slot}"], 16)

    def run(u0, n, m0=None, place=None):
        def one(k):
            unit(u0 + k, (u0 + k) % RAW, u0 + k < RAW)
            if m0 is not None:
                mod_unit((m0 + k, (m0 + k) % 2), place, m0 + k < 2)

        k = 0
        while k < n and ((u0 + k) % RAW or u0 + k < RAW):
            one(k)
            k += 1
        turns = (n - k) // RAW
        if turns > 1:
            with R.loop(turns, {"w lo_ready": RAW, "w mod_ready": RAW if m0 is not None else 0}) as i:
                for j in range(RAW):
                    unit(i * RAW + (u0 + k + j), j, False)
                    if m0 is not None:
                        mod_unit((i * RAW + (m0 + k + j), (m0 + k + j) % 2), place)
            k += RAW * turns
        while k < n:
            one(k)
            k += 1

    run(0, at["v"], 0, "qk")
    sp.wait_ge(*R.next("rel_table"))
    sp.dma_start(dram["reltab"], b.reltab[:]).then_inc(R.sems["rel_stored"], 16)
    sp.wait_ge(R.sems["rel_stored"], 16)
    tab = dram["reltab"]

    def window(h):
        return bass.AP(tensor=tab.tensor, offset=tab.offset + h * NG * 384, ap=[[1, P], [384, NG], [1, S]])

    run(at["v"], at["xbc"] - at["v"])
    sp.wait_ge(R.sems["mod_ready"], at["v"])
    for h in range(GROUP_HEADS):
        if h >= 2:
            sp.wait_ge(R.sems["logits_taken"], 2 * (h - 1))
        sp.dma_start(b.bias[h % 2][:], window(h)).then_inc(R.sems[f"rel_loaded{h % 2}"], 16)
    sp.wait_ge(R.sems["chunk_taken"], 2 * at["attn_branch"] + 1)
    run(at["xbc"], 12, at["v"], "xbc")
    done = at["xbc"] + 12
    for i in range(LAYERS):
        if i % 3 == 0:
            first = at[("gla_g1", i // 3)]
            run(done, first - done)
            done = first
            sp.wait_ge(R.sems["chunk_taken"], 2 * at[("gla_v", i // 3)])
            sp.dma_start(b.wg2[:], dram["wg2"][i // 3]).then_inc(R.sems["wg2_loaded"], 16)
        elif i % 3 == 2:
            first = at["att_v"]
            run(done, first - done)
            done = first
            sp.wait_ge(R.sems["chunk_taken"], 2 * at["att_qk"] + 4)
            sp.dma_start(b.rope[:], dram["rope"]).then_inc(R.sems["rope_loaded"], 16)
        if i < LAYERS - 1:
            first = at[(("mlp_in", i), 0)]
            run(done, first - done)
            sp.wait_ge(R.sems["chunk_taken"], 2 * (first - 4) + 1)
            run(first, MODU, MODU * (i + 1), "mlp")
            done = first + MODU
    run(done, units - done)
    sp.wait_ge(*R.next("result_ready"))
    sp.dma_start(dram["out"], b.x[:, :, 0:S]).then_inc(R.sems["stored"], 16)
    sp.wait_ge(R.sems["stored"], 16)


def products(nc, b, R, pe, at):
    mm = nc.tensor.matmul
    g = {"chunks": 0, "unit": 0, "norms": 0, "mods": 0}
    bank = b.bank
    cst = lambda name: b.cst[:, CST[name][0]:CST[name][0] + CST[name][1]]
    ident, ones, tri = cst("ident"), cst("ones"), cst("tri")

    def three(out, w, x, first, last):
        (wh, wl), (xh, xl) = w, x
        mm(out, wh, xh, start=first, stop=False)
        mm(out, wh, xl, start=False, stop=False)
        return mm(out, wl, xh, start=False, stop=last)

    def unit(x, t, kc=KC, k0=0, tokens_out=False, fresh=False):
        s = g["unit"] % SPL
        pe.wait_ge(*R.next("lo_ready"))
        for c in range(2):
            if g["chunks"] >= 4:
                pe.wait_ge(*R.next("chunk_taken"))
            out = bank[2 * s + c]
            if not tokens_out:
                for k in range(kc):
                    if fresh and c == 0:
                        pe.wait_ge(*R.next("part_lo"))
                    last = three(out[:, 0:t], [w[s][:, k, c * P:(c + 1) * P] for w in (b.whi, b.wlo)],
                                 [h[:, k0 + k, 0:t] for h in x], k == 0, k == kc - 1)
            else:
                tiles = t // P // 2
                for a in range(tiles):
                    o = (c * tiles + a) * P
                    for k in range(kc):
                        last = three(out[:, a * UC:(a + 1) * UC], [h[:, k0 + k, o:o + P] for h in x],
                                     [w[s][:, k, :] for w in (b.whi, b.wlo)], k == 0, k == kc - 1)
            last.then_inc(*R.made("chunk_ready"))
            g["chunks"] += 1
        g["unit"] += 1

    def mod_unit(sums, slot):
        pe.wait_ge(*R.next("weighted"))
        pe.wait_ge(*R.next("product_summed", KC - 1))
        if g["mods"]:
            pe.wait_ge(*R.next("mod_taken"))
        g["mods"] += 1
        for c in range(2):
            for stream in range(2):
                o = 2 * c + stream
                last = mm(bank[7][:, o:o + 1], sums[slot][:, stream, c * P:(c + 1) * P], ones[:, 0:1],
                          start=True, stop=True)
        last.then_inc(*R.made("mod_ready"))

    def stage(n, x, t, mod=None, fresh=False, **kw):
        def one(k, j):
            unit(x, t, fresh=fresh and isinstance(k, int) and k == 0, **kw)
            if mod:
                mod_unit(b.mods[mod], j % 2)
        R.groups(n, one)

    def norm_sum(t, n=KC):
        if g["norms"]:
            pe.wait_ge(*R.next("stat_read"))
        g["norms"] += 1
        pe.wait_ge(*R.next("square_summed", n - 1))
        mm(bank[4][:, 0:t], ones, b.part[2][:, 0:t], start=True, stop=True).then_inc(*R.made("sum_ready"))

    pe.wait_ge(R.sems["params_loaded"], 64)
    for gr in range(NG):
        last = mm(bank[5 + gr][0:GROUP_HEADS, 0:384], b.relb[:, gr * GROUP_HEADS:(gr + 1) * GROUP_HEADS],
                  b.rel[:, 0:384], start=True, stop=True)
    last.then_inc(*R.made("rel_rows"))
    norm_sum(S)
    stage(6, b.xn1, S, mod="qk", fresh=True)
    stage(6, b.xn1, S, mod="qk")
    stage(6, b.xn1, S, tokens_out=True)

    pe.wait_ge(R.sems["chunk_taken"], 2 * at["attn_branch"])
    steps = [(h, qt) for h in range(GROUP_HEADS) for qt in range(2)]

    def scores(n):
        h, qt = steps[n]
        nk = P * (qt + 1)
        base = HD * (h % 2)
        if n >= 2:
            pe.wait_ge(*R.next("logits_taken"))
        for gr in range(NG):
            c = gr * 4 + h // 2
            out = bank[4 + 2 * (n % 2) + gr // 2][:, (gr % 2) * S:(gr % 2) * S + nk]
            last = mm(out, b.qk[base:base + HD, c, qt * P:(qt + 1) * P],
                      b.qk[base:base + HD, 12 + c, 0:nk], start=True, stop=True)
        last.then_inc(*R.made("scores_ready"))

    before = R.n["w part_lo"]

    def values(n):
        h, qt = steps[n]
        kt = qt + 1
        if n >= 8 and n % 4 == 0:
            pe.wait_ge(R.sems["part_lo"], before + h // 2 - 1)
        base = HD * (h % 2)
        for i in range(NG * kt):
            col = (i // kt) * GROUP_HEADS * HD + h * HD
            last = mm(bank[2 + (h // 2) % 2][base:base + HD, qt * P:(qt + 1) * P],
                      b.v[:, i % kt, col:col + HD], b.turned[n % 2][:, i, :], start=(i == 0),
                      stop=(i == NG * kt - 1))
        last.then_inc(*R.made("values_ready"))

    scores(0)
    for n, (h, qt) in enumerate(steps):
        if n + 1 < len(steps):
            scores(n + 1)
        kt = qt + 1
        pe.wait_ge(*R.next("probs_ready"))
        if n:
            pe.wait_ge(*R.next("turned_taken"))
        for i in range(NG * kt):
            last = nc.tensor.transpose(bank[i // 4][:, (i % 4) * P:(i % 4 + 1) * P],
                                       b.logits[n % 2][:, i // kt, (i % kt) * P:(i % kt + 1) * P], ident)
        last.then_inc(*R.made("turned_ready"))
        if n:
            values(n - 1)
    pe.wait_ge(*R.next("turned_taken"))
    values(len(steps) - 1)
    stage(4, b.ao, S, kc=4, fresh=True)
    stage(12, b.xn1, S, mod="xbc")
    stage(1, b.xn1, S, tokens_out=True)

    for ct in range(2):
        for gr in range(SSM_G):
            if gr == 0 and ct == 0:
                pe.wait_ge(R.sems["chunk_taken"], 2 * at["z"])
            if ct * SSM_G + gr >= 2:
                pe.wait_ge(*R.next("xs_taken"))
            for c in range(4):
                last = nc.tensor.transpose(bank[4 + gr % 2][:, c * P:(c + 1) * P],
                                           b.xbc[:, gr * 4 + c, ct * P:(ct + 1) * P], ident)
            last.then_inc(*R.made("xs_turned"))
    pe.wait_ge(*R.next("dta_ready"))
    for ct in range(2):
        mm(bank[6][:, ct * 64:ct * 64 + 32], tri, b.dt[:, 2, ct, :], start=True, stop=True)
        last = mm(bank[6][:, ct * 64 + 32:ct * 64 + 64], ones, b.dt[:, 2, ct, :], start=True, stop=True)
    last.then_inc(*R.made("sums_ready"))
    for gr in range(SSM_G):
        last = nc.tensor.transpose(bank[7][:, gr * P:(gr + 1) * P], b.xbc[:, 16 + gr, 0:P], ident)
    last.then_inc(*R.made("b_turned"))
    pe.wait_ge(*R.next("xs_taken", 2))
    pe.wait_ge(*R.next("b_taken"))
    for gr in range(SSM_G):
        pe.wait_ge(*R.next("toend_ready"))
        mm(bank[4 + gr % 2][:, :], b.bt[:, gr, :], b.toend_x[:], start=True, stop=True) \
            .then_inc(*R.made("state_ready"))
    pe.wait_ge(*R.next("state_taken", SSM_G))
    spread = [5, 6]

    def spread_sums(n):
        ct, quad = n // 8, n % 8
        if 2 <= n < 10:
            pe.wait_ge(*R.next("gap_ready"))
        elif n >= 10:
            pe.wait_ge(*R.next("spread_exp"))
        for h in range(4):
            last = mm(bank[spread[n % 2]][:, h * P:(h + 1) * P],
                      b.dt[:, 2, ct, quad * 4 + h:quad * 4 + h + 1].to_broadcast([P, P]), tri,
                      start=True, stop=True)
        last.then_inc(*R.made("spread_ready"))

    for ct in range(2):
        if ct:
            pe.wait_ge(*R.next("cb_taken"))
        for gr in range(SSM_G):
            last = mm(bank[4][:, gr * P:(gr + 1) * P], b.xbc[:, 16 + gr, ct * P:(ct + 1) * P],
                      b.xbc[:, 20 + gr, ct * P:(ct + 1) * P], start=True, stop=True)
        last.then_inc(*R.made("cb_ready"))
        spread_sums(ct * 8)
        for quad in range(8):
            n = ct * 8 + quad
            if quad < 7:
                spread_sums(n + 1)
            pe.wait_ge(*R.next("mix_ready"))
            if n >= 2:
                pe.wait_ge(*R.next("y_taken"))
            for h in range(4):
                head = quad * 4 + h
                out = bank[n % 2][HD * (h % 2):HD * (h % 2) + HD, (h // 2) * P:(h // 2 + 1) * P]
                last = mm(out, b.xdt[:, ct, head * HD:(head + 1) * HD], b.gap[n % 2][:, h, :],
                          start=True, stop=(ct == 0))
                if ct:
                    last = mm(out, b.state1[:, head // 8, (head % 8) * HD:(head % 8 + 1) * HD],
                              b.part[2 + n % 2][:, h * P:(h + 1) * P], start=False, stop=True)
            last.then_inc(*R.made("y_ready"))
    pe.wait_ge(*R.next("y_taken", 2))
    stage(8, b.xn1, S)
    for gr in range(SSM_G):
        norm_sum(S, n=4)
    stage(4, b.big, S, fresh=True)
    stage(4, b.big, S, k0=KC, fresh=True)
    stage(8, b.xn1, S)
    stage(4, b.big, S, fresh=True)
    norm_sum(S)
    for p, n in enumerate((8, 8, 6)):
        stage(n, b.xn1, S, fresh=(p == 0))
        stage(4, b.big, S, kc=n, fresh=True)
    norm_sum(S)

    def gla(i, t):
        last_layer = i == LAYERS - 1
        stage(4, b.xn, T2, fresh=True)
        stage(4, b.xn, T2, tokens_out=True)
        stage(1, b.xn, T2)
        pe.wait_ge(R.sems["chunk_taken"], 2 * at[("gla_r", i // 3)])
        pe.wait_ge(R.sems["wg2_loaded"], 16 * (i // 3 + 1))

        def gate_input(h, d):
            mm(bank[4][:, :], b.wg2[32 * d:32 * d + 16, h * P:(h + 1) * P], b.g1[32 * d:32 * d + 16, :],
               start=True, stop=True).then_inc(*R.made("zg_ready"))

        def weights(h, d):
            pe.wait_ge(*R.next("kd_ready"))
            if d:
                pe.wait_ge(*R.next("att_taken"))
            for tt in range(4):
                last = nc.tensor.transpose(bank[5][:, tt * P:(tt + 1) * P], b.part[1][:, tt * P:(tt + 1) * P],
                                           ident)
            last.then_inc(*R.made("kdt_ready"))
            for n in range(8):
                half = 64 * (n % 2)
                last = mm(bank[6][half:half + 64, (n // 2) * GCH:(n // 2 + 1) * GCH],
                          b.part[3][:, n * GCH:(n + 1) * GCH], b.qb[h % 2][d][:, n * GCH:(n + 1) * GCH],
                          start=True, stop=True)
            last.then_inc(*R.made("att_ready"))

        def scan_step(h, s, d):
            n = [[4, 5, 6, 7, 0, 1, 2, 3], [7, 6, 5, 4, 3, 2, 1, 0]][d][s]
            half, tt = 64 * (n % 2), n // 2
            vv = b.gv[half:half + 64, tt, h * DV:(h + 1) * DV]
            if s:
                pe.wait_ge(*R.next("s_taken"))
            if s < 7:
                mm(bank[d][:, 0:DV], b.kdt[h % 2][d][half:half + 64, tt, :], vv, start=True, stop=True) \
                    .then_inc(*R.made("s_ready"))
            if s < 4 and last_layer:
                return
            if (s == 4 and not last_layer) or (s == (4 if last_layer else 0) and h):
                pe.wait_ge(*R.next("o_taken"))
            out = bank[2 + d][half:half + 64, (tt % 2) * DV:(tt % 2 + 1) * DV]
            if s:
                mm(out, b.qb[h % 2][d][:, n * GCH:(n + 1) * GCH], b.gs2[d][s % 2], start=True, stop=False)
            last = mm(out, b.att[h % 2][d][half:half + 64, tt, :], vv, start=(s == 0), stop=True)
            if s % 4 == 3:
                last.then_inc(*R.made("o_ready"))

        gate_input(0, 0)
        weights(0, 0)
        gate_input(0, 1)
        weights(0, 1)
        for h in range(GH):
            pe.wait_ge(*R.next("att_taken"))
            ahead = h + 1 < GH
            if ahead:
                gate_input(h + 1, 0)
            for s in range(8):
                for d in range(2):
                    scan_step(h, s, d)
                if ahead and s == 3:
                    weights(h + 1, 0)
                    gate_input(h + 1, 1)
                if ahead and s == 6:
                    weights(h + 1, 1)
        pe.wait_ge(*R.next("o_taken", 2))
        for fc in range(KC):
            if fc == 0:
                pe.wait_ge(*R.next("onorm_ready"))
            if fc >= 2:
                pe.wait_ge(*R.next("ot_taken"))
            for tt in range(t // P):
                last = nc.tensor.transpose(bank[5 + fc % 2][:, tt * P:(tt + 1) * P],
                                           b.go[:, tt, fc * P:(fc + 1) * P], ident)
            last.then_inc(*R.made("ot_ready"))
        pe.wait_ge(*R.next("ot_taken", 2))
        stage(4, b.xn, t)
        stage(4, b.xn, t, fresh=True)

    def conv():
        stage(8, b.xn, T2, fresh=True)
        pe.wait_ge(*R.next("mean_summed", KC - 1))
        mm(bank[5][:, :], ones, b.nmean[:], start=True, stop=True).then_inc(*R.made("mean_ready"))
        norm_sum(T2)
        stage(4, b.xn, T2, fresh=True)

    def attention():
        stage(6, b.xn, T2, fresh=True)
        stage(1, b.xn, T2, tokens_out=True)
        pe.wait_ge(R.sems["chunk_taken"], 2 * at["att_out"])
        pe.wait_ge(R.sems["rope_loaded"], 16)
        for c in range(12):
            pe.wait_ge(*R.next("head_squares"))
            if c >= 2:
                pe.wait_ge(*R.next("qstat_read"))
            mm(bank[4 + c % 2][:, :], cst("blocks"), b.part[c % 2][:, :], start=True, stop=True) \
                .then_inc(*R.made("heads_summed"))
            pe.wait_ge(*R.next("qn_ready"))
            if c >= 2:
                pe.wait_ge(*R.next("rot_taken"))
            mm(bank[6 + c % 2][:, 0:S], b.rope[:, 0:P], b.aqk[:, c, 0:S], start=True, stop=True) \
                .then_inc(*R.made("rot_ready"))
        pe.wait_ge(*R.next("qstat_read", 2))
        pe.wait_ge(*R.next("rot_taken", 2))
        steps = [(h, qt) for h in range(QH) for qt in range(4)]
        score_bank, turned_bank = (4, 5, 1), (6, 7)

        def scores(n):
            h, qt = steps[n]
            base = HD * (h % 2)
            keys = slice(0, T2) if qt < 2 else slice(S, T2)
            mm(bank[score_bank[n % 3]][:, 0:keys.stop - keys.start],
               b.aqk[base:base + HD, h // 2, qt * P:(qt + 1) * P],
               b.aqk[base:base + HD, 8 + h // 4, keys], start=True, stop=True).then_inc(*R.made("scores_ready"))

        def values(n):
            h, qt = steps[n]
            tiles = range(4) if qt < 2 else range(2, 4)
            pe.wait_ge(*R.next("turned_taken"))
            if n % 8 == 0 and n >= 16:
                pe.wait_ge(R.sems["part_lo"], before + h // 2 - 1)
            base = HD * (h % 2)
            for i, kt in enumerate(tiles):
                last = mm(bank[2 + (h // 2) % 2][base:base + HD, qt * P:(qt + 1) * P],
                          b.av[:, kt, (h // 4) * HD:(h // 4 + 1) * HD], b.pt[n % 2][:, i, :],
                          start=(i == 0), stop=(i == len(tiles) - 1))
            last.then_inc(*R.made("values_ready"))

        before = R.n["w part_lo"]
        scores(0)
        scores(1)
        for n, (h, qt) in enumerate(steps):
            if n + 2 < len(steps):
                scores(n + 2)
            pe.wait_ge(*R.next("probs_ready"))
            for i in range(4 if qt < 2 else 2):
                last = nc.tensor.transpose(bank[turned_bank[n % 2]][:, i * P:(i + 1) * P],
                                           b.prob[n % 3][:, i * P:(i + 1) * P], ident)
            last.then_inc(*R.made("turned_ready"))
            if n:
                values(n - 1)
        values(len(steps) - 1)
        stage(4, b.xn, T2, fresh=True)

    for i in range(LAYERS):
        t = S if i == LAYERS - 1 else T2
        norm_sum(T2)
        if i % 3 == 0:
            gla(i, t)
        elif i % 3 == 1:
            conv()
        else:
            attention()
        norm_sum(t)

        def piece(mod, fresh=False):
            stage(4, b.xn, t, mod=mod, fresh=fresh)
            stage(4, b.hid, t, mod=mod, fresh=True)

        per = {"w lo_ready": 8, "w chunk_taken": 16, "m chunk_ready": 16, "w part_lo": KC}
        if i < LAYERS - 1:
            per.update({"w weighted": 8, "w product_summed": 56, "w mod_taken": 8, "m mod_ready": 8})
        piece("mlp" if i < LAYERS - 1 else None, fresh=True)
        with R.loop(2, per):
            piece("mlp" if i < LAYERS - 1 else None)
        piece(None)


def splits_and_functions(nc, b, R, act, at):
    fn = nc.scalar.activation
    g = {"unit": 0, "taken": 0, "part": 0, "mods": 0}
    bank = b.bank
    total = at["units"]

    def split():
        u = g["unit"]
        act.wait_ge(*R.next(f"raw_loaded{u % RAW}", 16))
        if u >= SPL:
            act.wait_ge(*R.next("chunk_ready", 2, "hl_free"))
        nc.scalar.copy(b.whi[u % SPL][:], b.raw[u % RAW][:]).then_inc(*R.made("hi_ready"))
        g["unit"] += 1

    def part(dst, src=None, width=None, by_chunk=None):
        if by_chunk is None:
            act.wait_ge(*R.next("part_ready"))
        else:
            act.wait_ge(R.sems["chunk_taken"], by_chunk)
        src = b.part[g["part"] % 4][:, 0:width] if src is None else src
        nc.scalar.copy(dst, src).then_inc(*R.made("part_hi"))
        g["part"] += 1

    def chunk():
        act.wait_ge(*R.next("chunk_ready", 1, "evac"))

    def room():
        act.wait_ge(R.sems["chunk_taken"], R.value("evac") + (-2))

    def products(place, slot):
        act.wait_ge(*R.next(f"mod_loaded{slot}", 16))
        w = b.modw[place][slot]
        for k in range(KC):
            if k != 5 and (k >= 4 or g["mods"]):
                act.wait_ge(*R.next("product_summed"))
            fn(b.modp[place][:, k % 4, :], w[:, k, :], ACT.Copy, scale=b.cond[:, k, 1:2]) \
                .then_inc(*R.made("product_ready"))
        g["mods"] += 1

    def stage(n, body=None, last=False, mod=None):
        def one(k, j):
            if not (last and isinstance(k, int) and k == n - 1):
                split()
            if mod:
                products(mod, j % 2)
            if body is None:
                R.n["evac"] = R.n.get("evac", 0) + 2
            else:
                body(k)
            g["taken"] += 1
        R.groups(n, one)

    def bank_of(c):
        return bank[2 * (g["taken"] % SPL) + c]

    def square(c, src, t):
        if c == 2 or c >= 4:
            act.wait_ge(*R.next("square_summed"))
        fn(b.part[c % 2][:, 0:t], src, ACT.Square).then_inc(*R.made("square_ready"))

    def squares(src, t, n=KC):
        act.wait_ge(*R.next("norm_input"))
        act.wait_ge(R.sems["part_lo"], R.value("m part_hi"))
        for c in range(n):
            square(c, src(c), t)

    def taken_squares(t):
        def body(k):
            for c in range(2):
                R.n["evac"] += 1
                act.wait_ge(R.sems["chunk_taken"], R.value("evac"))
                square(2 * k + c, b.x[:, 2 * k + c, 0:t], t)
        return body

    def rstd(t, width):
        R.next("square_summed", 2)
        act.wait_ge(*R.next("sum_ready"))
        fn(b.rstd[:, 0:t], bank[4][:, 0:t], ACT.Ln, bias=b.small[:, 63:64], scale=1.0 / width) \
            .then_inc(*R.made("stat_read"))
        act.wait_ge(*R.own("stat_read"))
        fn(b.rstd[:, 0:t], b.rstd[:, 0:t], ACT.Exp, scale=-0.5).then_inc(*R.made("rstd_ready"))

    def norm(t):
        squares(lambda c: b.x[:, c, 0:t], t)
        rstd(t, D)

    act.wait_ge(R.sems["params_loaded"], 64)
    act.wait_ge(R.sems["dve_step"], 1)
    cv = VEC["c"][0]
    fn(b.small[:, 0:16], b.vec[:, cv:cv + 16], ACT.Sigmoid).then_inc(*R.made("gate_ready"))
    split()
    act.wait_ge(R.sems["x_loaded"], 16)
    norm(S)
    for c in range(KC):
        part(b.xn1[0][:, c, :], width=S)
    act.wait_ge(*R.next("cond_ready"))
    stage(6, mod="qk")
    stage(6, mod="qk")
    stage(6)

    def exponent(n):
        act.wait_ge(*R.next("neg_max"))
        nk = P * (n % 2 + 1)
        fn(b.logits[n % 2][:, :, 0:nk], b.logits[n % 2][:, :, 0:nk], ACT.Exp, bias=b.small[:, 20 + n % 2:21 + n % 2],
           accum_out=b.small[:, 24 + n % 2:25 + n % 2]).then_inc(*R.made("exp_ready"))

    for n in range(2 * GROUP_HEADS):
        exponent(n)
        act.wait_ge(*R.next("recip_ready"))
        nk = P * (n % 2 + 1)
        fn(b.logits[n % 2][:, :, 0:nk], b.logits[n % 2][:, :, 0:nk], ACT.Copy,
           scale=b.small[:, 28 + n % 2:29 + n % 2]).then_inc(*R.made("probs_ready"))
        if n % 4 == 1 and n > 1:
            part(b.ao[0][:, n // 4 - 1, :], width=S)
    part(b.ao[0][:, 3, :], width=S)
    stage(4)

    def conv_in(k):
        for c in range(2):
            chunk()
            nc.scalar.copy(b.cin[c][:, 3:3 + S], bank_of(c)[:, 0:S]).then_inc(*R.made("cin_ready"))
        for c in range(2):
            act.wait_ge(*R.next("conv_ready"))
            fn(b.sg[c][:, 0:S], b.cacc[c][:], ACT.Sigmoid).then_inc(*R.made("gate_ready"))

    stage(12, conv_in, mod="xbc")
    stage(1)

    al = VEC["a_log"][0]
    act.wait_ge(*R.next("dt_abs"))
    fn(b.dt[:, 7, 0, :], b.vec[:, al:al + SSM_HEADS], ACT.Exp).then_inc(*R.made("act_step"))
    ab = b.dt[:, 1, :, :]
    fn(ab, ab, ACT.Exp, scale=-1.0).then_inc(*R.made("act_step"))
    act.wait_ge(*R.own("act_step"))
    fn(ab, ab, ACT.Ln, bias=1.0).then_inc(*R.made("dt_log"))
    act.wait_ge(*R.next("toend_in"))
    fn(b.dt[:, 6, 0, :], b.dt[:, 6, 0, :], ACT.Exp).then_inc(*R.made("toend_exp"))
    for n in range(16):
        act.wait_ge(*R.next("gap_ready"))
        fn(b.gap[n % 2][:], b.gap[n % 2][:], ACT.Exp).then_inc(*R.made("decay_ready"))
        if n >= 8:
            fn(b.part[n % 2][:], bank[5 + n % 2][:], ACT.Exp).then_inc(*R.made("spread_exp"))

    def gates(k):
        for c in range(2):
            chunk()
            room()
            fn(b.sg[c][:, 0:S], bank_of(c)[:, 0:S], ACT.Sigmoid).then_inc(*R.made("gate_ready"))

    stage(8, gates)
    for gr in range(SSM_G):
        squares(lambda c: b.y[:, 4 * gr + c, :], S, 4)
        rstd(S, DI // SSM_G)
        for c in range(4):
            part(b.big[0][:, 4 * gr + c, :], width=S)
    stage(8)

    def branch_gates(k):
        gates(k)
        if k >= 4:
            for c in range(2):
                part(b.big[0][:, 2 * (k - 4) + c, :], width=S)

    stage(8, branch_gates)
    stage(4, taken_squares(S))
    rstd(S, D)
    for c in range(KC):
        part(b.xn1[0][:, c, :], width=S)
    for n in (8, 8, 6):
        def ffn(k):
            chunk()
            room()
            fn(b.sg[0][:, 0:S], bank_of(0)[:, 0:S], ACT.Sigmoid).then_inc(*R.made("gate_ready"))
            R.n["evac"] += 1
            part(b.big[0][:, k, :], width=S, by_chunk=R.value("evac"))
        stage(n, ffn)
        stage(4, taken_squares(S) if n == 6 else None)
    rstd(S, D)

    def operand_parts(t, dst=None):
        for c in range(KC):
            part(b.xn[0][:, c, 0:t], width=t)

    def wide_gates(t):
        def body(k):
            for c in range(2):
                chunk()
                room()
                fn(b.sg[c][:, 0:t], bank_of(c)[:, 0:t], ACT.Sigmoid).then_inc(*R.made("gate_ready"))
        return body

    def gla(i, t):
        stage(9)
        z, ab, eb, enb = b.part
        for h in range(GH):
            for d in range(2):
                act.wait_ge(*R.next("zabs_ready"))
                fn(ab[:], ab[:], ACT.Exp, scale=-1.0).then_inc(*R.made("act_step"))
                act.wait_ge(*R.own("act_step"))
                fn(ab[:], ab[:], ACT.Ln, bias=1.0).then_inc(*R.made("zlog_ready"))
                act.wait_ge(*R.next("cum_ready"))
                fn(eb[:], b.rstd[:], ACT.Exp, scale=1.0 / 16).then_inc(*R.made("expb_ready"))
                fn(enb[:], b.rstd[:], ACT.Exp, scale=-1.0 / 16).then_inc(*R.made("expb_ready"))
                act.wait_ge(*R.next("gaps_ready"))
                fn(z[:], z[:], ACT.Exp, scale=1.0 / 16).then_inc(*R.made("kd_exp"))
        act.wait_ge(*R.next("norm_input"))
        for tt in range(t // P):
            for h in range(GH):
                last = fn(b.part[0][:, 0:DV], b.go[:, tt, h * DV:(h + 1) * DV], ACT.Square,
                          accum_out=b.small[:, 4 * tt + h:4 * tt + h + 1])
                last.then_inc(*R.made("act_step"))
                act.wait_ge(*R.own("act_step"))
        n = 4 * (t // P)
        fn(b.small[:, 16:16 + n], b.small[:, 0:n], ACT.Ln, bias=b.small[:, 63:64], scale=1.0 / DV) \
            .then_inc(*R.made("act_step"))
        act.wait_ge(*R.own("act_step"))
        fn(b.small[:, 32:32 + n], b.small[:, 16:16 + n], ACT.Exp, scale=-0.5).then_inc(*R.made("osq_ready"))
        stage(4, wide_gates(t))
        for c in range(KC):
            part(b.xn[0][:, c, 0:t], src=b.gqk[:, c, 0:t], by_chunk=R.value("evac") - KC + 1 + c)
        stage(4, taken_squares(t))

    def conv():
        def glu(k):
            chunk()
            chunk()
            room()
            bg = VEC["pw1_b"][0] + KC + k
            fn(b.sg[0][:], bank_of(1)[:], ACT.Sigmoid, bias=b.vec[:, bg:bg + 1]).then_inc(*R.made("gate_ready"))
            act.wait_ge(R.sems["chunk_taken"], R.value("evac") - 1)
            for j in range(TAPS_BESIDE):
                tap = TAPS - TAPS_BESIDE + j
                if j != 5 and (j >= 4 or k):
                    act.wait_ge(*R.next("tap_summed"))
                w = VEC["dw_w"][0] + k * TAPS + tap
                fn(b.tap[(k * TAPS_BESIDE + j) % 4][:].rearrange("p (s t) -> p s t", s=2),
                   b.u[:, k, :, tap:tap + S], ACT.Copy, scale=b.vec[:, w:w + 1]).then_inc(*R.made("tap_product"))
        stage(8, glu)
        act.wait_ge(*R.next("mean_ready"))
        fn(b.nmean[:], bank[5][:], ACT.Copy, scale=1.0 / D).then_inc(*R.made("mean_taken"))
        squares(lambda c: b.dw[:, c, :], T2)
        rstd(T2, D)
        for c in range(KC):
            act.wait_ge(*R.next("ln_ready"))
            fn(b.sg[c % 2][:], b.dw[:, c, :], ACT.Sigmoid).then_inc(*R.made("gate_ready"))
            part(b.xn[0][:, c, :], width=T2)
        stage(4, taken_squares(T2))

    def attention():
        stage(7)
        act.wait_ge(*R.next("norm_input"))
        for c in range(12):
            fn(b.part[c % 2][:], b.aqk[:, c, :], ACT.Square).then_inc(*R.made("head_squares"))
            act.wait_ge(*R.next("heads_summed"))
            if c >= 2:
                act.wait_ge(*R.next("qn_ready"))
            fn(b.sg[c % 2][:], bank[4 + c % 2][:], ACT.Ln, bias=b.small[:, 63:64], scale=1.0 / HD) \
                .then_inc(*R.made("qstat_read"))
            act.wait_ge(*R.own("qstat_read"))
            fn(b.sg[c % 2][:], b.sg[c % 2][:], ACT.Exp, scale=-0.5).then_inc(*R.made("rstd_ready"))

        steps = [(h, qt) for h in range(QH) for qt in range(4)]
        score_bank = (4, 5, 1)

        def exponent(n):
            nk = T2 if steps[n][1] < 2 else S
            act.wait_ge(*R.next("neg_max"))
            fn(b.prob[n % 3][:, 0:nk], bank[score_bank[n % 3]][:, 0:nk], ACT.Exp,
               bias=b.small[:, 20 + n % 3:21 + n % 3], scale=HD ** -0.5,
               accum_out=b.small[:, 24 + n % 3:25 + n % 3]).then_inc(*R.made("exp_ready"))

        exponent(0)
        for n, (h, qt) in enumerate(steps):
            if n + 1 < len(steps):
                exponent(n + 1)
            nk = T2 if qt < 2 else S
            act.wait_ge(*R.next("recip_ready"))
            fn(b.prob[n % 3][:, 0:nk], b.prob[n % 3][:, 0:nk], ACT.Copy,
               scale=b.small[:, 28 + n % 3:29 + n % 3]).then_inc(*R.made("probs_ready"))
            if n % 8 == 1 and n > 1:
                part(b.xn[0][:, n // 8 - 1, :], width=T2)
        part(b.xn[0][:, KC - 1, :], width=T2)
        stage(4, taken_squares(T2))

    for i in range(LAYERS):
        t = S if i == LAYERS - 1 else T2
        if i == 0:
            norm(T2)
        else:
            rstd(T2, D)
        operand_parts(T2)
        if i % 3 == 0:
            gla(i, t)
        elif i % 3 == 1:
            conv()
        else:
            attention()
        rstd(t, D)
        operand_parts(t)

        def piece(mod=None, squared=False, last=False):
            def hidden(k):
                for c in range(2):
                    chunk()
                    room()
                    fn(b.sg[c][:, 0:t], bank_of(c)[:, 0:t], ACT.Relu).then_inc(*R.made("gate_ready"))
                for c in range(2):
                    n = R.value("evac") + (c - 1)
                    part(b.hid[0][:, 2 * k + c, 0:t], width=t, by_chunk=n)
            stage(4, hidden, mod=mod)
            stage(4, taken_squares(T2) if squared else None, last=last, mod=mod)

        per = {"hl_free": 16, "evac": 16, "m hi_ready": 8, "m gate_ready": 8, "m part_hi": 8}
        for j in range(RAW):
            per[f"w raw_loaded{j}"] = 16 * 2
        if i < LAYERS - 1:
            per.update({"w mod_loaded0": 64, "w mod_loaded1": 64, "w product_summed": 56, "m product_ready": 64})
        with R.loop(3, per):
            piece(mod="mlp" if i < LAYERS - 1 else None)
        piece(squared=(i < LAYERS - 1), last=(i == LAYERS - 1))


def halves_and_mixes(nc, b, R, pool):
    tt = nc.gpsimd.tensor_tensor
    g = {"part": 0, "mods": 0}

    def part(hi, lo, src=None, width=None):
        pool.wait_ge(*R.next("part_hi"))
        src = b.part[g["part"] % 4][:, 0:width] if src is None else src
        tt(lo, src, hi, ALU.subtract).then_inc(*R.made("part_lo"))
        g["part"] += 1

    def sum_squares(t, n=KC):
        total = b.part[2][:, 0:t]
        for c in range(1, n):
            pool.wait_ge(*R.next("square_ready", 2 if c == 1 else 1))
            if c > 1:
                pool.wait_ge(*R.own("square_summed"))
            tt(total, b.part[c % 2][:, 0:t], b.part[0][:, 0:t] if c == 1 else total, ALU.add) \
                .then_inc(*R.made("square_summed"))

    def parts(n, pair, t):
        for c in range(n):
            part(pair[0][:, c, 0:t], pair[1][:, c, 0:t], width=t)

    def weigh(place, slot):
        if g["mods"] >= 2:
            pool.wait_ge(*R.next("mod_ready"))
        g["mods"] += 1
        acc, product = b.mods[place][slot][:, 1, :], b.modp[place]
        for k in range(1, KC):
            pool.wait_ge(*R.next("product_ready", 2 if k == 1 else 1))
            if k > 1:
                pool.wait_ge(*R.own("product_summed"))
            tt(acc, product[:, k % 4, :], product[:, 0, :] if k == 1 else acc, ALU.add) \
                .then_inc(*R.made("product_summed"))

    sum_squares(S)
    parts(KC, b.xn1, S)
    for k in range(12):
        weigh("qk", k % 2)
    parts(4, b.ao, S)
    for k in range(12):
        weigh("xbc", k % 2)
    for n in range(16):
        ct, gr = n // 8, n % 8 // 2
        pool.wait_ge(*R.next("decay_ready"))
        last = tt(b.gap[n % 2][:], b.gap[n % 2][:], b.cbm[:, gr:gr + 1, :].to_broadcast([P, 4, P]), ALU.mult)
        if ct:
            pool.wait_ge(*R.next("spread_exp"))
            last = tt(b.part[2 + n % 2][:].rearrange("p (h t) -> p h t", h=4),
                      b.part[n % 2][:].rearrange("p (h t) -> p h t", h=4),
                      b.xbc[:, 20 + gr:21 + gr, P:2 * P].to_broadcast([P, 4, P]), ALU.mult)
        last.then_inc(*R.made("mix_ready"))
    for gr in range(SSM_G):
        sum_squares(S, 4)
        for c in range(4 * gr, 4 * gr + 4):
            part(b.big[0][:, c, 0:S], b.big[1][:, c, 0:S], width=S)
    parts(KC, b.big, S)
    sum_squares(S)
    parts(KC, b.xn1, S)
    for n in (8, 8, 6):
        parts(n, b.big, S)
    sum_squares(S)
    for i in range(LAYERS):
        t = S if i == LAYERS - 1 else T2
        sum_squares(T2)
        parts(KC, b.xn, T2)
        if i % 3 == 0:
            for c in range(KC):
                part(b.xn[0][:, c, 0:t], b.xn[1][:, c, 0:t], src=b.gqk[:, c, 0:t])
        elif i % 3 == 1:
            for k in range(KC):
                for j in range(1, TAPS_BESIDE):
                    n = k * TAPS_BESIDE + j
                    pool.wait_ge(*R.next("tap_product", 2 if j == 1 else 1))
                    if j > 1:
                        pool.wait_ge(*R.own("tap_summed"))
                    elif k:
                        pool.wait_ge(*R.own("dw_ready"))
                    tt(b.taps[:], b.tap[n % 4][:], b.tap[(n - 1) % 4][:] if j == 1 else b.taps[:], ALU.add) \
                        .then_inc(*R.made("tap_summed"))
                pool.wait_ge(*R.next("dw_partial"))
                pool.wait_ge(*R.own("tap_summed"))
                tt(b.dw[:, k, :], b.dw[:, k, :], b.taps[:], ALU.add).then_inc(*R.made("dw_ready"))
                if k:
                    pool.wait_ge(*R.own("dw_ready"))
                    if k > 1:
                        pool.wait_ge(*R.own("mean_summed"))
                    tt(b.nmean[:], b.dw[:, k, :], b.dw[:, 0, :] if k == 1 else b.nmean[:], ALU.add) \
                        .then_inc(*R.made("mean_summed"))
            sum_squares(T2)
            parts(KC, b.xn, T2)
        else:
            parts(KC, b.xn, T2)
        sum_squares(t)
        parts(KC, b.xn, t)
        per = {"w part_hi": KC, "m part_lo": KC}
        if i < LAYERS - 1:
            per.update({"w product_ready": 64, "w mod_ready": 8, "m product_summed": 56})
        with R.loop(3, per):
            for k in range(4):
                if i < LAYERS - 1:
                    weigh("mlp", k % 2)
                for c in range(2 * k, 2 * k + 2):
                    part(b.hid[0][:, c, 0:t], b.hid[1][:, c, 0:t], width=t)
            for k in range(4 if i < LAYERS - 1 else 0):
                weigh("mlp", k % 2)
        parts(KC, b.hid, t)


def vectors(nc, b, R, dve, at):
    ttn, sct, stt, cp = nc.vector.tensor_tensor, nc.vector.tensor_scalar, nc.vector.scalar_tensor_tensor, \
        nc.vector.tensor_copy
    g = {"unit": 0, "taken": 0, "part": 0, "mods": 0}
    bank = b.bank

    def vec(name, c=0, w=1):
        o = VEC[name][0]
        if isinstance(c, int):
            return b.vec[:, o + c:o + c + w]
        return b.vec[:, bass.ds(c + o, w)]

    def cst(name):
        return b.cst[:, CST[name][0]:CST[name][0] + CST[name][1]]

    def at_chunk(buf, c):
        if isinstance(c, int):
            return buf[:, c, :]
        return buf[:, bass.ds(c, 1), :].rearrange("p a t -> p (a t)")

    def step(ins):
        ins.then_inc(*R.made("dve_step"))
        dve.wait_ge(*R.own("dve_step"))

    def split():
        u = g["unit"]
        dve.wait_ge(*R.next("hi_ready"))
        ttn(b.wlo[u % SPL][:], b.raw[u % RAW][:], b.whi[u % SPL][:], ALU.subtract).then_inc(*R.made("lo_ready"))
        g["unit"] += 1

    def part(width):
        if g["part"] >= 4:
            dve.wait_ge(*R.next("part_lo"))
        g["part"] += 1
        return b.part[(g["part"] - 1) % 4][:, 0:width]

    def in_place():
        R.n["w part_lo"] += 1
        g["part"] += 1

    def chunk():
        dve.wait_ge(*R.next("chunk_ready"))

    def bank_of(c):
        return bank[2 * (g["taken"] % SPL) + c]

    def stage(n, body, mod=None, last=False):
        def one(k, j):
            if not (last and isinstance(k, int) and k == n - 1):
                split()
            if mod is not None:
                weigh(mod[2], j % 2)
            body(k)
            if mod is not None:
                dve.wait_ge(*R.next("mod_ready"))
                col = k * 4 + mod[1] * 2
                dst = b.mod[mod[0] % 2]
                dst = dst[:, col:col + 4] if isinstance(col, int) else dst[:, bass.ds(col, 4)]
                cp(dst, bank[7][:, 0:4]).then_inc(*R.made("mod_taken"))
            g["taken"] += 1
        R.groups(n, one)

    def take_to(buf, t, off=0, reverse=False, scale=None):
        def body(k):
            for c in range(2):
                chunk()
                dst, src = at_chunk(buf, k * 2 + (off + c)), bank_of(c)[:, 0:t]
                if reverse:
                    dst = dst.rearrange("p (a t) -> p a t", t=P)
                    src = src.rearrange("p (a t) -> p a t", t=P)[:, :, ::-1]
                if scale is None:
                    cp(dst, src).then_inc(*R.made("chunk_taken"))
                else:
                    sct(dst, src, scale, None, ALU.mult).then_inc(*R.made("chunk_taken"))
        return body

    def x_ready():
        cp(b.small[:, 62:63], b.small[:, 63:64]).then_inc(*R.made("norm_input"))

    def settle():
        step(cp(b.small[:, 61:62], b.small[:, 63:64]))

    def norm1(name, dst=None):
        if name == "norm1":
            x_ready()
        dve.wait_ge(*R.next("rstd_ready"))
        for c in range(KC):
            if dst is None:
                stt(part(S), b.x[:, c, 0:S], vec(name, c), b.rstd[:, 0:S], ALU.mult, ALU.mult) \
                    .then_inc(*R.made("part_ready"))
            else:
                stt(dst[:, c, 0:S], b.x[:, c, 0:S], vec(name, c), b.rstd[:, 0:S], ALU.mult, ALU.mult) \
                    .then_inc(*R.made("dve_step"))

    def weigh(place, slot):
        dve.wait_ge(*R.next(f"mod_loaded{slot}", 16))
        if g["mods"] >= 2:
            dve.wait_ge(*R.next("mod_ready", 1, "sums_free"))
        g["mods"] += 1
        w, acc = b.modw[place][slot], b.mods[place][slot][:, 0, :]
        step(sct(acc, w[:, 0, :], b.cond[:, 0, 0:1], None, ALU.mult))
        for k in range(1, KC):
            ins = stt(acc, w[:, k, :], b.cond[:, k, 0:1], acc, ALU.mult, ALU.add)
            if k < KC - 1:
                step(ins)
            else:
                ins.then_inc(*R.made("weighted"))

    step(nc.vector.memset(b.small[:], EPS))
    dve.wait_ge(R.sems["params_loaded"], 64)
    dve.wait_ge(*R.next("gate_ready"))
    ttn(b.cond[:].rearrange("p k s -> p (k s)"), vec("c", 0, 16), b.small[:, 0:16], ALU.mult) \
        .then_inc(*R.made("cond_ready"))
    split()
    dve.wait_ge(*R.next("rel_rows"))
    for gr in range(NG):
        last = ttn(b.reltab[:, gr, :], bank[5 + gr][0:GROUP_HEADS, 0:384],
                   b.rel[0:GROUP_HEADS, 384 * (gr + 1):384 * (gr + 2)], ALU.add)
    last.then_inc(*R.made("rel_table"))
    dve.wait_ge(R.sems["x_loaded"], 16)
    norm1("norm1")
    stage(6, take_to(b.qk, S, reverse=True), mod=(0, 0, "qk"))
    stage(6, take_to(b.qk, S, off=12), mod=(0, 12, "qk"))

    def take_v(k):
        for c in range(2):
            chunk()
            dst = b.v[:, c, k * UC:(k + 1) * UC] if isinstance(k, int) else b.v[:, c, bass.ds(k * UC, UC)]
            cp(dst, bank_of(c)[:, 0:UC]).then_inc(*R.made("chunk_taken"))
    stage(6, take_v)

    def front(n):
        h, qt = n // 2, n % 2
        nk = P * (qt + 1)
        L = b.logits[n % 2]
        dve.wait_ge(*R.next("scores_ready"))
        if qt == 0:
            dve.wait_ge(*R.next(f"rel_loaded{h % 2}", 16))
        o = P - P * qt
        two = bank[4 + 2 * (n % 2)][:].rearrange("p (g k) -> p g k", g=2)
        stt(L[:, 0:2, 0:nk], two[:, :, 0:nk], HD ** -0.5, b.bias[h % 2][:, 0:2, o:o + nk], ALU.mult, ALU.add) \
            .then_inc(*R.made("dve_step"))
        stt(L[:, 2, 0:nk], bank[5 + 2 * (n % 2)][:, 0:nk], HD ** -0.5, b.bias[h % 2][:, 2, o:o + nk],
            ALU.mult, ALU.add).then_inc(*R.made("logits_taken"))
        dve.wait_ge(*R.own("logits_taken"))
        step(nc.vector.tensor_reduce(b.small[:, 16 + n % 2:17 + n % 2], L[:, :, 0:nk], AX.XY, ALU.max))
        sct(b.small[:, 20 + n % 2:21 + n % 2], b.small[:, 16 + n % 2:17 + n % 2], -1.0, None, ALU.mult) \
            .then_inc(*R.made("neg_max"))

    def pair(c):
        dve.wait_ge(*R.next("values_ready", 4))
        cp(part(S).rearrange("p (a t) -> p a t", t=P),
           bank[2 + c % 2][:, 0:S].rearrange("p (a t) -> p a t", t=P)[:, :, ::-1]).then_inc(*R.made("part_ready"))

    front(0)
    for n in range(16):
        kt = n % 2 + 1
        dve.wait_ge(*R.next("exp_ready"))
        nc.vector.reciprocal(b.small[:, 28 + n % 2:29 + n % 2], b.small[:, 24 + n % 2:25 + n % 2]) \
            .then_inc(*R.made("recip_ready"))
        if n < 15:
            front(n + 1)
        dve.wait_ge(*R.next("turned_ready"))
        n0 = min(4, NG * kt)
        turned = b.turned[n % 2]
        last = cp(turned[:, 0:n0, :], bank[0][:, 0:n0 * P].rearrange("p (a t) -> p a t", t=P))
        if kt == 2:
            last = cp(turned[:, 4:6, :], bank[1][:, 0:2 * P].rearrange("p (a t) -> p a t", t=P))
        last.then_inc(*R.made("turned_taken"))
        if n % 4 == 0 and n:
            pair(n // 4 - 1)
    pair(3)
    stage(4, take_to(b.attn_out, S))

    for c in range(2):
        step(nc.vector.memset(b.cin[c][:, 0:3], 0.0))

    def conv4(k):
        for c in range(2):
            dve.wait_ge(*R.next("cin_ready"))
            R.n["w chunk_ready"] += 1
            ch = k * 2 + c
            if c == 0:
                dve.wait_ge(*R.own("dve_step"))
            sct(b.cacc[c][:], b.cin[c][:, 0:S], vec("conv_w", ch * 4), vec("conv_b", ch), ALU.mult, ALU.add) \
                .then_inc(*R.made("chunk_taken"))
            dve.wait_ge(*R.own("chunk_taken"))
            for tap in (1, 2, 3):
                ins = stt(b.cacc[c][:], b.cin[c][:, tap:tap + S], vec("conv_w", ch * 4 + tap), b.cacc[c][:],
                          ALU.mult, ALU.add)
                if tap < 3:
                    step(ins)
                else:
                    ins.then_inc(*R.made("conv_ready"))
        for c in range(2):
            dve.wait_ge(*R.next("gate_ready"))
            ttn(at_chunk(b.xbc, k * 2 + c), b.cacc[c][:], b.sg[c][:, 0:S], ALU.mult).then_inc(*R.made("dve_step"))
    stage(12, conv4, mod=(0, 24, "xbc"))

    def take_dt(k):
        for c in range(2):
            chunk()
            ttn(b.dt[:, 0, c, :], bank_of(c)[:, 0:SSM_HEADS], vec("dt_b", 0, SSM_HEADS), ALU.add) \
                .then_inc(*R.made("chunk_taken"))
    stage(1, take_dt)
    dve.wait_ge(*R.own("chunk_taken"))
    lin, ab = b.dt[:, 0, :, :], b.dt[:, 1, :, :]
    stt(ab, lin, -1.0, lin, ALU.mult, ALU.max).then_inc(*R.made("dt_abs"))
    dve.wait_ge(*R.next("dt_log"))
    step(stt(b.dt[:, 3, :, :], lin, 0.0, ab, ALU.max, ALU.add))
    for ct in range(2):
        last = stt(b.dt[:, 2, ct, :], b.dt[:, 3, ct, :], -1.0, b.dt[:, 7, 0, :], ALU.mult, ALU.mult)
    last.then_inc(*R.made("dta_ready"))
    for ct in range(2):
        for gr in range(SSM_G):
            dve.wait_ge(*R.next("xs_turned"))
            ttn(b.xdt[:, ct, gr * 512:(gr + 1) * 512].rearrange("p (h d) -> p h d", d=HD),
                bank[4 + gr % 2][:].rearrange("p (h d) -> p h d", d=HD),
                b.dt[:, 3, ct, gr * 8:gr * 8 + 8].unsqueeze(2).to_broadcast([P, 8, HD]), ALU.mult) \
                .then_inc(*R.made("xs_taken"))
    dve.wait_ge(*R.next("sums_ready"))
    for s in range(2):
        last = cp(b.dt[:, 4 + s, :, :], bank[6][:, 0:128].rearrange("p (c s h) -> p s c h", c=2, s=2)[:, s, :, :])
        step(last)
    ttn(b.dt[:, 6, 0, :], b.dt[:, 5, 0, :], b.dt[:, 4, 0, :], ALU.subtract).then_inc(*R.made("toend_in"))
    dve.wait_ge(*R.next("b_turned"))
    cp(b.bt[:].rearrange("p g t -> p (g t)"), bank[7][:]).then_inc(*R.made("b_taken"))
    dve.wait_ge(*R.next("toend_exp"))
    dve.wait_ge(*R.own("xs_taken"))
    for gr in range(SSM_G):
        ttn(b.toend_x[:].rearrange("p (h d) -> p h d", d=HD),
            b.xdt[:, 0, gr * 512:(gr + 1) * 512].rearrange("p (h d) -> p h d", d=HD),
            b.dt[:, 6, 0, gr * 8:gr * 8 + 8].unsqueeze(2).to_broadcast([P, 8, HD]), ALU.mult) \
            .then_inc(*R.made("toend_ready"))
        dve.wait_ge(*R.next("state_ready"))
        cp(b.state1[:, gr, :], bank[4 + gr % 2][:]).then_inc(*R.made("state_taken"))

    def cb():
        dve.wait_ge(*R.next("cb_ready"))
        ttn(b.cbm[:], bank[4][:].rearrange("p (g t) -> p g t", g=4),
            cst("tri").unsqueeze(1).to_broadcast([P, 4, P]), ALU.mult).then_inc(*R.made("cb_taken"))

    def gap(n):
        ct, quad = n // 8, n % 8
        dve.wait_ge(*R.next("spread_ready"))
        for h in range(4):
            head = quad * 4 + h
            last = sct(b.gap[n % 2][:, h, :], bank[5 + n % 2][:, h * P:(h + 1) * P], b.dt[:, 4, ct, head:head + 1],
                       0.0, ALU.subtract, ALU.min)
        last.then_inc(*R.made("gap_ready"))

    cb()
    gap(0)
    for n in range(16):
        if n < 15 and n != 7:
            gap(n + 1)
        ct, quad = n // 8, n % 8
        dve.wait_ge(*R.next("y_ready"))
        for c in range(2):
            ch = quad * 2 + c
            last = stt(b.y[:, ch, ct * P:(ct + 1) * P], b.xbc[:, ch, ct * P:(ct + 1) * P], vec("dskip", ch),
                       bank[n % 2][:, c * P:(c + 1) * P], ALU.mult, ALU.add)
        last.then_inc(*R.made("y_taken"))
        if n == 7:
            cb()
            gap(8)

    dve.wait_ge(*R.own("y_taken"))

    def take_z(k):
        for c in range(2):
            chunk()
            dve.wait_ge(*R.next("gate_ready"))
            y = at_chunk(b.y, k * 2 + c)
            step(ttn(y, y, b.sg[c][:, 0:S], ALU.mult))
            ttn(y, bank_of(c)[:, 0:S], y, ALU.mult).then_inc(*R.made("chunk_taken"))
    stage(8, take_z)
    for gr in range(SSM_G):
        x_ready()
        dve.wait_ge(*R.next("rstd_ready"))
        for c in range(4):
            ch = 4 * gr + c
            stt(part(S), b.y[:, ch, :], vec("ssm_norm", ch), b.rstd[:, 0:S], ALU.mult, ALU.mult) \
                .then_inc(*R.made("part_ready"))

    def take_ssm(k):
        for c in range(2):
            chunk()
            o = b.ssm_out[:, 2 * (k % 4) + c, :]
            if k < 4:
                cp(o, bank_of(c)[:, 0:S]).then_inc(*R.made("chunk_taken"))
            else:
                ttn(o, bank_of(c)[:, 0:S], o, ALU.add).then_inc(*R.made("chunk_taken"))
    stage(8, take_ssm)
    dve.wait_ge(*R.own("chunk_taken"))

    def take_gates(k):
        for c in range(2):
            R.n["w chunk_ready"] += 1
            dve.wait_ge(*R.next("gate_ready"))
            ch = 2 * (k % 4) + c
            o = b.attn_out[:, ch, :] if k < 4 else b.ssm_out[:, ch, :]
            ttn(o, o, b.sg[c][:, 0:S], ALU.mult).then_inc(*R.made("chunk_taken"))
            if k >= 4:
                dve.wait_ge(*R.own("chunk_taken"))
                ttn(part(S), o, b.attn_out[:, ch, :], ALU.add).then_inc(*R.made("part_ready"))
    stage(8, take_gates)

    def add_to_x(k):
        for c in range(2):
            chunk()
            o = b.x[:, 2 * k + c, 0:S]
            ttn(o, bank_of(c)[:, 0:S], o, ALU.add).then_inc(*R.made("chunk_taken"))
    stage(4, add_to_x)
    norm1("norm2")
    for n in (8, 8, 6):
        def ffn(k):
            chunk()
            dve.wait_ge(*R.next("gate_ready"))
            ttn(b.sg[1][:, 0:S], bank_of(0)[:, 0:S], b.sg[0][:, 0:S], ALU.mult).then_inc(*R.made("chunk_taken"))
            dve.wait_ge(*R.own("chunk_taken"))
            p = part(S)
            chunk()
            ttn(p, bank_of(1)[:, 0:S], b.sg[1][:, 0:S], ALU.mult).then_inc(*R.made("chunk_taken"))
        stage(n, ffn)
        stage(4, add_to_x)
    norm1("final", b.x)
    settle()

    def streams(t):
        return [(s, s * S) for s in range(t // S)]

    def mcol(i, v, c, s):
        o = 2 * (v * KC + c) + s
        return b.mod[i % 2][:, o:o + 1]

    def norm_mod(i, which, t):
        if i == 0 and which == 0:
            x_ready()
        if which == 0:
            m = b.mod[i % 2][:].rearrange("p (m s) -> p m s", s=2)
            step(ttn(m, m, vec("b_mod", i * MODC, MODC).unsqueeze(2).to_broadcast([P, MODC, 2]), ALU.add))
            for n, name in enumerate(("g_mix", "g_mlp")):
                sc = m[:, (1 + 3 * n) * KC:(2 + 3 * n) * KC, :]
                step(stt(b.modg[:].rearrange("p (n c s) -> p n c s", n=2, s=2)[:, n, :, :], sc, 1.0,
                         vec(name, i * KC, KC).unsqueeze(2).to_broadcast([P, KC, 2]), ALU.add, ALU.mult))
        dve.wait_ge(*R.next("rstd_ready"))
        for c in range(KC):
            p = part(t)
            step(ttn(p, b.x[:, c, 0:t], b.rstd[:, 0:t], ALU.mult))
            for s, o in streams(t):
                gcol = 2 * (which * KC + c) + s
                last = sct(p[:, o:o + S], p[:, o:o + S], b.modg[:, gcol:gcol + 1],
                           mcol(i, 3 * which, c, s), ALU.mult, ALU.add)
            last.then_inc(*R.made("part_ready"))

    def add_gated(i, v, t):
        def body(k):
            for c in range(2):
                chunk()
                for s, o in streams(t):
                    ch = 2 * k + c
                    last = stt(b.x[:, ch, o:o + S], bank_of(c)[:, o:o + S], mcol(i, v, ch, s),
                               b.x[:, ch, o:o + S], ALU.mult, ALU.add)
                last.then_inc(*R.made("chunk_taken"))
        return body

    def gla(i, t):
        last_layer = i == LAYERS - 1
        gi = i // 3

        def qk(k):
            for c in range(2):
                chunk()
                ch = 2 * k + c
                scale = (D // 2 // GH) ** -0.5 if k < 2 else 1.0
                sct(b.gqk[:, ch, :], bank_of(c)[:], scale, None, ALU.mult).then_inc(*R.made("chunk_taken"))
        stage(4, qk)

        def vtake(k):
            for c in range(2):
                chunk()
                cp(b.gv[:, 2 * c:2 * c + 2, k * UC:(k + 1) * UC], bank_of(c)[:].rearrange("p (a n) -> p a n", a=2)) \
                    .then_inc(*R.made("chunk_taken"))
        stage(4, vtake)

        def g1take(k):
            for c in range(2):
                chunk()
                cp(b.g1[32 * c:32 * c + 16, :], bank_of(c)[32 * c:32 * c + 16, :]).then_inc(*R.made("chunk_taken"))
        stage(1, g1take)
        dve.wait_ge(*R.own("chunk_taken"))
        z, ab, eb, enb = b.part
        cum = b.rstd

        def log_gate(h, d):
            dve.wait_ge(*R.next("zg_ready"))
            step(sct(z[:], bank[4][:], vec("gla_b", (gi * 2 + d) * GH + h), None, ALU.add))
            stt(ab[:], z[:], -1.0, z[:], ALU.mult, ALU.max).then_inc(*R.made("zabs_ready"))

        def sum_gates(d):
            dve.wait_ge(*R.next("zlog_ready"))
            step(stt(z[:], z[:], 0.0, ab[:], ALU.min, ALU.subtract))
            way = lambda a: a[:] if d == 0 else a[:, ::-1]
            nc.vector.tensor_tensor_scan(way(cum), cst("restart"), way(z), 0.0, ALU.mult, ALU.add) \
                .then_inc(*R.made("cum_ready"))
            dve.wait_ge(*R.own("cum_ready"))
            c3 = cum[:].rearrange("p (n t) -> p n t", t=GCH)
            ttn(z[:].rearrange("p (n t) -> p n t", t=GCH), c3[:, :, END[d]:END[d] + 1].to_broadcast([P, 8, GCH]),
                c3, ALU.subtract).then_inc(*R.made("gaps_ready"))

        def decay(h, d):
            q, k = b.gqk[:, h, :], b.gqk[:, GH + h, :]
            dve.wait_ge(*R.next("expb_ready"))
            ttn(b.qb[h % 2][d][:], q, eb[:], ALU.mult).then_inc(*R.made("dve_step"))
            cp(b.ends[h % 2][d][:].unsqueeze(2),
               eb[:].rearrange("p (n t) -> p n t", t=GCH)[:, :, END[d]:END[d] + 1]).then_inc(*R.made("dve_step"))
            dve.wait_ge(*R.next("expb_ready"))
            ttn(enb[:], k, enb[:], ALU.mult).then_inc(*R.made("dve_step"))
            dve.wait_ge(*R.next("kd_exp"))
            ttn(ab[:], k, z[:], ALU.mult).then_inc(*R.made("kd_ready"))

        def take_weights(h, d):
            dve.wait_ge(*R.next("kdt_ready"))
            cp(b.kdt[h % 2][d][:, :, :], bank[5][:].rearrange("p (a t) -> p a t", t=P)).then_inc(*R.made("dve_step"))
            dve.wait_ge(*R.next("att_ready"))
            ttn(b.att[h % 2][d][:, :, :], bank[6][:, 0:4 * GCH].rearrange("p (a t) -> p a t", t=GCH),
                cst("causal" if d == 0 else "anticausal").unsqueeze(1).to_broadcast([P, 4, GCH]), ALU.mult) \
                .then_inc(*R.made("att_taken"))

        def update(h, s, d):
            n = [[4, 5, 6, 7, 0, 1, 2, 3], [7, 6, 5, 4, 3, 2, 1, 0]][d][s]
            dve.wait_ge(*R.next("s_ready"))
            new, old = b.gs2[d][(s + 1) % 2], b.gs2[d][s % 2]
            if s == 0:
                cp(new, bank[d][:, 0:DV]).then_inc(*R.made("s_taken"))
            else:
                dve.wait_ge(R.sems["s_taken"], R.n["m s_taken"] - 1)
                stt(new, old, b.ends[h % 2][d][:, n:n + 1], bank[d][:, 0:DV], ALU.mult, ALU.add) \
                    .then_inc(*R.made("s_taken"))

        def take_o(h, s):
            for d in range(2):
                dve.wait_ge(*R.next("o_ready"))
                st = 0 if s == 7 else 2
                dst = b.go[:, st:st + 2, h * DV:(h + 1) * DV]
                src = bank[2 + d][:].rearrange("p (a n) -> p a n", a=2)
                if d == 0:
                    cp(dst, src).then_inc(*R.made("o_taken"))
                else:
                    dve.wait_ge(*R.own("o_taken"))
                    ttn(dst, src, dst, ALU.add).then_inc(*R.made("o_taken"))

        END = (GCH - 1, 0)
        for d in range(2):
            log_gate(0, d)
            sum_gates(d)
            decay(0, d)
            take_weights(0, d)
        for h in range(GH):
            ahead = h + 1 < GH
            for s in range(7):
                for d in range(2):
                    update(h, s, d)
                if s == 3 and not last_layer:
                    take_o(h, 3)
                if not ahead:
                    continue
                if s == 0:
                    log_gate(h + 1, 0)
                elif s == 1:
                    sum_gates(0)
                elif s == 2:
                    decay(h + 1, 0)
                elif s == 3:
                    take_weights(h + 1, 0)
                    log_gate(h + 1, 1)
                elif s == 4:
                    sum_gates(1)
                elif s == 5:
                    decay(h + 1, 1)
                else:
                    take_weights(h + 1, 1)
            take_o(h, 7)
        x_ready()
        dve.wait_ge(*R.next("osq_ready"))
        gh = VEC["g_head"][0] + gi * DV
        for tt in range(t // P):
            for h in range(GH):
                o = b.go[:, tt, h * DV:(h + 1) * DV]
                col = 32 + 4 * tt + h
                last = stt(o, o, b.small[:, col:col + 1], b.vec[:, gh:gh + DV], ALU.mult, ALU.mult)
        last.then_inc(*R.made("onorm_ready"))
        for fc in range(KC):
            dve.wait_ge(*R.next("ot_ready"))
            cp(b.gqk[:, fc, 0:t], bank[5 + fc % 2][:, 0:t]).then_inc(*R.made("ot_taken"))
        dve.wait_ge(*R.own("ot_taken"))

        def take_r(k):
            for c in range(2):
                chunk()
                dve.wait_ge(*R.next("gate_ready"))
                in_place()
                o = b.gqk[:, 2 * k + c, 0:t]
                step(ttn(o, o, b.sg[c][:, 0:t], ALU.mult))
                ttn(o, bank_of(c)[:, 0:t], o, ALU.mult).then_inc(*R.made("chunk_taken"))
        stage(4, take_r)
        stage(4, add_gated(i, 2, t))

    def conv(i):
        for c in range(KC):
            for o in (0, PADT + S):
                nc.vector.memset(b.u[:, c, :, o:o + PADT], 0.0).then_inc(*R.made("dve_step"))
        dve.wait_ge(*R.own("dve_step"))

        def glu(k):
            chunk()
            dve.wait_ge(*R.next("gate_ready"))
            u = b.u[:, k, :, PADT:PADT + S]
            stt(u, bank_of(0)[:].rearrange("p (s t) -> p s t", s=2), vec("pw1_b", k),
                b.sg[0][:].rearrange("p (s t) -> p s t", s=2), ALU.add, ALU.mult).then_inc(*R.made("chunk_taken"))
            chunk()
            dve.wait_ge(*R.own("chunk_taken"))
            acc = b.dw[:, k, :].rearrange("p (s t) -> p s t", s=2)
            w = lambda tap: vec("dw_w", k * TAPS + tap)
            sct(acc, b.u[:, k, :, 0:S], w(0), vec("dw_b", k), ALU.mult, ALU.add).then_inc(*R.made("chunk_taken"))
            dve.wait_ge(*R.own("chunk_taken"))
            for tap in range(1, TAPS - TAPS_BESIDE):
                ins = stt(acc, b.u[:, k, :, tap:tap + S], w(tap), acc, ALU.mult, ALU.add)
                if tap < TAPS - TAPS_BESIDE - 1:
                    step(ins)
                else:
                    ins.then_inc(*R.made("dw_partial"))
        stage(8, glu)
        dve.wait_ge(*R.next("mean_taken"))
        for c in range(KC):
            ttn(b.dw[:, c, :], b.dw[:, c, :], b.nmean[:], ALU.subtract).then_inc(*R.made("dve_step"))
        x_ready()
        dve.wait_ge(*R.next("rstd_ready"))
        for c in range(KC):
            step(ttn(b.dw[:, c, :], b.dw[:, c, :], b.rstd[:], ALU.mult))
            sct(b.dw[:, c, :], b.dw[:, c, :], vec("ln_g", c), vec("ln_b", c), ALU.mult, ALU.add) \
                .then_inc(*R.made("ln_ready"))
            if c:
                silu(c - 1)
        silu(KC - 1)

        def take(k):
            for c in range(2):
                chunk()
                ch = 2 * k + c
                step(sct(b.sg[c][:], bank_of(c)[:], vec("pw2_b", ch), None, ALU.add))
                for s, o in streams(T2):
                    last = stt(b.x[:, ch, o:o + S], b.sg[c][:, o:o + S], mcol(i, 2, ch, s),
                               b.x[:, ch, o:o + S], ALU.mult, ALU.add)
                last.then_inc(*R.made("chunk_taken"))
        stage(4, take)

    def silu(c):
        dve.wait_ge(*R.next("gate_ready"))
        ttn(part(T2), b.dw[:, c, :], b.sg[c % 2][:], ALU.mult).then_inc(*R.made("part_ready"))

    def attention(i):
        stage(6, take_to(b.aqk, T2))

        def vtake(k):
            for c in range(2):
                chunk()
                cp(b.av[:, 2 * c:2 * c + 2, :], bank_of(c)[:].rearrange("p (a n) -> p a n", a=2)) \
                    .then_inc(*R.made("chunk_taken"))
        stage(1, vtake)
        x_ready()
        dve.wait_ge(R.sems["rope_loaded"], 16)
        cos, sin = b.rope[:, P:P + S], b.rope[:, P + S:P + 2 * S]
        for c in range(12):
            dve.wait_ge(*R.next("rstd_ready"))
            stt(b.aqk[:, c, :], b.aqk[:, c, :], vec("g_q" if c < 8 else "g_k"), b.sg[c % 2][:], ALU.mult,
                ALU.mult).then_inc(*R.made("qn_ready"))
            dve.wait_ge(*R.next("rot_ready"))
            ttn(b.part[2][:, 0:S], bank[6 + c % 2][:, 0:S], sin, ALU.mult).then_inc(*R.made("dve_step"))
            step(ttn(b.part[2][:, S:T2], b.aqk[:, c, 0:S], cos, ALU.mult))
            ttn(b.aqk[:, c, 0:S], b.part[2][:, 0:S], b.part[2][:, S:T2], ALU.add).then_inc(*R.made("rot_taken"))

        steps = [(h, qt) for h in range(QH) for qt in range(4)]

        score_bank, turned_bank = (4, 5, 1), (6, 7)

        def front(n):
            nk = T2 if steps[n][1] < 2 else S
            dve.wait_ge(*R.next("scores_ready"))
            m = b.small[:, 16 + n % 3:17 + n % 3]
            step(nc.vector.tensor_reduce(m, bank[score_bank[n % 3]][:, 0:nk], AX.X, ALU.max))
            sct(b.small[:, 20 + n % 3:21 + n % 3], m, -(HD ** -0.5), None, ALU.mult).then_inc(*R.made("neg_max"))

        def inverse(n):
            dve.wait_ge(*R.next("exp_ready"))
            nc.vector.reciprocal(b.small[:, 28 + n % 3:29 + n % 3], b.small[:, 24 + n % 3:25 + n % 3]) \
                .then_inc(*R.made("recip_ready"))

        def pair(c):
            dve.wait_ge(*R.next("values_ready", 8))
            cp(part(T2), bank[2 + c % 2][:]).then_inc(*R.made("part_ready"))

        front(0)
        front(1)
        inverse(0)
        for n, (h, qt) in enumerate(steps):
            if n + 1 < len(steps):
                inverse(n + 1)
            if n + 2 < len(steps):
                front(n + 2)
            nt = 4 if qt < 2 else 2
            dve.wait_ge(*R.next("turned_ready"))
            cp(b.pt[n % 2][:, 0:nt, :], bank[turned_bank[n % 2]][:, 0:nt * P].rearrange("p (a t) -> p a t", t=P)) \
                .then_inc(*R.made("turned_taken"))
            if n % 8 == 0 and n:
                pair(n // 8 - 1)
        pair(KC - 1)
        stage(4, add_gated(i, 2, T2))

    for i in range(LAYERS):
        t = S if i == LAYERS - 1 else T2
        norm_mod(i, 0, T2)
        if i % 3 == 0:
            gla(i, t)
        elif i % 3 == 1:
            conv(i)
        else:
            attention(i)
        norm_mod(i, 1, t)
        mixed = i < LAYERS - 1

        def piece(mod0, last=False):
            def hidden(k):
                for c in range(2):
                    chunk()
                    dve.wait_ge(*R.next("gate_ready"))
                    stt(part(t), bank_of(c)[:, 0:t], 0.0, b.sg[c][:, 0:t], ALU.max, ALU.mult) \
                        .then_inc(*R.made("chunk_taken"))
            stage(4, hidden, mod=None if mod0 is None else (i + 1, mod0, "mlp"))
            stage(4, add_gated(i, 5, t), mod=None if mod0 is None else (i + 1, mod0 + 8, "mlp"), last=last)

        per = {"w hi_ready": 8, "m lo_ready": 8, "w chunk_ready": 16, "m chunk_taken": 16, "w gate_ready": 8,
               "w part_lo": 8}
        if mixed:
            per.update({"w mod_ready": 8, "m mod_taken": 8, "w mod_loaded0": 64, "w mod_loaded1": 64,
                        "sums_free": 8, "m dve_step": 56, "m weighted": 8})
        with R.loop(3, per) as p:
            piece(p * 16 if mixed else None)
        piece(None, last=not mixed)
    cp(b.small[:, 60:61], b.small[:, 63:64]).then_inc(*R.made("result_ready"))


def program(nc, x, vec, cst, rel, relb, wall, wmod, wg2, rope, out):
    plan = unit_plan()
    at = {"units": len(plan)}
    for n, (what, k) in enumerate(plan):
        if k == 0:
            at[what] = n
    reltab = nc.dram_tensor("relative_offsets", [GROUP_HEADS, NG, 384], F32, kind="Internal").ap()
    dram = {"x": x, "vec": vec, "cst": cst, "rel": rel, "relb": relb, "wall": wall, "wmod": wmod, "wg2": wg2, "rope": rope,
            "out": out, "reltab": reltab, "at": at}
    with ExitStack() as ctx:
        b = place(nc, ctx)
        sems = {n: ctx.enter_context(nc.semaphore(n)) for n in SEMS}
        block = ctx.enter_context(nc.Block())

        @block.sync
        def _(sp):
            loads(nc, b, dram, Role(nc.sync, sems), sp)

        @block.tensor
        def _(pe):
            products(nc, b, Role(nc.tensor, sems), pe, at)

        @block.scalar
        def _(act):
            splits_and_functions(nc, b, Role(nc.scalar, sems), act, at)

        @block.gpsimd
        def _(pool):
            halves_and_mixes(nc, b, Role(nc.gpsimd, sems), pool)

        @block.vector
        def _(dve):
            vectors(nc, b, Role(nc.vector, sems), dve, at)


def lay_out(a):
    def feat(v):
        return np.ascontiguousarray(v.reshape(-1, P).T)

    def rows(v):
        return np.broadcast_to(v.reshape(1, -1), (P, v.size))

    def taps(w):
        t, n = w.shape
        return w.reshape(t, n // P, P).transpose(2, 1, 0).reshape(P, -1)

    cols = {
        "norm1": feat(a["norm1_w"]), "norm2": feat(a["norm2_w"]), "final": feat(a["final_norm_w"]),
        "conv_w": taps(a["conv_w"][0]), "conv_b": feat(a["conv_b"]),
        "dskip": feat(np.repeat(a["d_skip"][0], HD)), "ssm_norm": feat(a["ssm_norm_w"]),
        "b_mod": feat(a["b_mod_2"]), "g_mix": feat(a["g_norm_mix_2"]), "g_mlp": feat(a["g_norm_mlp_2"]),
        "gla_b": feat(a["gla_b_g_2"]), "pw1_b": feat(a["conv_b_pw1_2"]), "dw_w": taps(a["conv_w_dw_2"][0]),
        "dw_b": feat(a["conv_b_dw_2"]), "ln_g": feat(a["conv_ln_g_2"]), "ln_b": feat(a["conv_ln_b_2"]),
        "pw2_b": feat(a["conv_b_pw2_2"]), "g_q": np.tile(a["attn_g_q_2"][0], 2)[:, None],
        "g_k": np.tile(a["attn_g_k_2"][0], 2)[:, None],
        "c": np.stack([feat(a["c_2"]), feat(a["c_ctx_2"])], axis=2).reshape(P, -1),
        "dt_b": rows(a["dt_bias"]), "a_log": rows(a["a_log"]), "g_head": rows(a["gla_g_head_2"]),
    }
    vec = np.concatenate([cols[n] for n in VEC], axis=1)

    def unit(w):
        r, c = w.shape
        u = np.zeros((P, KC, UC), np.float32)
        u[:, :r // P, :c] = w.reshape(r // P, P, c).transpose(1, 0, 2)
        return u.reshape(P, UW)

    w_in = a["w_in"][0]
    o_k, o_v = AW, 2 * AW
    o_z = 3 * AW
    o_xbc = o_z + DI
    o_dt = o_xbc + XBC
    o_gate = o_dt + SSM_HEADS
    ffn_in, ffn_out = a["w_ffn_in"][0], a["w_ffn_out"][0]
    att = a["attn_w_qkv_2"][0]
    kv = D + 4 * HD

    def one(what, k):
        c = slice(k * UC, (k + 1) * UC)
        if isinstance(what, tuple):
            kind, i = what
            if kind == "ffn_in":
                f = (8 * i + k) * P
                return np.concatenate([ffn_in[:, f:f + P], ffn_in[:, FF + f:FF + f + P]], axis=1)
            if kind == "ffn_out":
                return ffn_out[i * D:min((i + 1) * D, FF), c]
            if kind == "gla_qk":
                return a["gla_w_in_2"][i][:, c]
            if kind == "gla_v":
                return a["gla_w_in_2"][i][:, D:][:, c]
            if kind == "gla_r":
                return a["gla_w_in_2"][i][:, 2 * D:][:, c]
            if kind == "gla_g1":
                w = np.zeros((D, UC), np.float32)
                w[:, 0:16] = a["gla_w_g1_2"][i, 0]
                w[:, P + 32:P + 48] = a["gla_w_g1_2"][i, 1]
                return w
            if kind == "gla_out":
                return a["gla_w_out_2"][i][:, c]
            (kind, layer), p = kind, i
            if kind == "mlp_in":
                return a["w_mlp_in_2"][layer][:, p * D:(p + 1) * D][:, c]
            return a["w_mlp_out_2"][layer][p * D:(p + 1) * D][:, c]
        if what == "q":
            return w_in[:, c]
        if what == "k":
            return w_in[:, o_k:][:, c]
        if what == "v":
            return w_in[:, o_v:][:, c]
        if what == "attn_branch":
            return a["w_attn_branch"][0][:, c]
        if what == "xbc":
            return w_in[:, o_xbc:][:, c]
        if what == "dt":
            return w_in[:, o_dt:o_gate]
        if what == "z":
            return w_in[:, o_z:][:, c]
        if what == "ssm":
            return a["w_ssm_branch"][0][(k // 4) * D:(k // 4 + 1) * D, (k % 4) * UC:(k % 4 + 1) * UC]
        if what == "gates":
            return w_in[:, o_gate:][:, c]
        if what == "out":
            return a["w_out"][0][:, c]
        if what == "pw1":
            w = a["conv_w_pw1_2"][0]
            return np.concatenate([w[:, k * P:(k + 1) * P], w[:, D + k * P:D + (k + 1) * P]], axis=1)
        if what == "pw2":
            return a["conv_w_pw2_2"][0][:, c]
        if what == "att_qk":
            if k < 4:
                return att[:, c]
            heads = [att[:, D + (2 * (k - 4) + n) * HD:D + (2 * (k - 4) + n + 1) * HD] for n in range(2)]
            return np.concatenate([heads[0], heads[0], heads[1], heads[1]], axis=1)
        if what == "att_v":
            return att[:, kv:kv + UC]
        return a["attn_w_out_2"][0][:, c]

    plan = unit_plan()
    wall = np.empty((len(plan), P, UW), np.float32)
    for n, (what, k) in enumerate(plan):
        wall[n] = unit(one(what, k))
    wmod = np.stack([unit(a["w_mod_2"][i][:, k * UC:(k + 1) * UC]) for i in range(LAYERS) for k in range(MODU)])
    wg2 = np.zeros((2, 48, 512), np.float32)
    wg2[:, 0:16] = a["gla_w_g2_2"][:, 0]
    wg2[:, 32:48] = a["gla_w_g2_2"][:, 1]
    relb = np.ascontiguousarray(a["rel_bias"])
    tokens = np.concatenate([a["x"][0], a["ctx_2"][0]])
    x = np.ascontiguousarray(tokens.T.reshape(KC, P, T2).transpose(1, 0, 2))
    cst, rel, rope = constants()
    return {"x": x, "vec": vec, "cst": cst, "rel": rel, "relb": relb, "wall": wall, "wmod": wmod, "wg2": wg2, "rope": rope}


def kernel(**inputs):
    import concourse.bacc as _bacc
    from concourse.bass_utils import run_bass_kernel_spmd as _run

    arrays = lay_out({k: np.asarray(v) for k, v in inputs.items()})
    nc = _bacc.Bacc("TRN2", target_bir_lowering=False, num_devices=1)
    args = {n: nc.dram_tensor(f"in_{n}", v.shape, mybir.dt.from_np(v.dtype), kind="ExternalInput").ap()
            for n, v in arrays.items()}
    out = nc.dram_tensor("out", (P, KC, S), F32, kind="ExternalOutput").ap()
    program(nc, out=out, **args)
    r = _run(nc, [{f"in_{n}": v for n, v in arrays.items()}], core_ids=[0])
    y = r.results[0]["out"]
    return np.ascontiguousarray(y.transpose(1, 0, 2).reshape(D, S).T).reshape(1, S, D)
```
